# Optimizing a Trainium2 kernel written in Bass

```python
import math
import jax, jax.numpy as jnp
from jax import lax
import numpy as np

D_MODEL = 1024
BATCH = 1
SEQ = 256
DEPTH = 2
DEC_BATCH = 8
DEC_SEQ = 4
PAST_LEN = 2048
PAGE_SIZE = 128

D_MIX = D_MODEL
GROUP_W = D_MIX // 4
H_A = 4
HD_A = GROUP_W // H_A
CONV_W = 4
LRU_C = 8.0
H_B = 4
DK_B = GROUP_W // H_B
DV_B = GROUP_W // H_B
H_C = 4
DK_C = GROUP_W // H_C
DV_C = GROUP_W // H_C
H_D = 4
DK_D = GROUP_W // H_D
DV_D = GROUP_W // H_D
CHUNK = 64
ROPE_BASE = 10000.0
D_FF = 2816
N_EXPERTS = 8
TOP_K = 2
D_FF_EXPERT = 1408
N_DENSE = (DEPTH + 1) // 2
N_MOE = DEPTH // 2
ALPHA = (2.0 * DEPTH) ** 0.25
BETA = (8.0 * DEPTH) ** -0.25
LN_EPS = 1e-5
HEAD_EPS = 1e-6
NEG_BIG = -1e30
LB_FLOOR = 1e-30
PROJ_SIZES = (GROUP_W, GROUP_W,
              H_B * DK_B, H_B * DK_B, H_B * DV_B, H_B * DV_B, H_B, H_B,
              H_C * DK_C, H_C * DK_C, H_C * DV_C, H_C * DV_C,
              H_D * DK_D, H_D * DK_D, H_D * DV_D, H_D * DV_D)
D_IN = sum(PROJ_SIZES)

kernel_name = 'hybrid_rglru_mlstm_retnet_hgrn2_decode_step'

def layer_norm(x, g, b):
    xf = x.astype(jnp.float32)
    mu = xf.mean(-1, keepdims=True)
    var = jnp.square(xf - mu).mean(-1, keepdims=True)
    y = (xf - mu) * lax.rsqrt(var + LN_EPS) * g.astype(jnp.float32) + b.astype(jnp.float32)
    return y.astype(x.dtype)

def head_norm(h, g, center):
    if center:
        h = h - h.mean(-1, keepdims=True)
    var = jnp.square(h).mean(-1, keepdims=True)
    B, T, H, dh = h.shape
    return (h * lax.rsqrt(var + HEAD_EPS)).reshape(B, T, H * dh) * g

def rotary(x, pos0):
    T, dh = x.shape[1], x.shape[-1]
    half = dh // 2
    inv_freq = ROPE_BASE ** (-jnp.arange(half, dtype=jnp.float32) / half)
    ang = (pos0 + jnp.arange(T, dtype=jnp.float32))[:, None] * inv_freq[None, :]
    cos = jnp.cos(ang)[None, :, None, :]
    sin = jnp.sin(ang)[None, :, None, :]
    x1, x2 = x[..., :half], x[..., half:]
    return jnp.concatenate([x1 * cos - x2 * sin, x1 * sin + x2 * cos], axis=-1)

def to_chunks(a, L):
    B, T = a.shape[:2]
    return jnp.swapaxes(a.reshape((B, T // L, L) + a.shape[2:]), 0, 1)

def from_chunks(a):
    nc, B, L = a.shape[:3]
    return jnp.swapaxes(a, 0, 1).reshape((B, nc * L) + a.shape[3:])

def chunk_scalar_decay(q, k, v, log_f, log_i, c0, m0, stabilise):
    T = q.shape[1]
    L = math.gcd(T, CHUNK)
    causal = jnp.tril(jnp.ones((L, L), dtype=bool))[None, :, :, None]

    def step(carry, inp):
        c, m = carry
        qc, kc, vc, lf, li = inp
        b = jnp.cumsum(lf, axis=1)
        d = jnp.where(causal, b[:, :, None] - b[:, None] + li[:, None], NEG_BIG)
        inter = b + m[:, None]
        b_end = b[:, -1]
        w_end = b_end[:, None] - b + li
        if stabilise:
            mq = jnp.maximum(d.max(axis=2), inter)
            m_new = jnp.maximum(b_end + m, w_end.max(axis=1))
        else:
            mq = jnp.zeros_like(inter)
            m_new = m
        s = jnp.einsum('bihd,bjhd->bijh', qc, kc) * jnp.exp(d - mq[:, :, None])
        y = (jnp.einsum('bijh,bjhv->bihv', s, vc)
             + jnp.einsum('bihd,bhdv->bihv', qc, c) * jnp.exp(inter - mq)[..., None])
        c_new = (c * jnp.exp(b_end + m - m_new)[..., None, None]
                 + jnp.einsum('bjhd,bjhv->bhdv', kc * jnp.exp(w_end - m_new[:, None])[..., None], vc))
        return (c_new, m_new), (y, mq)

    xs = tuple(to_chunks(a, L) for a in (q, k, v, log_f, log_i))
    (c, m), (y, mq) = lax.scan(step, (c0, m0), xs)
    return from_chunks(y), from_chunks(mq), c, m

def chunk_channel_decay(q, k, v, log_g, s0):
    T = q.shape[1]
    L = math.gcd(T, CHUNK)
    causal = jnp.tril(jnp.ones((L, L), dtype=bool))[None, :, :, None, None]

    def step(s, inp):
        qc, kc, vc, lg = inp
        b = jnp.cumsum(lg, axis=1)
        decay = jnp.exp(jnp.where(causal, b[:, :, None] - b[:, None], NEG_BIG))
        a = jnp.einsum('bihd,bjhd,bijhd->bijh', qc, kc, decay)
        y = (jnp.einsum('bijh,bjhv->bihv', a, vc)
             + jnp.einsum('bihd,bhdv->bihv', qc * jnp.exp(b), s))
        b_end = b[:, -1]
        s_new = (jnp.exp(b_end)[..., None] * s
                 + jnp.einsum('bjhd,bjhv->bhdv', kc * jnp.exp(b_end[:, None] - b), vc))
        return s_new, y

    xs = tuple(to_chunks(a, L) for a in (q, k, v, log_g))
    s, y = lax.scan(step, s0, xs)
    return from_chunks(y), s

def lin_combine(e1, e2):
    a1, u1 = e1
    a2, u2 = e2
    return a1 * a2, a2 * u1 + u2

def rglru_group(xa, ga, h0, buf0, conv_w, conv_b, wr, br, wi, bi, lam):
    B, T, W = xa.shape
    xp = jnp.concatenate([buf0, xa], axis=1)
    xc = conv_b + sum(conv_w[j] * xp[:, j:j + T] for j in range(CONV_W))
    xh = xc.reshape(B, T, H_A, HD_A)
    r = jax.nn.sigmoid(jnp.einsum('bthi,hij->bthj', xh, wr).reshape(B, T, W) + br)
    ig = jax.nn.sigmoid(jnp.einsum('bthi,hij->bthj', xh, wi).reshape(B, T, W) + bi)
    log_a = -LRU_C * r * jax.nn.softplus(-lam)
    a = jnp.exp(log_a)
    u = jnp.sqrt(-jnp.expm1(2.0 * log_a)) * (ig * xc)
    u = u.at[:, 0].add(a[:, 0] * h0)
    _, h = lax.associative_scan(lin_combine, (a, u), axis=1)
    return h * jax.nn.gelu(ga), h[:, -1], xp[:, T:]

def mlstm_group(qb, kb, vb, ob, ib, fb, c0, n0, m0, bias_i, bias_f, g):
    B, T, _ = qb.shape
    q = qb.reshape(B, T, H_B, DK_B)
    k = kb.reshape(B, T, H_B, DK_B) * DK_B ** -0.5
    v = vb.reshape(B, T, H_B, DV_B)
    log_i = ib + bias_i
    log_f = jax.nn.log_sigmoid(fb + bias_f)
    v_aug = jnp.concatenate([v, jnp.ones((B, T, H_B, 1), v.dtype)], axis=-1)
    c_aug0 = jnp.concatenate([c0, n0[..., None]], axis=-1)
    y, mq, c_aug, m1 = chunk_scalar_decay(q, k, v_aug, log_f, log_i, c_aug0, m0, True)
    h = y[..., :DV_B] / jnp.maximum(jnp.abs(y[..., DV_B:]), jnp.exp(-mq)[..., None])
    out = jax.nn.sigmoid(ob) * head_norm(h, g, True)
    return out, c_aug[..., :DV_B], c_aug[..., DV_B], m1

def retention_group(qc, kc, vc, gc, s0, g, pos0):
    B, T, _ = qc.shape
    q = rotary(qc.reshape(B, T, H_C, DK_C), pos0)
    k = rotary(kc.reshape(B, T, H_C, DK_C), pos0) * DK_C ** -0.5
    v = vc.reshape(B, T, H_C, DV_C)
    log_gamma = jnp.log1p(-(2.0 ** (-5.0 - jnp.arange(H_C, dtype=jnp.float32))))
    log_f = jnp.broadcast_to(log_gamma, (B, T, H_C))
    log_i = jnp.zeros((B, T, H_C), jnp.float32)
    y, _, s1, _ = chunk_scalar_decay(q, k, v, log_f, log_i, s0, jnp.zeros((B, H_C), jnp.float32), False)
    out = jax.nn.silu(gc) * head_norm(y, g, True)
    return out, s1

def hgrn2_group(qd, fd, id_, gd, s0, lb, g):
    B, T, _ = qd.shape
    log_g = jnp.logaddexp(jnp.log(jnp.maximum(lb, LB_FLOOR)), jnp.log1p(-lb) + jax.nn.log_sigmoid(fd))
    k = (1.0 - lb) * jax.nn.sigmoid(-fd)
    q = jax.nn.silu(qd)
    y, s1 = chunk_channel_decay(q.reshape(B, T, H_D, DK_D), k.reshape(B, T, H_D, DK_D),
                                id_.reshape(B, T, H_D, DV_D), log_g.reshape(B, T, H_D, DK_D), s0)
    out = jax.nn.silu(gd) * head_norm(y, g, False)
    return out, s1

def swiglu(x, w1, w3, w2):
    h = jax.nn.silu(jnp.einsum('btd,df->btf', x, w1)) * jnp.einsum('btd,df->btf', x, w3)
    return jnp.einsum('btf,fd->btd', h, w2)

def moe_swiglu(x, router, router_b, w1, w3, w2):
    logits = (jnp.einsum('btd,de->bte', x, router) + router_b).astype(jnp.float32)
    probs = jax.nn.softmax(logits, axis=-1)
    top_p, top_i = lax.top_k(probs, TOP_K)
    top_p = top_p / top_p.sum(-1, keepdims=True)
    gates = jnp.einsum('btk,btke->bte', top_p, jax.nn.one_hot(top_i, N_EXPERTS, dtype=jnp.float32))
    y = jnp.zeros(x.shape, jnp.float32)
    for e in range(N_EXPERTS):
        y = y + gates[..., e:e + 1] * swiglu(x, w1[e], w3[e], w2[e]).astype(jnp.float32)
    return y.astype(x.dtype)

def mixing_block(x, st, l, P, lb, pos0):
    def f(name):
        return P[name][l].astype(jnp.float32)
    proj = jnp.einsum('btd,de->bte', x, P['w_in'][l]).astype(jnp.float32)
    cuts = np.cumsum(PROJ_SIZES)[:-1].tolist()
    (xa, ga, qb, kb, vb, ob, ib, fb, qc, kc, vc, gc, qd, fd, id_, gd) = jnp.split(proj, cuts, axis=-1)
    h0, buf0, c0, n0, m0, sr0, sh0 = (s.astype(jnp.float32) for s in st)
    ya, h1, buf1 = rglru_group(xa, ga, h0, buf0, f('conv_w'), f('conv_b'), f('lru_wr'), f('lru_br'),
                               f('lru_wi'), f('lru_bi'), f('lru_lambda'))
    yb, c1, n1, m1 = mlstm_group(qb, kb, vb, ob, ib, fb, c0, n0, m0, f('mlstm_bi'), f('mlstm_bf'),
                                 f('mlstm_norm_g'))
    yc, sr1 = retention_group(qc, kc, vc, gc, sr0, f('ret_norm_g'), pos0)
    yd, sh1 = hgrn2_group(qd, fd, id_, gd, sh0, lb, f('hgrn_norm_g'))
    mixed = jnp.concatenate([ya, yb, yc, yd], axis=-1).astype(x.dtype)
    out = jnp.einsum('bte,ed->btd', mixed, P['w_out'][l])
    return out, (h1, buf1, c1, n1, m1, sr1, sh1)

def run_trunk(x, states, pos0, P, lb_all):
    new_states = []
    for l in range(DEPTH):
        st = tuple(s[l] for s in states)
        mix, st_new = mixing_block(x, st, l, P, lb_all[l], pos0)
        x = layer_norm(ALPHA * x + mix, P['ln_mix_g'][l], P['ln_mix_b'][l])
        j = l // 2
        if l % 2 == 0:
            ffn = swiglu(x, P['ffn_w1'][j], P['ffn_w3'][j], P['ffn_w2'][j])
        else:
            ffn = moe_swiglu(x, P['moe_router'][j], P['moe_router_b'][j], P['moe_w1'][j],
                             P['moe_w3'][j], P['moe_w2'][j])
        x = layer_norm(ALPHA * x + ffn, P['ln_ffn_g'][l], P['ln_ffn_b'][l])
        new_states.append(st_new)
    stacked = tuple(jnp.stack([s[i] for s in new_states]) for i in range(7))
    return x, stacked

def zero_states(B):
    f32 = jnp.float32
    return (jnp.zeros((DEPTH, B, GROUP_W), f32),
            jnp.zeros((DEPTH, B, CONV_W - 1, GROUP_W), f32),
            jnp.zeros((DEPTH, B, H_B, DK_B, DV_B), f32),
            jnp.zeros((DEPTH, B, H_B, DK_B), f32),
            jnp.zeros((DEPTH, B, H_B), f32),
            jnp.zeros((DEPTH, B, H_C, DK_C, DV_C), f32),
            jnp.zeros((DEPTH, B, H_D, DK_D, DV_D), f32))

def setup_inputs(seed: int = 0) -> dict:
    key = jax.random.key(seed)
    keys = iter(jax.random.split(key, 64))

    def nrm(shape, scale):
        return scale * jax.random.normal(next(keys), shape, jnp.float32)

    def gain(shape):
        return 1.0 + nrm(shape, 0.05)

    u = jax.random.uniform(next(keys), (DEPTH, GROUP_W), jnp.float32, 0.9, 0.999)
    s_base = u ** (1.0 / LRU_C)
    lru_lambda = jnp.log(s_base) - jnp.log1p(-s_base)
    return {
        'x_prompt': nrm((BATCH, SEQ, D_MODEL), 1.0),
        'x_sample': nrm((DEC_BATCH, DEC_SEQ, D_MODEL), 1.0),
        'state_rglru_h': nrm((DEPTH, DEC_BATCH, GROUP_W), 0.5),
        'state_rglru_conv': nrm((DEPTH, DEC_BATCH, CONV_W - 1, GROUP_W), 0.5),
        'state_mlstm_C': nrm((DEPTH, DEC_BATCH, H_B, DK_B, DV_B), 0.3),
        'state_mlstm_n': nrm((DEPTH, DEC_BATCH, H_B, DK_B), 0.3),
        'state_mlstm_m': nrm((DEPTH, DEC_BATCH, H_B), 1.0),
        'state_ret_S': nrm((DEPTH, DEC_BATCH, H_C, DK_C, DV_C), 0.3),
        'state_hgrn_S': nrm((DEPTH, DEC_BATCH, H_D, DK_D, DV_D), 0.3),
        'w_in': nrm((DEPTH, D_MODEL, D_IN), D_MODEL ** -0.5),
        'w_out': nrm((DEPTH, D_MIX, D_MODEL), BETA * D_MIX ** -0.5),
        'ln_mix_g': gain((DEPTH, D_MODEL)),
        'ln_mix_b': nrm((DEPTH, D_MODEL), 0.02),
        'ln_ffn_g': gain((DEPTH, D_MODEL)),
        'ln_ffn_b': nrm((DEPTH, D_MODEL), 0.02),
        'conv_w': nrm((DEPTH, CONV_W, GROUP_W), CONV_W ** -0.5),
        'conv_b': nrm((DEPTH, GROUP_W), 0.02),
        'lru_wr': nrm((DEPTH, H_A, HD_A, HD_A), HD_A ** -0.5),
        'lru_br': nrm((DEPTH, GROUP_W), 0.02),
        'lru_wi': nrm((DEPTH, H_A, HD_A, HD_A), HD_A ** -0.5),
        'lru_bi': nrm((DEPTH, GROUP_W), 0.02),
        'lru_lambda': lru_lambda,
        'mlstm_bi': nrm((DEPTH, H_B), 0.1),
        'mlstm_bf': jnp.linspace(3.0, 6.0, H_B, dtype=jnp.float32)[None, :] + nrm((DEPTH, H_B), 0.1),
        'mlstm_norm_g': gain((DEPTH, GROUP_W)),
        'ret_norm_g': gain((DEPTH, GROUP_W)),
        'hgrn_lb': nrm((DEPTH, H_D * DK_D), 0.5),
        'hgrn_norm_g': gain((DEPTH, GROUP_W)),
        'ffn_w1': nrm((N_DENSE, D_MODEL, D_FF), D_MODEL ** -0.5),
        'ffn_w3': nrm((N_DENSE, D_MODEL, D_FF), D_MODEL ** -0.5),
        'ffn_w2': nrm((N_DENSE, D_FF, D_MODEL), BETA * D_FF ** -0.5),
        'moe_router': nrm((N_MOE, D_MODEL, N_EXPERTS), D_MODEL ** -0.5),
        'moe_router_b': nrm((N_MOE, N_EXPERTS), 0.01),
        'moe_w1': nrm((N_MOE, N_EXPERTS, D_MODEL, D_FF_EXPERT), D_MODEL ** -0.5),
        'moe_w3': nrm((N_MOE, N_EXPERTS, D_MODEL, D_FF_EXPERT), D_MODEL ** -0.5),
        'moe_w2': nrm((N_MOE, N_EXPERTS, D_FF_EXPERT, D_MODEL), BETA * D_FF_EXPERT ** -0.5),
    }

def reference(x_prompt, x_sample, state_rglru_h, state_rglru_conv, state_mlstm_C, state_mlstm_n,
              state_mlstm_m, state_ret_S, state_hgrn_S, w_in, w_out, ln_mix_g, ln_mix_b, ln_ffn_g,
              ln_ffn_b, conv_w, conv_b, lru_wr, lru_br, lru_wi, lru_bi, lru_lambda, mlstm_bi, mlstm_bf,
              mlstm_norm_g, ret_norm_g, hgrn_lb, hgrn_norm_g, ffn_w1, ffn_w3, ffn_w2, moe_router,
              moe_router_b, moe_w1, moe_w3, moe_w2):
    P = dict(w_in=w_in, w_out=w_out, ln_mix_g=ln_mix_g, ln_mix_b=ln_mix_b, ln_ffn_g=ln_ffn_g,
             ln_ffn_b=ln_ffn_b, conv_w=conv_w, conv_b=conv_b, lru_wr=lru_wr, lru_br=lru_br,
             lru_wi=lru_wi, lru_bi=lru_bi, lru_lambda=lru_lambda, mlstm_bi=mlstm_bi, mlstm_bf=mlstm_bf,
             mlstm_norm_g=mlstm_norm_g, ret_norm_g=ret_norm_g, hgrn_norm_g=hgrn_norm_g,
             ffn_w1=ffn_w1, ffn_w3=ffn_w3, ffn_w2=ffn_w2, moe_router=moe_router,
             moe_router_b=moe_router_b, moe_w1=moe_w1, moe_w3=moe_w3, moe_w2=moe_w2)
    sm = jax.nn.softmax(hgrn_lb.astype(jnp.float32), axis=0)
    lb_all = jnp.cumsum(sm, axis=0) - sm[0]

    y_prompt, (p_h, p_conv, p_C, p_n, p_m, p_ret, p_hgrn) = run_trunk(
        x_prompt, zero_states(x_prompt.shape[0]), 0, P, lb_all)
    sample_states = (state_rglru_h, state_rglru_conv, state_mlstm_C, state_mlstm_n, state_mlstm_m,
                     state_ret_S, state_hgrn_S)
    y_sample, (s_h, s_conv, s_C, s_n, s_m, s_ret, s_hgrn) = run_trunk(
        x_sample, sample_states, PAST_LEN, P, lb_all)
    return (y_prompt, y_sample, p_h, p_conv, p_C, p_n, p_m, p_ret, p_hgrn,
            s_h, s_conv, s_C, s_n, s_m, s_ret, s_hgrn)


_drawn_inputs = setup_inputs


def setup_inputs(seed=0):
    import zlib

    import numpy as np

    out = dict(_drawn_inputs(seed))
    spreads = {}
    factors = {'lru_br': 8.0,
     'lru_bi': 8.0,
     'mlstm_norm_g': 6.142,
     'ret_norm_g': 5.967,
     'hgrn_norm_g': 4.54,
     'moe_router_b': 4.14}
    for name, (base, spread) in spreads.items():
        noise = np.random.default_rng([zlib.crc32(name.encode()), seed]).standard_normal(out[name].shape)
        drawn = base * np.exp(spread * noise) if base else spread * noise
        out[name] = __import__('jax').numpy.asarray(drawn.astype(out[name].dtype))
    for name, factor in factors.items():
        out[name] = (out[name] * factor).astype(out[name].dtype)
    return out
```

```python
from contextlib import ExitStack

import numpy as np

import concourse.bass as bass
from concourse import mybir

F32 = mybir.dt.float32
U32 = mybir.dt.uint32
ALU = mybir.AluOpType
ACT = mybir.ActivationFunctionType
AX_X = mybir.AxisListType.X

P = 128
D, KT = 1024, 8
SEQ, NB, DSEQ = 256, 8, 4
NS = NB * DSEQ
T = SEQ + NS
DEPTH, GW, NH, HD = 2, 256, 4, 64
PAST = 2048
D_FF, NE, D_FE = 2816, 8, 1408
FT_E = D_FE // P
GATE_COL = 2 * GW + 4 * GW
NPT = 28
XA, GA, QB, KB, VB, OB, QC, KC, VC, GC, QD, FD, ID, GD = range(0, NPT, 2)
ALPHA = (2.0 * DEPTH) ** 0.25
LN_EPS, HEAD_EPS = 1e-5, 1e-6
TINY = 2.0 ** -60
WP = 3 + SEQ + NB * (3 + DSEQ)
WC = WP - 3
SC = 3 + SEQ
WS = SEQ + P + NS
LEVELS = (64, 32, 16, 8, 4, 2, 1)
NEG = -1e30

U_IN, U_OUT = (0, 33), (14, 47)
U_UP, U_DOWN, U_MOE = 18, 29, 51
CAP = 96
UP_SLOTS = ((6, 7), (0, 1))
DOWN_SLOTS = ((2, 3, 4), (8, 9, 10))
E_SLOTS = (0, 1, 6, 7, 8, 9, 10, 2, 3, 4, 5)
LOADS_MOE = (19, 19, 4, 4, 4, 2, 6, 6, 2, 2, 2) + (0,) * 6
LOADS_L1 = (12, 12, 3, 3, 3, 1, 6, 6, 2, 2, 2)
A_IN = (2, 16)
D_IN, D_OUT = (2, 35), (16, 49)
D_UP, D_DOWN = 20, 31
N_INPUTS = 13 + 3 + 3
STORES = 3 * 3 + 2 + 6

VEC = {}
for _name, _rows in (("ln_mix_g", 16), ("ln_mix_b", 16), ("ln_ffn_g", 16), ("ln_ffn_b", 16), ("conv_w", 16),
                     ("conv_b", 4), ("lru_br", 4), ("lru_bi", 4), ("lru_lambda", 4), ("mlstm_norm_g", 4),
                     ("ret_norm_g", 4), ("hgrn_norm_g", 4), ("hgrn_lb", 4)):
    VEC[_name] = (sum(r for _, r in VEC.values()), _rows)
NVEC = sum(r for _, r in VEC.values())


SEMAPHORES = """
tables_in inputs_in g_ps gate_weights_in ps mixed_ready moe_up x_ready_d x_ready_a w2_used y_rows_a
y_rows_d y_stored small_in lru_zeroed lru_ps lru_in states_stored s0_in vm_r vm_m vm_h v_tok a_done
rot_done rst_ps hl_ps rst_done mst_done hst_done orow_done cols_ps x_ps ln_mean_ps ln_sq ln_var_ps
ev_a ev_d v_ps g_sb gif_ps swap_ps xc_ready li_done rs_ps lru_read rk_ps rw_done ry_ps rk_done
mrow_done mcol_ps ry_done mb_ps ma_ps me_done ms_ps mcol_done mk_ps mw_done mq_done mb_done my_ps
mk_done mst_ps my_done hl_ready hl_done hk_ready hk_ps hk_done hc_ps hc_done hy_ps hst_ps mean_ps
sq6_done var_ps outc_done centered orow_ps logits_ps xtk_ps gates_done gt_ps slots_done xtk_done
pt_ps flag_ready gbc_ps sel_ready ga_ps xe_done moe_h dn_ps yt_done sc_ev sc_ps gbc_done moe_y pb_ps
sg_done moe_sum y_ps prep_e prep_exp prep_s ln_xc ln_sd ln_xn mz act_chain m_ln gl_sq gl_in gl_tanh
la_ready a_exp om_ready a_sqrt m_rows hf_ready hf_exp hg_ready hq_tanh hg_ln hx hz hi_ready hi_exp
th_done sd6_done sl lg_ready pr_exp moe_s dve_chain ye_ready moe_g
""".split()


def shape_tables():
    parts, where, at = [], {}, 0

    def put(name, a):
        nonlocal at
        a = np.asarray(a, np.float32)
        full = np.zeros((P,) + a.shape[1:], np.float32)
        full[:a.shape[0]] = a
        flat = full.reshape(P, -1)
        where[name] = (at, a.shape[0], a.shape[1:])
        parts.append(flat)
        at += flat.shape[1]

    r = np.arange(P)
    put("ident", np.eye(P))
    put("iota8", np.ones((P, 1)) * np.arange(NE)[None])
    put("iotacap", np.ones((P, 1)) * np.arange(CAP)[None])
    put("iotarow", r[:, None])
    put("ones", np.ones((P, P)))
    put("lnmean", np.full((P, P), 1.0 / D))
    put("headmean", (r[:, None] // HD == r[None] // HD) / HD)
    half = HD // 2
    put("swap", r[:, None] == (r[None] // HD) * HD + (r[None] % HD + half) % HD)
    pos = np.concatenate([np.arange(SEQ), PAST + np.tile(np.arange(DSEQ), NB)]).astype(np.float32)
    inv = (np.float32(10000.0) ** (-np.arange(half, dtype=np.float32) / np.float32(half))).astype(np.float32)
    ang = (pos[None, :] * inv[:, None]).astype(np.float32)
    rows = r % HD % half
    put("cos", np.cos(ang.astype(np.float64))[rows])
    put("sin", np.sin(ang.astype(np.float64))[rows] * np.where(r % HD < half, -1.0, 1.0)[:, None])
    j = r[:, None]
    i_seq = np.arange(SEQ)[None]
    s_i = np.arange(NS)[None]
    sample_ok = (j < NS) & (j // DSEQ == s_i // DSEQ) & (j <= s_i)
    dist = np.concatenate([i_seq - j, np.arange(P)[None] - j, np.where(sample_ok, s_i - j, -1)], 1)
    put("causal", np.where(dist >= 0, 0.0, NEG))
    lg = np.log1p(-(2.0 ** (-5.0 - np.arange(NH))))
    decay = np.exp(lg[None, :, None] * np.maximum(dist, 0)[:, None, :]) * (dist >= 0)[:, None, :]
    put("retdecay", decay * HD ** -0.5)
    w = np.zeros((P, 3, NH))
    w[:, 0] = np.exp(lg[None] * (SEQ - 1 - j))
    w[:, 1] = np.exp(lg[None] * (P - 1 - j))
    w[:, 2] = np.exp(lg[None] * (DSEQ - 1 - j % DSEQ))
    put("retkeyw", w * HD ** -0.5)
    head_of = np.stack([r // HD, 2 + r // HD], 1)
    put("retinter", np.exp(lg[head_of][:, :, None] * (1 + np.arange(NS) % DSEQ)))
    put("retstate", np.exp(lg[head_of] * DSEQ))
    put("selpair", np.arange(NH)[:, None, None] == head_of.T[None])
    put("batchmask", (np.arange(NS)[:, None] // DSEQ == np.arange(NB)[None]))
    lv = []
    for s in LEVELS:
        same = j // (2 * s) == r[None] // (2 * s)
        lv.append(same & (j % (2 * s) < s) & (r[None] % (2 * s) >= s))
    lv.append(j == r[None])
    put("levels", np.stack(lv, 1))
    t = np.arange(T)
    start4 = (t >= SEQ) & ((t - SEQ) % DSEQ == 0)
    put("keep128", np.ones((P, 1)) * (1.0 - (start4 | (t == 0) | (t == P)))[None])
    put("keep256", np.ones((NH, 1)) * (1.0 - (start4 | (t == 0)))[None])
    put("negstart", np.ones((NH, 1)) * np.where(start4, NEG, 0.0)[None])

    return np.ascontiguousarray(np.concatenate(parts, 1)), where



def decoder_kernel(nc, A, out, tab, where):
    with ExitStack() as ctx:
        def sb(name, shape):
            return ctx.enter_context(nc.sbuf_tensor(name, shape, F32))

        S = {n: ctx.enter_context(nc.semaphore(n)) for n in SEMAPHORES}
        full = [ctx.enter_context(nc.semaphore(f"slot_full_{i}")) for i in range(17)]

        UP = sb("up_slots", [P, 11, 2048])
        OV = sb("overlay", [P, 11264])
        TB = sb("tables", [P, tab.shape[1]])
        X = sb("x", [P, KT, T])[:, :, :]
        VE = sb("vectors", [P, NVEC])
        STC = sb("state_cols", [P, 160])
        OUTC = sb("out_cols", [P, 96])
        MB = sb("mix_or_moe", [P, 8576])
        WG = sb("gate_weights", [P, KT, 8])
        LW = sb("lru_weights", [P, 2, 2, P])
        GB = sb("mlstm_gate_bias", [NH, 2, DEPTH])
        M0 = sb("mlstm_m", [NH, DEPTH, NB])
        M1 = sb("mlstm_m_new", [NH, 1 + NB])
        SM = sb("small", [P, 640])
        LC = sb("layer_consts", [P, 16])
        RW = sb("router", [P, KT, NE])
        RB = sb("router_bias", [P, NE])
        PS = ctx.enter_context(nc.psum_tensor("ps", [P, 8, 512], F32))

        def tb(name):
            at, rows, shape = where[name]
            n = int(np.prod(shape))
            a = TB[0:rows, at:at + n]
            if len(shape) == 2:
                a = a.rearrange("p (a b) -> p a b", a=shape[0])
            return a

        def cut(buf, at, *shape):
            a = buf[:, at:at + int(np.prod(shape))]
            if len(shape) == 2:
                a = a.rearrange("p (a b) -> p a b", a=shape[0])
            if len(shape) == 3:
                a = a.rearrange("p (a b c) -> p a b c", a=shape[0], b=shape[1])
            if len(shape) == 4:
                a = a.rearrange("p (a b c d) -> p a b c d", a=shape[0], b=shape[1], c=shape[2])
            return a

        ident = tb("ident")
        onesc = tb("ones")
        proj = cut(OV, 0, NPT, T)
        mixed = cut(OV, NPT * T, KT, T)
        ROWS = OV[0:NH, (NPT + KT) * T:11264]
        hid = cut(OV, 0, 22, T)
        sil = cut(OV, 22 * T, 4, T)
        SQ = cut(OV, 0, KT, T)
        RSTD = cut(OV, KT * T, 1, T)[:, 0]
        SDEV = cut(OV, KT * T + T, 1, T)[:, 0]
        W2 = cut(OV, 0, 11, 1024)
        xtok = cut(OV, 0, 3, D)
        vrows = OV[:, 3 * D:3 * D + P]
        srows = OV[:, 3 * D + P:3 * D + 2 * P]
        nrows = OV[:, 3 * D + 2 * P:3 * D + 3 * P]
        scr = UP[:, 8:11, :].rearrange("p a b -> p (a b)")
        R = [scr[:, 640 * i:640 * i + 640] for i in range(9)]
        VT = cut(MB, 0, 3, 6 * P)
        KTK = cut(MB, 2304, 2, 3, 2 * P)
        S0 = cut(MB, 3840, 3, 2 * NB * HD)
        WT = cut(MB, 6912, NH, WS)
        hid_e = cut(MB, 0, FT_E, T)
        sil_e = cut(MB, 3168, 2, T)
        YE = cut(MB, 3744, KT, T)
        GBC = cut(MB, 6048, NE, T)
        XTK = cut(MB, 0, 3, D)
        XE = cut(MB, 3072, KT, CAP)
        SELT = cut(MB, 3840, 3, CAP)
        sil_g = cut(MB, 4128, 2, CAP)
        free_tb = where["headmean"][0]
        SG = cut(TB, free_tb, NE, T)[0:CAP]
        hid_g = cut(TB, free_tb + NE * T, FT_E, CAP)
        YTK = TB[0:CAP, free_tb + NE * T + FT_E * CAP:free_tb + NE * T + FT_E * CAP + D]
        vec = {name: VE[:, at:at + n] for name, (at, n) in VEC.items()}

        def slot(s):
            return UP[:, s, :].rearrange("p (k n) -> p k n", k=8)

        w_in = A["w_in"].rearrange("l (k p) c -> l p k c", p=P)
        w_out = A["w_out"].rearrange("l (k p) c -> l p k c", p=P)
        f_w1 = A["ffn_w1"].rearrange("l (k p) c -> l p k c", p=P)
        f_w3 = A["ffn_w3"].rearrange("l (k p) c -> l p k c", p=P)
        f_w2 = A["ffn_w2"].rearrange("l (k p) c -> l p k c", p=P)
        m_w1 = A["moe_w1"].rearrange("l e (k p) c -> (l e) p k c", p=P)
        m_w3 = A["moe_w3"].rearrange("l e (k p) c -> (l e) p k c", p=P)
        m_w2 = A["moe_w2"].rearrange("l e (k p) c -> (l e) p k c", p=P)

        PFIN = sb("prompt_states", [P, 3, 2, HD])
        OROW = sb("out_rows", [96, P])
        QH = sb("sample_queries", [P, 2, 2, NS])
        GE = sb("end_decay", [P, 2, 1 + NB])
        SC0 = sb("chunk_state", [P, 2, HD])
        N0S = sb("tmp_small", [P, 64])
        rli, rlf, rtmp = ROWS[:, 0:T], ROWS[:, T:2 * T], ROWS[:, 2 * T:3 * T]
        risc = ROWS[:, 3 * T:3 * T + NS]
        rb, rm = SM[0:NH, 0:T], SM[0:NH, T:2 * T]
        gsb = SM[0:8, 0:T]
        mcol = SM[:, 2 * T:2 * T + 24].rearrange("p (t k h) -> p t k h", t=3, k=2)
        A2 = {n: R[i][:, 0:2 * WP].rearrange("p (a w) -> p a w", a=2)
              for n, i in (("xc", 1), ("r", 2), ("ig", 3), ("a", 4), ("h", 5), ("om", 6))}
        xpad = R[0][:, 0:2 * WP].rearrange("p (a w) -> p a w", a=2)
        C2 = [R[i][:, 0:2 * T].rearrange("p (a t) -> p a t", a=2) for i in range(9)]
        rotmp = MB[:, 6912:6912 + 4 * T].rearrange("p (a t) -> p a t", a=4)
        Vm = scr[0:NS, 0:4 * NB * HD].rearrange("p (h b v) -> p h b v", h=NH, b=NB)
        E = scr[:, 3840:3840 + NH * WS].rearrange("p (h w) -> p h w", h=NH)
        embc = R[4][:, 0:640].rearrange("p (a w) -> p a w", a=2)
        TH = scr[:, 2560:2560 + 6 * T].rearrange("p (a t) -> p a t", a=6)
        AT = WT.rearrange("p h w -> p (h w)")[:, 0:1024].rearrange("p (c h i) -> p c h i", c=2, h=NH)
        ATs = WT.rearrange("p h w -> p (h w)")[0:NS, 1024:1024 + NH * NS].rearrange("p (h i) -> p h i", h=NH)
        Y = proj[:, QC:QC + 6]
        Y_RET, Y_ML, Y_HG = 0, 2, 4
        SQ6 = proj[:, QB:QB + 6]
        SD6 = proj[:, QD:QD + 6]
        NL = len(LEVELS) + 1
        LG, PR, EQ, TM, SEL, PX = (SM[:, 24 * i:24 * i + 24].rearrange("p (t e) -> p t e", t=3) for i in range(6))
        T3 = [SM[:, 144 + 3 * i:147 + 3 * i] for i in range(6)]
        GTOK = SM[:, 168:192].rearrange("p (t e) -> p t e", t=3)
        CNT = SM[0:NE, 162:163]
        FLAG = ctx.enter_context(nc.sbuf_tensor("dense_flag", [1, 1], mybir.dt.int32))
        GROW = SM[0:NE, 200:200 + T]
        free_tb += NE * T + FT_E * CAP + D
        SROW = TB[0:NE, free_tb:free_tb + T]
        PROW = TB[0:NE, free_tb + T:free_tb + 2 * T]
        PTK = SM[:, 500:524].rearrange("p (t e) -> p t e", t=3)
        block = ctx.enter_context(nc.Block())

        def level_view(x, s):
            w = SEQ if s >= DSEQ else T
            b = x[:, :, 0:w].rearrange("p a (n h s) -> p a n h s", h=2, s=s)
            return b[:, :, :, 0], b[:, :, :, 1]

        def state_view(ap, l, b0, nb):
            return ap[l, b0:b0 + nb].rearrange("b (p h) d v -> (h d) p b v", h=2)

        def s0(kind):
            return S0[:, kind].rearrange("p (a b v) -> p a b v", a=2, b=NB)

        @block.sync
        def _(sp):
            sp.dma_start(TB[:, :], tab).then_inc(S["tables_in"], 16)
            for name, (at, n) in VEC.items():
                src = A[name]
                src = src.rearrange("l c (w p) -> (l c w) p", p=P) if len(src.shape) == 3 else \
                    src.rearrange("l (w p) -> (l w) p", p=P)
                sp.dma_start(vrows[at:at + n, :], src).then_inc(S["inputs_in"], 16)
            sp.dma_start(srows[0:96, :], A["state_rglru_conv"].rearrange("l b c (w p) -> (l b c w) p", p=P)
                         ).then_inc(S["inputs_in"], 16)
            sp.dma_start(srows[96:128, :], A["state_rglru_h"].rearrange("l b (w p) -> (l b w) p", p=P)
                         ).then_inc(S["inputs_in"], 16)
            sp.dma_start(nrows[0:32, :], A["state_mlstm_n"].rearrange("l b (w h) d -> (l b w) (h d)", h=2)
                         ).then_inc(S["inputs_in"], 16)
            xp = A["x_prompt"].rearrange("a (t p) d -> (a t) p d", p=P)
            for t in range(2):
                sp.dma_start(xtok[:, t], xp[t]).then_inc(S["inputs_in"], 16)
            sp.dma_start(xtok[0:NS, 2], A["x_sample"].rearrange("b t d -> (b t) d")).then_inc(S["inputs_in"], 16)

            def refill(s, dst, src):
                sp.dma_start(dst, src).then_inc(full[s], 16)

            def in_panel(l, u, h):
                skip = 8 if isinstance(u, int) and u >= 6 else 0
                refill(h, slot(h), w_in[l][:, :, u * 256 + skip:u * 256 + skip + 256])

            for l in range(DEPTH):
                if l:
                    sp.wait_ge(S["g_ps"], l)
                sp.dma_start(WG[:, :, :], w_in[l][:, :, GATE_COL:GATE_COL + 8]).then_inc(S["gate_weights_in"], 16)
                if l:
                    sp.wait_ge(S["ps"], U_UP + 10)
                for h in range(2):
                    in_panel(l, h, h)
                for first, end, skip in ((1, 3, 0), (3, 7, 8)):
                    with sp.Fori(first, end) as i:
                        for h in range(2):
                            sp.wait_ge(S["ps"], i * 2 + (U_IN[l] + h - 1))
                            refill(h, slot(h), w_in[l][:, :, bass.ds(i * 512 + (h * 256 + skip), 256)])
                if l:
                    sp.wait_ge(S["ps"], U_DOWN + 4)
                for u in range(4):
                    refill(2 + u, slot(2 + u), w_out[l][:, :, u * 256:u * 256 + 256])
                if l == 0:
                    def up_panel(h, c):
                        for s, w in zip(UP_SLOTS[h], (f_w1, f_w3)):
                            refill(s, slot(s), w[0][:, :, c])
                    up_panel(0, slice(0, 256))
                    sp.wait_ge(S["ps"], U_IN[0] + 14)
                    up_panel(1, slice(256, 512))
                    with sp.Fori(1, 5) as i:
                        for h in range(2):
                            sp.wait_ge(S["ps"], i * 2 + (U_UP + h - 1))
                            up_panel(h, bass.ds(i * 512 + h * 256, 256))
                    sp.wait_ge(S["ps"], U_UP + 9)
                    up_panel(0, slice(2560, 2816))
                    sp.wait_ge(S["ps"], U_OUT[0] + 4)
                    for m in range(4):
                        if m == 1:
                            sp.wait_ge(S["mixed_ready"], 1)
                        elif m > 1:
                            sp.wait_ge(S["ps"], U_DOWN + m - 1)
                        for j, s in enumerate(DOWN_SLOTS[m % 2]):
                            nk = min(8, 22 - 8 * j)
                            refill(s, slot(s)[:, 0:nk], f_w2[0][:, 8 * j:8 * j + nk, m * 256:m * 256 + 256])

            def expert(e, first):
                for ft in range(FT_E):
                    s = E_SLOTS[ft]
                    if first:
                        if ft == 0:
                            sp.wait_ge(S["ps"], U_IN[1] + 14)
                        if s == 8:
                            sp.wait_ge(S["mixed_ready"], 2)
                        if s == 2:
                            sp.wait_ge(S["ps"], U_OUT[1] + 4)
                    else:
                        sp.wait_ge(S["moe_up"], e * FT_E + (ft + 1 - FT_E))
                    for i, w in enumerate((m_w1, m_w3)):
                        src = w[bass.ds(e, 1), :, :, ft * P:ft * P + P].rearrange("e p k c -> p (e k) c")
                        sp.dma_start(slot(s)[:, :, i * P:i * P + P], src).then_inc(full[s], 16)
                if first:
                    sp.wait_ge(S["x_ready_d"], 3)
                    sp.wait_ge(S["x_ready_a"], 3)
                else:
                    sp.wait_ge(S["w2_used"], e)
                for j in range(6):
                    nk = min(2, FT_E - 2 * j)
                    src = m_w2[bass.ds(e, 1), :, 2 * j:2 * j + nk, :].rearrange("e p k c -> p (e k) c")
                    refill(11 + j, W2[:, 2 * j:2 * j + nk, :], src)
            expert(0, True)
            with sp.Fori(1, NE) as e:
                expert(e, False)
            sp.wait_ge(S["y_rows_a"], 1)
            sp.wait_ge(S["y_rows_d"], 1)
            yp = out["y_prompt"].rearrange("a (t p) d -> (a t) p d", p=P)
            for t in range(2):
                sp.dma_start(yp[t], xtok[:, t]).then_inc(S["y_stored"], 16)
            sp.dma_start(out["y_sample"].rearrange("b t d -> (b t) d"), xtok[0:NS, 2]).then_inc(S["y_stored"], 16)
            sp.wait_ge(S["y_stored"], 48)

        @block.gpsimd
        def _(pool):
            pool.dma_start(GB[:, 0, :], A["mlstm_bi"].rearrange("l h -> h l"), allow_slow_non_contiguous=True).then_inc(S["small_in"], 16)
            pool.dma_start(GB[:, 1, :], A["mlstm_bf"].rearrange("l h -> h l"), allow_slow_non_contiguous=True).then_inc(S["small_in"], 16)
            pool.dma_start(M0[:, :, :], A["state_mlstm_m"].rearrange("l b h -> h l b"), allow_slow_non_contiguous=True).then_inc(S["small_in"], 16)
            pool.dma_start(RW[:, :, :], A["moe_router"][0].rearrange("(k p) e -> p k e", p=P)).then_inc(S["small_in"], 16)
            pool.dma_start(RB[:, :], A["moe_router_b"][0:1, :].to_broadcast([P, NE])).then_inc(S["small_in"], 16)
            pool.memset(LW[:, :, :, :], 0.0).then_inc(S["lru_zeroed"], 1)
            pool.wait_ge(S["lru_zeroed"], 1)
            for l in range(DEPTH):
                if l:
                    pool.wait_ge(S["lru_ps"], l)
                for ri, name in enumerate(("lru_wr", "lru_wi")):
                    src = A[name][l].rearrange("(p h) i j -> h i p j", h=2)
                    for h in range(2):
                        pool.dma_start(LW[HD * h:HD * h + HD, ri, :, HD * h:HD * h + HD], src[h]
                                       ).then_inc(S["lru_in"], 16)
                if l:
                    pool.wait_ge(S["states_stored"], 16 * STORES * l)
                for kind, name in enumerate(("state_mlstm_C", "state_ret_S", "state_hgrn_S")):
                    for p in range(2):
                        pool.dma_start(s0(kind)[:, p], state_view(A[name], l, 0, NB)[:, p]).then_inc(S["s0_in"], 16)
                for kind, ready in ((1, S["vm_r"]), (0, S["vm_m"]), (2, S["vm_h"])):
                    pool.wait_ge(S["v_tok"], l + 1)
                    if kind == 1:
                        pool.wait_ge(S["a_done"], l + 1)
                        pool.wait_ge(S["rot_done"], l + 1)
                    elif kind == 0:
                        pool.wait_ge(S["rst_ps"], l + 1)
                    else:
                        pool.wait_ge(S["hl_ps"], NL * (l + 1))
                    pool.tensor_tensor(
                        Vm, VT[0:NS, 2, kind * 256:kind * 256 + 256].rearrange("p (h v) -> p h v", h=NH)
                        .unsqueeze(2).to_broadcast([NS, NH, NB, HD]),
                        tb("batchmask").unsqueeze(1).unsqueeze(3).to_broadcast([NS, NH, NB, HD]),
                        ALU.mult).then_inc(ready, 1)
                def store(dst, src, **kw):
                    pool.dma_start(dst, src, **kw).then_inc(S["states_stored"], 16)
                for kind, done, tail in ((1, S["rst_done"], "ret_S"), (0, S["mst_done"], "mlstm_C"),
                                         (2, S["hst_done"], "hgrn_S")):
                    pool.wait_ge(done, l + 1)
                    store(state_view(out["prompt_" + tail], l, 0, 1)[:, :, 0], PFIN[:, kind])
                    for p in range(2):
                        store(state_view(out["sample_" + tail], l, 0, NB)[:, p], s0(kind)[:, p])
                    if kind == 0:
                        store(out["prompt_mlstm_m"][l].rearrange("b h -> h b"), M1[:, 0:1], allow_slow_non_contiguous=True)
                        store(out["sample_mlstm_m"][l].rearrange("b h -> h b"), M1[:, 1:1 + NB],
                              allow_slow_non_contiguous=True)
                pool.wait_ge(S["orow_done"], l + 1)
                store(out["prompt_rglru_conv"][l].rearrange("b c (w p) -> (b c w) p", p=P), OROW[0:6, :])
                store(out["sample_rglru_conv"][l].rearrange("b c (w p) -> (b c w) p", p=P), OROW[6:54, :])
                store(out["prompt_rglru_h"][l].rearrange("b (w p) -> (b w) p", p=P), OROW[54:56, :])
                store(out["sample_rglru_h"][l].rearrange("b (w p) -> (b w) p", p=P), OROW[56:72, :])
                store(out["prompt_mlstm_n"][l].rearrange("b (w h) d -> (b w) (h d)", h=2), OROW[72:74, :])
                store(out["sample_mlstm_n"][l].rearrange("b (w h) d -> (b w) (h d)", h=2), OROW[74:90, :])
            pool.wait_ge(S["states_stored"], 16 * DEPTH * STORES)

        @block.tensor
        def _(pe):
            def mm(o, lhsT, rhs, start=True, stop=True):
                return pe.matmul(o, lhsT, rhs, start=start, stop=stop)

            def tr(o, src, k):
                return pe.transpose(o, src, ident[0:k, 0:k])

            pe.wait_ge(S["tables_in"], 16)
            pe.wait_ge(S["inputs_in"], 16 * N_INPUTS)
            tr(PS[:, 0, 0:NVEC], vrows[0:NVEC, :], NVEC)
            tr(PS[:, 1, 0:P], srows, P)
            tr(PS[:, 1, P:P + 32], nrows[0:32, :], 32).then_inc(S["cols_ps"], 1)
            for t in range(3):
                n = P if t < 2 else NS
                for k in range(KT):
                    last = tr(PS[:, 2 + 2 * t + k // 4, (k % 4) * P:(k % 4) * P + n],
                              xtok[0:n, t, k * P:k * P + P], n)
            last.then_inc(S["x_ps"], 1)

            def layer_norm(q, src, summed, count):
                pe.wait_ge(summed, count)
                for k in range(KT):
                    last = mm(PS[:, 6, 0:T], tb("lnmean"), src[:, k], k == 0, k == KT - 1)
                last.then_inc(S["ln_mean_ps"], 1)
                for k in range(KT):
                    if k % 4 == 0:
                        pe.wait_ge(S["ln_sq"], 2 * q + k // 4 + 1)
                    last = mm(PS[:, 7, 0:T], tb("lnmean"), SQ[:, k], k == 0, k == KT - 1)
                last.then_inc(S["ln_var_ps"], 1)

            def tile_out(bank, w, nk, rhs, k0=0, kend=None):
                kend = nk if kend is None else kend
                for k in range(nk):
                    last = mm(PS[:, bank, 0:T], w(k), rhs[:, k0 + k], k0 + k == 0, k0 + k == kend - 1)
                return last

            def mix(l):
                done = l + 1
                pe.wait_ge(S["gate_weights_in"], 16 * done)
                for k in range(KT):
                    last = mm(PS[0:8, 6, 0:T], WG[:, k, :], X[:, k], k == 0, k == KT - 1)
                last.then_inc(S["g_ps"], 1)
                pe.wait_ge(S["ev_a"], A_IN[l] + 14)
                pe.wait_ge(S["ev_d"], D_IN[l] + 14)
                for t in range(3):
                    n = P if t < 2 else NS
                    for i, tile in enumerate((VB, VB + 1, VC, VC + 1, ID, ID + 1)):
                        last = tr(PS[0:n, 2 * t + i // 3, (i % 3) * P:(i % 3) * P + P],
                                  proj[:, tile, t * P:t * P + n], P)
                last.then_inc(S["v_ps"], 1)
                pe.wait_ge(S["g_sb"], done)
                mm(PS[0:NH, 7, 0:T], ident[0:8, 0:NH], gsb)
                mm(PS[0:NH, 6, 0:T], ident[0:8, NH:8], gsb).then_inc(S["gif_ps"], 1)
                pe.wait_ge(S["v_tok"], done)
                for i in range(4):
                    last = mm(PS[:, i, 0:T], tb("swap"), proj[:, QC + i])
                last.then_inc(S["swap_ps"], 1)
                pe.wait_ge(S["xc_ready"], done)
                pe.wait_ge(S["lru_in"], 64 * done)
                pe.wait_ge(S["li_done"], done)
                for ri in range(2):
                    for p in range(2):
                        last = mm(PS[:, 4 + 2 * ri + p, 0:WC], LW[:, ri, p, :], A2["xc"][:, p, 0:WC])
                last.then_inc(S["lru_ps"], 1)

                def rows_of(h):
                    return HD * (h % 2), h // 2

                def scores(q, k, ready):
                    for h in range(NH):
                        r, p = rows_of(h)
                        kk, qq = proj[r:r + HD, k + p], proj[r:r + HD, q + p]
                        mm(PS[:, h, 0:SEQ], kk[:, 0:P], qq[:, 0:SEQ])
                        mm(PS[:, h, SEQ:SEQ + P], kk[:, P:SEQ], qq[:, P:SEQ])
                        last = mm(PS[0:NS, h, SEQ + P:WS], kk[:, SEQ:T], qq[:, SEQ:T])
                    last.then_inc(ready, 1)

                def keys(src, ready):
                    for t in range(3):
                        n = P if t < 2 else NS
                        for p in range(2):
                            at = (t % 2) * 256 + p * P
                            last = tr(PS[0:n, 6 + t // 2, at:at + P], src(p)[:, t * P:t * P + n], P)
                    last.then_inc(ready, 1)

                def outputs(bank, kind, v, carry):
                    for h in range(NH):
                        r, p = rows_of(h)
                        o = PS[r:r + HD, bank + p]
                        mm(o[:, 0:SEQ], v(0, h), WT[:, h, 0:SEQ], True, False)
                        mm(o[:, P:SEQ], v(1, h), WT[:, h, SEQ:SEQ + P], False, True)
                        mm(o[:, SEQ:T], v(2, h), WT[0:NS, h, SEQ + P:WS], True, False)
                        for b in range(NB):
                            c = slice(DSEQ * b, DSEQ * b + DSEQ)
                            last = mm(o[:, SEQ + DSEQ * b:SEQ + DSEQ * b + DSEQ], carry(r, p, b),
                                      QH[r:r + HD, kind, p, c], False, b == NB - 1)
                    return last

                def value(kind):
                    return lambda t, h: VT[0:(P if t < 2 else NS), t, kind * 256 + h * HD:kind * 256 + h * HD + HD]

                def key(buf, t, h):
                    return KTK[0:(P if t < 2 else NS), buf, t, h * HD:h * HD + HD]

                def sample_states(buf, bank):
                    for h in range(NH):
                        r, p = rows_of(h)
                        last = mm(PS[r:r + HD, bank + p, :], key(buf, 2, h), Vm[:, h].rearrange("p b v -> p (b v)"))
                    return last

                pe.wait_ge(S["rot_done"], done)
                scores(QC, KC, S["rs_ps"])
                pe.wait_ge(S["lru_read"], done)
                keys(lambda p: proj[:, KC + p], S["rk_ps"])
                pe.wait_ge(S["rw_done"], done)
                pe.wait_ge(S["s0_in"], 96 * done)
                outputs(4, 1, value(1), lambda r, p, b: s0(1)[r:r + HD, p, b, :]).then_inc(S["ry_ps"], 1)
                pe.wait_ge(S["rk_done"], done)
                for h in range(NH):
                    r, p = rows_of(h)
                    o = PS[r:r + HD, 6, p * HD:p * HD + HD]
                    mm(o, key(1, 0, h), value(1)(0, h), True, False)
                    mm(o, key(1, 1, h), value(1)(1, h), False, True)
                pe.wait_ge(S["vm_r"], done)
                sample_states(1, 0).then_inc(S["rst_ps"], 1)
                pe.wait_ge(S["mrow_done"], done)
                for t in range(3):
                    n = P if t < 2 else NS
                    for k, row in enumerate((rli, rtmp)):
                        last = tr(PS[0:n, 7, t * 8 + k * 4:t * 8 + k * 4 + 4], row[:, t * P:t * P + n], NH)
                last.then_inc(S["mcol_ps"], 1)
                pe.wait_ge(S["ry_done"], done)
                for p in range(2):
                    mm(PS[:, 4 + p, 0:T], tb("selpair")[:, p], rlf)
                    last = mm(PS[:, 4 + p, T:T + NS], tb("selpair")[:, p], risc)
                last.then_inc(S["mb_ps"], 1)
                pe.wait_ge(S["rst_done"], done)
                for h in range(NH):
                    sel = ident[0:NH, h:h + 1].to_broadcast([NH, P])
                    mm(PS[:, h, 0:WS], ident, tb("causal"), True, False)
                    mm(PS[:, h, 0:SEQ], sel, rb[:, 0:SEQ], False, False)
                    mm(PS[:, h, SEQ:SEQ + P], sel, rb[:, P:SEQ], False, False)
                    last = mm(PS[:, h, SEQ + P:WS], sel, rb[:, SEQ:T], False, True)
                last.then_inc(S["ma_ps"], 1)
                pe.wait_ge(S["me_done"], done)
                scores(QB, KB, S["ms_ps"])
                pe.wait_ge(S["mcol_done"], done)
                keys(lambda p: proj[:, KB + p], S["mk_ps"])
                pe.wait_ge(S["mw_done"], done)
                pe.wait_ge(S["mq_done"], done)
                pe.wait_ge(S["mb_done"], done)
                outputs(4, 0, value(0), lambda r, p, b: s0(0)[r:r + HD, p, b, :])
                outputs(0, 0, lambda t, h: onesc[0:(P if t < 2 else NS), 0:HD],
                        lambda r, p, b: STC[r:r + HD, 128 + 16 * l + 2 * b + p:129 + 16 * l + 2 * b + p]
                        .to_broadcast([HD, HD])).then_inc(S["my_ps"], 1)
                pe.wait_ge(S["mk_done"], done)
                for h in range(NH):
                    r, p = rows_of(h)
                    for c, n, rhs in ((p * HD, HD, lambda t: value(0)(t, h)), (P + p, 1, lambda t: onesc[:, 0:1])):
                        o = PS[r:r + HD, 6, c:c + n]
                        mm(o, key(0, 0, h), rhs(0), True, False)
                        mm(o, key(0, 1, h), rhs(1), False, True)
                    mm(PS[r:r + HD, 6, P + 8 + 8 * p:P + 16 + 8 * p], key(0, 2, h), tb("batchmask"))
                pe.wait_ge(S["vm_m"], done)
                sample_states(0, 2).then_inc(S["mst_ps"], 1)
                pe.wait_ge(S["my_done"], done)
                pe.wait_ge(S["mst_done"], done)
                for e in range(NL):
                    lo = 2 * (e % 2)
                    pe.wait_ge(S["hl_ready"], (NL - 1) * l + min(e + 1, NL - 1))
                    if e >= 2:
                        pe.wait_ge(S["hl_done"], NL * l + e - 1)
                    qq, kk = (C2[lo], C2[lo + 1]) if e < NL - 1 else (C2[5], C2[4])
                    for h in range(NH):
                        r, p = rows_of(h)
                        for c in range(2):
                            last = mm(PS[:, lo + h % 2, (2 * c + p) * P:(2 * c + p) * P + P],
                                      kk[r:r + HD, p, c * P:c * P + P], qq[r:r + HD, p, c * P:c * P + P])
                        if e >= NL - 3:
                            last = mm(PS[0:NS, 4 + lo + h % 2, p * NS:p * NS + NS], kk[r:r + HD, p, SEQ:T],
                                      qq[r:r + HD, p, SEQ:T])
                    last.then_inc(S["hl_ps"], 1)
                pe.wait_ge(S["hk_ready"], done)
                keys(lambda p: C2[8][:, p], S["hk_ps"])
                pe.wait_ge(S["hk_done"], done)
                for c in range(2):
                    for h in range(NH):
                        r, p = rows_of(h)
                        last = mm(PS[r:r + HD, 6 + c, p * HD:p * HD + HD], key(0, c, h), value(2)(c, h))
                    last.then_inc(S["hc_ps"], 1)
                pe.wait_ge(S["hl_done"], NL * done)
                pe.wait_ge(S["hc_done"], done)
                for h in range(NH):
                    r, p = rows_of(h)
                    o = PS[r:r + HD, 4 + p]
                    mm(o[:, 0:P], value(2)(0, h), AT[:, 0, h])
                    mm(o[:, P:SEQ], value(2)(1, h), AT[:, 1, h], True, False)
                    mm(o[:, P:SEQ], SC0[r:r + HD, p], C2[7][r:r + HD, p, P:SEQ], False, True)
                    mm(o[:, SEQ:T], value(2)(2, h), ATs[:, h], True, False)
                    for b in range(NB):
                        c = slice(SEQ + DSEQ * b, SEQ + DSEQ * b + DSEQ)
                        last = mm(o[:, c], s0(2)[r:r + HD, p, b, :], C2[7][r:r + HD, p, c], False, b == NB - 1)
                last.then_inc(S["hy_ps"], 1)
                pe.wait_ge(S["vm_h"], done)
                sample_states(0, 2).then_inc(S["hst_ps"], 1)
                for i in range(4):
                    if i == 2:
                        pe.wait_ge(S["hst_done"], done)
                    last = mm(PS[:, (0, 1, 6, 7)[i], 0:T], tb("headmean"), Y[:, i])
                last.then_inc(S["mean_ps"], 1)
                pe.wait_ge(S["sq6_done"], done)
                for i in range(6):
                    last = mm(PS[:, i, 0:T], tb("headmean"), SQ6[:, i])
                last.then_inc(S["var_ps"], 1)
                pe.wait_ge(S["outc_done"], done)
                pe.wait_ge(S["centered"], done)
                tr(PS[0:90, 6, 0:P], OUTC[:, 0:90], P).then_inc(S["orow_ps"], 1)

            for l in range(DEPTH):
                pe.wait_ge(S["ev_a"], A_IN[l])
                pe.wait_ge(S["ev_d"], D_IN[l])
                if l:
                    pe.wait_ge(S["x_ready_a"], 2 * l)
                    pe.wait_ge(S["x_ready_d"], 2 * l)
                with pe.Fori(0, 7) as i:
                    for h in range(2):
                        pe.wait_ge(full[h], i * 16 + 16 * ((LOADS_L1[h] if l else 0) + 1))
                        pe.wait_ge(S["ev_a"], i * 2 + (A_IN[l] + h - 1))
                        pe.wait_ge(S["ev_d"], i * 2 + (D_IN[l] + h - 1))
                        for b in range(2):
                            last = tile_out(2 * h + b, lambda k: slot(h)[:, k, b * P:b * P + P], KT, X)
                        last.then_inc(S["ps"], 1)
                mix(l)
                pe.wait_ge(S["mixed_ready"], l + 1)
                for u in range(4):
                    s = 2 + u
                    pe.wait_ge(full[s], 16 * ((LOADS_L1[s] if l else 0) + 1))
                    if u >= 2:
                        pe.wait_ge(S["ev_d"], D_OUT[l] + u - 1)
                    for b in range(2):
                        last = tile_out(2 * (u % 2) + b, lambda k: slot(s)[:, k, b * P:b * P + P], KT, mixed)
                    last.then_inc(S["ps"], 1)
                pe.wait_ge(S["orow_done"], l + 1)
                layer_norm(2 * l, X, S["ev_d"], D_OUT[l] + 4)
                pe.wait_ge(S["x_ready_a"], 2 * l + 1)
                pe.wait_ge(S["x_ready_d"], 2 * l + 1)
                if l == 0:
                    def up(n, h):
                        for j, s in enumerate(UP_SLOTS[h]):
                            pe.wait_ge(full[s], n * 8 + (16 * ((0, 7)[h] + 1) - 8 * h))
                            for b in range(2):
                                last = tile_out(4 * h + 2 * j + b, lambda k: slot(s)[:, k, b * P:b * P + P], KT, X)
                        last.then_inc(S["ps"], 1)
                    pe.wait_ge(S["ev_d"], D_UP)
                    with pe.Fori(0, 5) as i:
                        for h in range(2):
                            pe.wait_ge(S["ev_d"], i * 2 + (D_UP + h - 1))
                            up(i * 2 + h, h)
                    pe.wait_ge(S["ev_d"], D_UP + 9)
                    up(10, 0)
                    pe.wait_ge(S["ev_d"], D_UP + 11)
                    for m in range(4):
                        if m >= 2:
                            pe.wait_ge(S["ev_d"], D_DOWN + m - 1)
                        for j, s in enumerate(DOWN_SLOTS[m % 2]):
                            before = (1, 0)[m % 2] + m // 2
                            pe.wait_ge(full[s], 16 * (before + 1))
                        for b in range(2):
                            for j, s in enumerate(DOWN_SLOTS[m % 2]):
                                last = tile_out(2 * (m % 2) + b, lambda k: slot(s)[:, k, b * P:b * P + P],
                                                min(8, 22 - 8 * j), hid, 8 * j, 22)
                        last.then_inc(S["ps"], 1)
                    layer_norm(1, X, S["ev_d"], D_DOWN + 4)
            pe.wait_ge(S["small_in"], 16 * 5)
            for t in range(3):
                n = P if t < 2 else NS
                for k in range(KT):
                    last = mm(PS[0:n, 0, t * NE:t * NE + NE], X[:, k, t * P:t * P + n], RW[:, k], k == 0, k == KT - 1)
            last.then_inc(S["logits_ps"], 1)
            for t in range(3):
                n = P if t < 2 else NS
                for k in range(KT):
                    last = tr(PS[0:n, 2 + 2 * t + k // 4, (k % 4) * P:(k % 4) * P + P], X[:, k, t * P:t * P + n], P)
            last.then_inc(S["xtk_ps"], 1)
            pe.wait_ge(S["gates_done"], 1)
            for bank, src in ((1, GTOK), (0, SEL)):
                for t in range(3):
                    n = P if t < 2 else NS
                    last = tr(PS[0:NE, bank, t * P:t * P + n], src[0:n, t], n)
            last.then_inc(S["gt_ps"], 1)
            pe.wait_ge(S["slots_done"], 1)
            pe.wait_ge(S["xtk_done"], 1)
            for t in range(3):
                n = P if t < 2 else NS
                tr(PS[0:n, 2, t * NE:t * NE + NE], PROW[:, t * P:t * P + n], NE)
            tr(PS[0:1, 3, 0:NE], CNT, NE).then_inc(S["pt_ps"], 1)
            pe.wait_ge(S["flag_ready"], 1)
            for e in range(NE):
                last = mm(PS[:, e, 0:T], ident[0:NE, e:e + 1].to_broadcast([NE, P]), GROW)
            last.then_inc(S["gbc_ps"], 1)
            dense = pe.value_load(FLAG[0:1, 0:1], min_val=0, max_val=1)

            def gather(n):
                pe.wait_ge(S["sel_ready"], n + 1)
                for k in range(KT):
                    for t in range(3):
                        r = P if t < 2 else NS
                        last = mm(PS[:, 6 + k // 4, (k % 4) * CAP:(k % 4) * CAP + CAP],
                                  XTK[0:r, t, k * P:k * P + P], SELT[0:r, t], t == 0, t == 2)
                last.then_inc(S["ga_ps"], 1)

            def gathered_expert(e, final):
                pe.wait_ge(S["xe_done"], e + 1)
                for ft in range(FT_E):
                    s = E_SLOTS[ft]
                    pe.wait_ge(full[s], e * 32 + (16 * LOADS_MOE[s] + 32))
                    if ft >= 2:
                        pe.wait_ge(S["moe_h"], e * FT_E + (ft - 1))
                    for b in range(2):
                        for k in range(KT):
                            last = mm(PS[:, ft % 2, b * CAP:b * CAP + CAP], slot(s)[:, k, b * P:b * P + P],
                                      XE[:, k], k == 0, k == KT - 1)
                    last.then_inc(S["moe_up"], 1)
                if not final:
                    gather(e + 1)
                pe.wait_ge(S["moe_h"], e * FT_E + FT_E)
                for j in range(6):
                    pe.wait_ge(full[11 + j], e * 16 + 16)
                for h in range(2):
                    for ft in range(FT_E):
                        last = mm(PS[0:CAP, 2 + h, :], hid_g[:, ft], W2[:, ft, 512 * h:512 * h + 512],
                                  ft == 0, ft == FT_E - 1)
                    last.then_inc(S["dn_ps"], 1)
                for k in range(KT):
                    if k % 4 == 0:
                        pe.wait_ge(S["yt_done"], e * 2 + (k // 4 + 1))
                    if k >= 2:
                        pe.wait_ge(S["sc_ev"], e * KT + (k - 1))
                    mm(PS[:, 4 + k % 2, 0:T], YTK[:, k * P:k * P + P],
                       SG[:, bass.ds(e, 1), :].rearrange("p e t -> p (e t)")).then_inc(S["sc_ps"], 1)
                    if k == 0:
                        pe.wait_ge(S["dn_ps"], e * 2 + 2)
                        pe.sem_inc(S["w2_used"], 1)

            with pe.If(dense):
                pe.wait_ge(S["gbc_done"], 1)
                with pe.Fori(0, NE) as e:
                    for ft in range(FT_E):
                        s = E_SLOTS[ft]
                        pe.wait_ge(full[s], e * 32 + (16 * LOADS_MOE[s] + 32))
                        if ft >= 2:
                            pe.wait_ge(S["moe_h"], e * FT_E + (ft - 1))
                        for b in range(2):
                            last = tile_out(2 * (ft % 2) + b, lambda k: slot(s)[:, k, b * P:b * P + P], KT, X)
                        last.then_inc(S["moe_up"], 1)
                    pe.wait_ge(S["moe_h"], e * FT_E + FT_E)
                    for j in range(6):
                        pe.wait_ge(full[11 + j], e * 16 + 16)
                    for m in range(KT):
                        if m >= 2:
                            pe.wait_ge(S["moe_y"], e * KT + (m - 1))
                        tile_out(4 + m % 2, lambda k: W2[:, k, m * P:m * P + P], FT_E, hid_e).then_inc(S["dn_ps"], 1)
                    pe.wait_ge(S["dn_ps"], e * KT + KT)
                    pe.sem_inc(S["w2_used"], 1)
            with pe.Else():
                pe.wait_ge(S["gbc_done"], 1)
                for e in range(NE):
                    mm(PS[:, e, 0:T], ident[0:NE, e:e + 1].to_broadcast([NE, P]), PROW).then_inc(S["pb_ps"], 1)
                pe.wait_ge(S["sg_done"], 1)
                gather(0)
                with pe.Fori(0, NE - 1) as e:
                    gathered_expert(e, False)
                gathered_expert(NE - 1, True)
            layer_norm(3, X, S["moe_sum"], 1)
            pe.wait_ge(S["x_ready_a"], 4)
            pe.wait_ge(S["x_ready_d"], 4)
            for t in range(3):
                n = P if t < 2 else NS
                for k in range(KT):
                    last = tr(PS[0:n, 2 * t + k // 4, (k % 4) * P:(k % 4) * P + P], X[:, k, t * P:t * P + n], P)
            last.then_inc(S["y_ps"], 1)

        @block.scalar
        def _(act):
            def f(o, i, fn, **kw):
                return act.activation(o, i, fn, **kw)

            act.wait_ge(S["x_ps"], 1)
            f(X[:, 4:8, 0:P], PS[:, 3, :].rearrange("p (k t) -> p k t", k=4), ACT.Copy)
            f(X[:, 4:8, P:SEQ], PS[:, 5, :].rearrange("p (k t) -> p k t", k=4), ACT.Copy)
            f(X[:, 4:8, SEQ:T], PS[:, 7, :].rearrange("p (k t) -> p k t", k=4)[:, :, 0:NS], ACT.Copy
              ).then_inc(S["ev_a"], 2)
            act.wait_ge(S["prep_e"], 1)
            f(N0S[:, 0:4], N0S[:, 0:4], ACT.Exp).then_inc(S["prep_exp"], 1)
            act.wait_ge(S["prep_s"], 1)
            f(N0S[:, 40:44], N0S[:, 40:44], ACT.Exp).then_inc(S["prep_exp"], 1)

            def layer_norm(q, l, g, b):
                for h in range(2):
                    act.wait_ge(S["ln_xc"], 2 * q + h + 1)
                    f(SQ[:, 4 * h:4 * h + 4], X[:, 4 * h:4 * h + 4], ACT.Square).then_inc(S["ln_sq"], 1)
                act.wait_ge(S["ln_var_ps"], q + 1)
                f(SDEV, PS[:, 7, 0:T], ACT.Sqrt, bias=LN_EPS).then_inc(S["ln_sd"], 1)
                act.wait_ge(S["ln_xn"], q + 1)
                for k in range(4):
                    last = f(X[:, k], X[:, k], ACT.Identity, scale=vec[g][:, KT * l + k:KT * l + k + 1],
                             bias=vec[b][:, KT * l + k:KT * l + k + 1])
                last.then_inc(S["x_ready_a"], 1)

            def mix(l):
                done = l + 1
                act.wait_ge(S["v_ps"], done)
                for t in range(3):
                    n = P if t < 2 else NS
                    for i in range(2):
                        last = f(VT[0:n, t, 384 * i:384 * i + 384], PS[0:n, 2 * t + i, 0:384], ACT.Copy)
                last.then_inc(S["v_tok"], 1)
                act.wait_ge(S["mz"], done)
                f(rtmp, rtmp, ACT.Exp, scale=-1.0).then_inc(S["act_chain"], 1)
                act.wait_ge(S["act_chain"], done)
                f(rtmp, rtmp, ACT.Ln, bias=1.0).then_inc(S["m_ln"], 1)
                f(C2[7], proj[:, GA:GA + 2], ACT.Square).then_inc(S["gl_sq"], 1)
                act.wait_ge(S["lru_ps"], done)
                for ri, name in enumerate(("r", "ig")):
                    for p in range(2):
                        c = 2 * l + p
                        last = f(A2[name][:, p, 0:WC], PS[:, 4 + 2 * ri + p, 0:WC], ACT.Tanh, scale=0.5,
                                 bias=vec[("lru_br", "lru_bi")[ri]][:, c:c + 1])
                last.then_inc(S["lru_read"], 1)
                act.wait_ge(S["gl_in"], done)
                f(C2[7], C2[7], ACT.Tanh).then_inc(S["gl_tanh"], 1)
                act.wait_ge(S["la_ready"], done)
                f(A2["a"][:, :, 0:WC], A2["r"][:, :, 0:WC], ACT.Exp)
                f(A2["h"][:, :, 0:WC], A2["r"][:, :, 0:WC], ACT.Tanh).then_inc(S["a_exp"], 1)
                act.wait_ge(S["om_ready"], done)
                f(A2["om"][:, :, 0:WC], A2["om"][:, :, 0:WC], ACT.Sqrt, scale=-1.0).then_inc(S["a_sqrt"], 1)
                act.wait_ge(S["m_rows"], done)
                f(rlf, rm, ACT.Exp, scale=-1.0)
                f(risc, risc, ACT.Exp)
                f(rtmp, rtmp, ACT.Exp).then_inc(S["mrow_done"], 1)
                act.wait_ge(S["mb_ps"], done)
                act.wait_ge(S["a_done"], done)
                f(embc, PS[:, 4:6, 0:T + NS], ACT.Copy).then_inc(S["mb_done"], 1)
                act.wait_ge(S["ma_ps"], done)
                act.wait_ge(S["mcol_done"], done)
                for h in range(NH):
                    f(E[:, h, 0:SEQ], PS[:, h, 0:SEQ], ACT.Exp, bias=mcol[:, 0, 0, h:h + 1])
                    f(E[:, h, SEQ:SEQ + P], PS[:, h, SEQ:SEQ + P], ACT.Exp, bias=mcol[:, 1, 0, h:h + 1])
                    last = f(E[0:NS, h, SEQ + P:WS], PS[0:NS, h, SEQ + P:WS], ACT.Exp, bias=mcol[0:NS, 2, 0, h:h + 1])
                last.then_inc(S["me_done"], 1)
                act.wait_ge(S["hf_ready"], done)
                f(C2[4], C2[4], ACT.Exp).then_inc(S["hf_exp"], 1)
                act.wait_ge(S["hg_ready"], done)
                f(C2[5], proj[:, QD:QD + 2], ACT.Tanh, scale=0.5).then_inc(S["hq_tanh"], 1)
                f(C2[7], C2[7], ACT.Ln)
                f(C2[8], C2[8], ACT.Ln).then_inc(S["hg_ln"], 1)
                for e, s in enumerate(LEVELS):
                    act.wait_ge(S["hx"], len(LEVELS) * l + e + 1)
                    left, right = level_view(C2[7 + e % 2], s)
                    f(right, right, ACT.Exp)
                    f(left, left, ACT.Exp, scale=-1.0).then_inc(S["hz"], 1)
                act.wait_ge(S["hi_ready"], done)
                f(C2[7], C2[6], ACT.Exp)
                f(C2[8], C2[8], ACT.Exp)
                f(GE[:, :, 0:1], C2[6][:, :, SEQ - 1:SEQ], ACT.Exp)
                f(GE[:, :, 1:1 + NB], C2[6][:, :, SEQ + DSEQ - 1:T:DSEQ], ACT.Exp).then_inc(S["hi_exp"], 1)
                act.wait_ge(S["hk_ready"], done)
                for i, tile in enumerate((OB, GC, GD)):
                    last = f(TH[:, 2 * i:2 * i + 2], proj[:, tile:tile + 2], ACT.Tanh, scale=0.5)
                last.then_inc(S["th_done"], 1)
                act.wait_ge(S["centered"], done)
                f(SQ6, Y, ACT.Square).then_inc(S["sq6_done"], 1)
                act.wait_ge(S["var_ps"], done)
                f(SD6, PS[:, 0:6, 0:T], ACT.Sqrt, bias=HEAD_EPS).then_inc(S["sd6_done"], 1)
                act.wait_ge(S["orow_ps"], done)
                f(OROW[0:90, :], PS[0:90, 6, 0:P], ACT.Copy).then_inc(S["orow_done"], 1)

            for l in range(DEPTH):
                with act.Fori(0, 7) as i:
                    for h in range(2):
                        act.wait_ge(S["ps"], i * 2 + (U_IN[l] + h + 1))
                        f(proj[:, bass.ds(i * 4 + 2 * h, 1), :], PS[:, 2 * h:2 * h + 1, 0:T], ACT.Copy
                          ).then_inc(S["ev_a"], 1)
                act.wait_ge(S["ev_a"], A_IN[l] + 14)
                act.wait_ge(S["ev_d"], D_IN[l] + 14)
                mix(l)
                layer_norm(2 * l, l, "ln_mix_g", "ln_mix_b")
                if l == 0:
                    def up(n, h):
                        act.wait_ge(S["ps"], n + (U_UP + 1))
                        act.wait_ge(S["ev_d"], n + (D_UP - 1))
                        f(sil[:, 2 * h:2 * h + 2], PS[:, 4 * h:4 * h + 2, 0:T], ACT.Silu).then_inc(S["sl"], 1)
                    with act.Fori(0, 5) as i:
                        for h in range(2):
                            up(i * 2 + h, h)
                    up(10, 0)
                    layer_norm(1, 0, "ln_ffn_g", "ln_ffn_b")
            act.wait_ge(S["xtk_ps"], 1)
            act.wait_ge(S["states_stored"], 16 * STORES * DEPTH)
            for t in range(3):
                n = P if t < 2 else NS
                for i in range(2):
                    last = f(XTK[0:n, t, 512 * i:512 * i + 512], PS[0:n, 2 + 2 * t + i, :], ACT.Copy)
            last.then_inc(S["xtk_done"], 1)
            act.wait_ge(S["lg_ready"], 1)
            f(PR, LG, ACT.Exp).then_inc(S["pr_exp"], 1)
            act.wait_ge(S["gbc_ps"], 1)
            for e in range(NE):
                last = f(GBC[:, e], PS[:, e, 0:T], ACT.Copy)
            last.then_inc(S["gbc_done"], 1)
            dense = act.value_load(FLAG[0:1, 0:1], min_val=0, max_val=1)

            def tokens(n):
                act.wait_ge(S["ga_ps"], n + 1)
                for i in range(2):
                    last = f(XE[:, 4 * i:4 * i + 4], PS[:, 6 + i, 0:4 * CAP].rearrange("p (k c) -> p k c", k=4), ACT.Copy)
                last.then_inc(S["xe_done"], 1)

            def gathered_expert(e, final):
                for ft in range(FT_E):
                    act.wait_ge(S["moe_up"], e * FT_E + (ft + 1))
                    if ft >= 2:
                        act.wait_ge(S["moe_h"], e * FT_E + (ft - 1))
                    f(sil_g[:, ft % 2], PS[:, ft % 2, 0:CAP], ACT.Silu).then_inc(S["moe_s"], 1)
                if not final:
                    tokens(e + 1)
                for h in range(2):
                    act.wait_ge(S["dn_ps"], e * 2 + (h + 1))
                    f(YTK[:, 512 * h:512 * h + 512], PS[0:CAP, 2 + h, :], ACT.Copy).then_inc(S["yt_done"], 1)

            with act.If(dense):
                with act.Fori(0, NE) as e:
                    for ft in range(FT_E):
                        act.wait_ge(S["moe_up"], e * FT_E + (ft + 1))
                        if ft >= 2:
                            act.wait_ge(S["moe_h"], e * FT_E + (ft - 1))
                        f(sil_e[:, ft % 2], PS[:, 2 * (ft % 2), 0:T], ACT.Silu).then_inc(S["moe_s"], 1)
            with act.Else():
                tokens(0)
                with act.Fori(0, NE - 1) as e:
                    gathered_expert(e, False)
                gathered_expert(NE - 1, True)
            layer_norm(3, 1, "ln_ffn_g", "ln_ffn_b")
            act.wait_ge(S["y_ps"], 1)
            for t in range(3):
                n = P if t < 2 else NS
                last = f(xtok[0:n, t, 0:512], PS[0:n, 2 * t, :], ACT.Copy)
            last.then_inc(S["y_rows_a"], 1)

        @block.vector
        def _(v):
            chain = [0]

            def link(ins):
                chain[0] += 1
                ins.then_inc(S["dve_chain"], 1)
                v.wait_ge(S["dve_chain"], chain[0])

            def sig(ins, s, n):
                ins.then_inc(s, 1)
                v.wait_ge(s, n)

            tt, ts, stt, cp = v.tensor_tensor, v.tensor_scalar, v.scalar_tensor_tensor, v.tensor_copy
            M, AD, SU, MX, MN = ALU.mult, ALU.add, ALU.subtract, ALU.max, ALU.min

            v.wait_ge(S["cols_ps"], 1)
            cp(VE[:, :], PS[:, 0, 0:NVEC])
            link(cp(STC[:, :], PS[:, 1, 0:160]))
            v.wait_ge(S["x_ps"], 1)
            cp(X[:, 0:4, 0:P], PS[:, 2, :].rearrange("p (k t) -> p k t", k=4))
            cp(X[:, 0:4, P:SEQ], PS[:, 4, :].rearrange("p (k t) -> p k t", k=4))
            cp(X[:, 0:4, SEQ:T], PS[:, 6, :].rearrange("p (k t) -> p k t", k=4)[:, :, 0:NS]).then_inc(S["ev_d"], 2)
            lam = vec["lru_lambda"]
            e_, z, y2, pl, t0 = (N0S[:, 4 * i:4 * i + 4] for i in range(5))
            hlb = vec["hgrn_lb"]
            mx2, d2 = N0S[:, 24:26], N0S[:, 40:44]
            link(stt(t0, lam, -1.0, lam, M, MX))
            sig(ts(e_, t0, -1.0, None, M), S["prep_e"], 1)
            link(tt(mx2, hlb[:, 0:2], hlb[:, 2:4], MX))
            tt(d2[:, 0:2], hlb[:, 0:2], mx2, SU)
            sig(tt(d2[:, 2:4], hlb[:, 2:4], mx2, SU), S["prep_s"], 1)
            v.wait_ge(S["prep_exp"], 2)
            link(ts(t0, e_, 2.0, None, AD))
            link(v.reciprocal(t0, t0))
            link(tt(z, e_, t0, M))
            link(tt(y2, z, z, M))
            link(ts(pl, y2, 1.0 / 19, 1.0 / 17, M, AD))
            for n in (15, 13, 11, 9, 7, 5, 3, 1):
                link(tt(pl, pl, y2, M))
                link(ts(pl, pl, 1.0 / n, None, AD))
            link(tt(pl, pl, z, M))
            link(ts(t0, lam, -1.0, 0.0, M, MX))
            link(stt(t0, pl, 2.0, t0, M, AD))
            link(ts(LC[:, 0:4], t0, -4.0, None, M))
            for name in ("lru_br", "lru_bi"):
                link(ts(vec[name], vec[name], 0.5, None, M))
            s2 = N0S[:, 26:28]
            link(tt(s2, d2[:, 0:2], d2[:, 2:4], AD))
            link(v.reciprocal(s2, s2))
            tt(d2[:, 0:2], d2[:, 0:2], s2, M)
            link(tt(d2[:, 2:4], d2[:, 2:4], s2, M))
            link(tt(d2[:, 2:4], d2[:, 0:2], d2[:, 2:4], AD))
            link(tt(d2[:, 2:4], d2[:, 2:4], d2[:, 0:2], SU))
            link(tt(d2[:, 0:2], d2[:, 0:2], d2[:, 0:2], SU))
            ts(LC[:, 4:8], d2, 1e-30, None, MX)
            link(ts(LC[:, 8:12], d2, -1.0, 1.0, M, AD))
            v.memset(SM[:, :], 0.0).then_inc(S["dve_chain"], 1)
            chain[0] += 1

            def layer_norm(q, l, src, g, b):
                v.wait_ge(S["ln_mean_ps"], q + 1)
                for h in range(2):
                    k = slice(4 * h, 4 * h + 4)
                    sig(tt(X[:, k], src[:, k], PS[:, 6, 0:T].unsqueeze(1).to_broadcast([P, 4, T]), SU),
                        S["ln_xc"], 2 * q + h + 1)
                v.wait_ge(S["ln_sd"], q + 1)
                link(v.reciprocal(RSTD, SDEV))
                rb4 = RSTD.unsqueeze(1).to_broadcast([P, 4, T])
                tt(X[:, 0:4], X[:, 0:4], rb4, M).then_inc(S["ln_xn"], 1)
                link(tt(X[:, 4:8], X[:, 4:8], rb4, M))
                for k in range(4, 8):
                    last = ts(X[:, k], X[:, k], vec[g][:, KT * l + k:KT * l + k + 1],
                              vec[b][:, KT * l + k:KT * l + k + 1], M, AD)
                last.then_inc(S["x_ready_d"], 1)

            def mix(l):
                done = l + 1
                if l:
                    v.wait_ge(S["orow_ps"], l)
                    v.wait_ge(S["states_stored"], 16 * STORES * l)
                xs = xpad[:, :, SC:WP].rearrange("p a (b s) -> p a b s", b=NB)
                v.memset(xpad[:, :, 0:3], 0.0)
                cp(xpad[:, :, 3:SC], proj[:, XA:XA + 2, 0:SEQ])
                cp(xs[:, :, :, 3:7], proj[:, XA:XA + 2, SEQ:T].rearrange("p a (b t) -> p a b t", b=NB))
                link(cp(xs[:, :, :, 0:3], STC[:, 48 * l:48 * l + 48].rearrange("p (b c w) -> p w b c", b=NB, c=3)))
                cw, cb, xc = vec["conv_w"], vec["conv_b"], A2["xc"]
                for j in range(4):
                    for p in range(2):
                        c = 8 * l + 2 * j + p
                        src = xpad[:, p, j:j + WC]
                        if j == 0:
                            last = ts(xc[:, p, 0:WC], src, cw[:, c:c + 1], cb[:, 2 * l + p:2 * l + p + 1], M, AD)
                        else:
                            last = stt(xc[:, p, 0:WC], src, cw[:, c:c + 1], xc[:, p, 0:WC], M, AD)
                    if j < 3:
                        link(last)
                last.then_inc(S["xc_ready"], 1)
                cp(OUTC[:, 0:6].rearrange("p (c w) -> p w c", c=3), xpad[:, :, SEQ:SEQ + 3])
                cp(OUTC[:, 6:54].rearrange("p (b c w) -> p w b c", b=NB, c=3), xs[:, :, :, 4:7])
                v.wait_ge(S["g_ps"], done)
                cp(gsb, PS[0:8, 6, 0:T]).then_inc(S["g_sb"], 1)
                v.wait_ge(S["gif_ps"], done)
                v.wait_ge(S["small_in"], 80)
                ts(rli, PS[0:NH, 7, 0:T], GB[:, 0, l:l + 1], None, AD)
                sig(ts(rlf, PS[0:NH, 6, 0:T], GB[:, 1, l:l + 1], None, AD), S["li_done"], done)
                stt(rtmp, rlf, -1.0, rlf, M, MX).then_inc(S["mz"], 1)
                v.wait_ge(S["swap_ps"], done)
                qk = proj[:, QC:QC + 4]
                tt(rotmp, PS[:, 0:4, 0:T], tb("sin").unsqueeze(1).to_broadcast([P, 4, T]), M)
                link(tt(qk, qk, tb("cos").unsqueeze(1).to_broadcast([P, 4, T]), M))
                sig(tt(qk, qk, rotmp, AD), S["rot_done"], done)
                link(tt(QH[:, 1], qk[:, 0:2, SEQ:T], tb("retinter"), M))
                v.wait_ge(S["m_ln"], done)
                link(stt(rlf, rlf, 0.0, rtmp, MN, SU))
                v.tensor_tensor_scan(rb, tb("keep256"), rlf, 0.0, M, AD)
                tt(rtmp, rlf, tb("negstart"), AD)
                link(tt(N0S[0:NH, 48:56], rlf[:, SEQ:T:DSEQ], M0[:, l, :], AD))
                link(cp(rlf, rli))
                link(tt(rlf[:, SEQ:T:DSEQ], rli[:, SEQ:T:DSEQ], N0S[0:NH, 48:56], MX))
                link(v.tensor_tensor_scan(rm, rtmp, rlf, 0.0, AD, MX))
                cp(M1[:, 0:1], rm[:, SEQ - 1:SEQ])
                cp(M1[:, 1:1 + NB], rm[:, SEQ + DSEQ - 1:T:DSEQ])
                tt(rli, rli, rb, SU)
                link(tt(rb, rb, rm, SU))
                m0b = M0[:, l, :].unsqueeze(2).to_broadcast([NH, NB, DSEQ])
                four = "p (b t) -> p b t"
                tt(risc.rearrange(four, b=NB), rb[:, SEQ:T].rearrange(four, b=NB), m0b, AD)
                ts(rtmp[:, 0:SEQ], rli[:, 0:SEQ], rb[:, SEQ - 1:SEQ], None, AD)
                aend = rb[:, SEQ + DSEQ - 1:T:DSEQ].unsqueeze(2).to_broadcast([NH, NB, DSEQ])
                tt(rtmp[:, SEQ:T].rearrange(four, b=NB), rli[:, SEQ:T].rearrange(four, b=NB), aend, AD
                   ).then_inc(S["m_rows"], 1)
                r, ig, a, hh, om = (A2[n][:, :, 0:WC] for n in ("r", "ig", "a", "h", "om"))
                ga = proj[:, GA:GA + 2]
                v.wait_ge(S["gl_sq"], done)
                c0 = 0.7978845608028654
                link(ts(C2[7], C2[7], 0.044715 * c0, c0, M, AD))
                tt(C2[7], C2[7], ga, M).then_inc(S["gl_in"], 1)
                v.wait_ge(S["lru_read"], done)
                for p in range(2):
                    c = LC[:, 2 * l + p:2 * l + p + 1]
                    last = ts(r[:, p], r[:, p], c, c, M, AD)
                last.then_inc(S["la_ready"], 1)
                link(ts(ig, ig, 0.5, 0.5, M, AD))
                link(tt(ig, ig, xc[:, :, 0:WC], M))
                v.wait_ge(S["a_exp"], done)
                link(tt(om, a, a, M))
                stt(om, om, 1.0, hh, AD, M).then_inc(S["om_ready"], 1)
                v.wait_ge(S["rs_ps"], done)
                rd = tb("retdecay")
                tt(WT[:, :, 0:SEQ + P], PS[:, 0:4, 0:SEQ + P], rd[:, :, 0:SEQ + P], M)
                tt(WT[0:NS, :, SEQ + P:WS], PS[0:NS, 0:4, SEQ + P:WS], rd[0:NS, :, SEQ + P:WS], M
                   ).then_inc(S["rw_done"], 1)
                v.wait_ge(S["rk_ps"], done)
                kw = tb("retkeyw")
                for t in range(3):
                    n = P if t < 2 else NS
                    last = tt(KTK[0:n, 1, t, :].rearrange("p (h d) -> p h d", h=NH),
                              PS[0:n, 6 + t // 2, (t % 2) * 256:(t % 2) * 256 + 256].rearrange("p (h d) -> p h d", h=NH),
                              kw[0:n, t].unsqueeze(2).to_broadcast([n, NH, HD]), M)
                last.then_inc(S["rk_done"], 1)
                v.wait_ge(S["a_sqrt"], done)
                link(tt(ig, ig, om, M))
                starts = slice(SC, WC, 3 + DSEQ)
                h0 = STC[:, 96 + 16 * l:112 + 16 * l].rearrange("p (b w) -> p w b", b=NB)
                tmp = N0S[:, 0:16].rearrange("p (w b) -> p w b", w=2)
                link(tt(tmp, a[:, :, starts], h0, M))
                link(tt(ig[:, :, starts], ig[:, :, starts], tmp, AD))
                link(v.memset(a[:, :, starts], 0.0))
                for p in range(2):
                    last = v.tensor_tensor_scan(hh[:, p], a[:, p], ig[:, p], 0.0, M, AD)
                link(last)
                cp(OUTC[:, 54:56], hh[:, :, SEQ - 1])
                cp(OUTC[:, 56:72].rearrange("p (b w) -> p w b", b=NB), hh[:, :, SC + DSEQ - 1:WC:3 + DSEQ])
                v.wait_ge(S["gl_tanh"], done)
                link(ts(C2[7], C2[7], 0.5, 0.5, M, AD))
                link(tt(C2[7], C2[7], ga, M))
                tt(mixed[:, 0:2, 0:SEQ], hh[:, :, 0:SEQ], C2[7][:, :, 0:SEQ], M)
                tt(mixed[:, 0:2, SEQ:T].rearrange("p a (b t) -> p a b t", b=NB),
                   A2["h"][:, :, SC:WP].rearrange("p a (b s) -> p a b s", b=NB)[:, :, :, 0:DSEQ],
                   C2[7][:, :, SEQ:T].rearrange("p a (b t) -> p a b t", b=NB), M).then_inc(S["a_done"], 1)
                v.wait_ge(S["ry_ps"], done)
                cp(Y[:, Y_RET:Y_RET + 2], PS[:, 4:6, 0:T]).then_inc(S["ry_done"], 1)
                v.wait_ge(S["rst_ps"], done)
                cp(PFIN[:, 1], PS[:, 6, 0:P].rearrange("p (a v) -> p a v", a=2))
                for p in range(2):
                    st = S0[:, 1, 512 * p:512 * p + 512]
                    last = stt(st, st, tb("retstate")[:, p:p + 1], PS[:, p, :], M, AD)
                last.then_inc(S["rst_done"], 1)
                v.wait_ge(S["mcol_ps"], done)
                cp(mcol[:, 0:2], PS[:, 7, 0:16].rearrange("p (t k h) -> p t k h", t=2, k=2))
                sig(cp(mcol[0:NS, 2], PS[0:NS, 7, 16:24].rearrange("p (k h) -> p k h", k=2)), S["mcol_done"], done)
                v.wait_ge(S["mb_done"], done)
                tt(QH[:, 0], proj[:, QB:QB + 2, SEQ:T], embc[:, :, T:T + NS], M).then_inc(S["mq_done"], 1)
                v.wait_ge(S["ms_ps"], done)
                stt(WT[:, :, 0:SEQ + P], PS[:, 0:4, 0:SEQ + P], HD ** -0.5, E[:, :, 0:SEQ + P], M, M)
                stt(WT[0:NS, :, SEQ + P:WS], PS[0:NS, 0:4, SEQ + P:WS], HD ** -0.5, E[0:NS, :, SEQ + P:WS], M, M
                    ).then_inc(S["mw_done"], 1)
                v.wait_ge(S["mk_ps"], done)
                for t in range(3):
                    n = P if t < 2 else NS
                    last = stt(KTK[0:n, 0, t, :].rearrange("p (h d) -> p h d", h=NH),
                               PS[0:n, 6 + t // 2, (t % 2) * 256:(t % 2) * 256 + 256].rearrange("p (h d) -> p h d", h=NH),
                               HD ** -0.5, mcol[0:n, t, 1].unsqueeze(2).to_broadcast([n, NH, HD]), M, M)
                last.then_inc(S["mk_done"], 1)
                v.wait_ge(S["my_ps"], done)
                ym = Y[:, Y_ML:Y_ML + 2]
                link(tt(ym, PS[:, 0:2, 0:T], embc[:, :, 0:T], MX))
                link(stt(ym, PS[:, 0:2, 0:T], -1.0, ym, M, MX))
                link(v.reciprocal(ym, ym))
                sig(tt(ym, ym, PS[:, 4:6, 0:T], M), S["my_done"], done)
                v.wait_ge(S["mst_ps"], done)
                cp(PFIN[:, 0], PS[:, 6, 0:P].rearrange("p (a v) -> p a v", a=2))
                cp(OUTC[:, 72:74], PS[:, 6, P:P + 2])
                cs = embc[:, :, T + DSEQ - 1:T + NS:DSEQ]
                n0 = STC[:, 128 + 16 * l:144 + 16 * l].rearrange("p (b w) -> p w b", b=NB)
                tt(tmp, n0, cs, M)
                for p in range(2):
                    last = tt(s0(0)[:, p], s0(0)[:, p], cs[:, p].unsqueeze(2).to_broadcast([P, NB, HD]), M)
                link(last)
                tt(OUTC[:, 74:90].rearrange("p (b w) -> p w b", b=NB), tmp,
                   PS[:, 6, P + 8:P + 24].rearrange("p (w b) -> p w b", w=2), AD).then_inc(S["outc_done"], 1)
                for p in range(2):
                    st = S0[:, 0, 512 * p:512 * p + 512]
                    last = tt(st, st, PS[:, 2 + p, :], AD)
                last.then_inc(S["mst_done"], 1)
                k_, q_, b_ = C2[4], C2[5], C2[6]
                ts(k_, proj[:, FD:FD + 2], -1.0, 80.0, M, MN).then_inc(S["hf_ready"], 1)
                v.memset(scr[:, 0:2560], 0.0)
                link(v.memset(MB[:, 6912:8576], 0.0))
                v.wait_ge(S["hf_exp"], done)
                link(ts(q_, k_, 1.0, None, AD))
                link(v.reciprocal(q_, q_))
                for p in range(2):
                    c = 2 * l + p
                    link(stt(k_[:, p], k_[:, p], LC[:, 8 + c:9 + c], q_[:, p], M, M))
                    last = ts(q_[:, p], q_[:, p], LC[:, 8 + c:9 + c], LC[:, 4 + c:5 + c], M, AD)
                link(last)
                ts(C2[7], q_, TINY, None, MX)
                ts(C2[8], q_, TINY, 1.0 / TINY, MN, M).then_inc(S["hg_ready"], 1)
                v.wait_ge(S["hq_tanh"], done)
                link(ts(q_, q_, 0.5, 0.5, M, AD))
                link(tt(q_, q_, proj[:, QD:QD + 2], M))
                v.wait_ge(S["hg_ln"], done)
                link(tt(C2[7], C2[7], C2[8], AD))
                for p in range(2):
                    last = v.tensor_tensor_scan(b_[:, p], tb("keep128"), C2[7][:, p], 0.0, M, AD)
                link(last)

                def boundary(e):
                    s = LEVELS[e]
                    w = SEQ if s >= DSEQ else T
                    bv = b_[:, :, 0:w].rearrange("p a (n s) -> p a n s", s=2 * s)
                    xv = C2[7 + e % 2][:, :, 0:w].rearrange("p a (n s) -> p a n s", s=2 * s)
                    ref = bv[:, :, :, s - 1:s].to_broadcast([P, 2, w // (2 * s), 2 * s])
                    tt(xv, bv, ref, SU).then_inc(S["hx"], 1)

                def merge(e):
                    lo = 2 * (e % 2)
                    v.wait_ge(S["hl_ps"], NL * l + e + 1)
                    if l or e:
                        v.wait_ge(S["hl_done"], NL * l + e)
                    mask = tb("levels")[:, e].bitcast(U32)
                    for odd in range(2):
                        last = v.copy_predicated(AT[:, :, odd:NH:2, :],
                                                 mask.unsqueeze(1).unsqueeze(1).to_broadcast([P, 2, 2, P]),
                                                 PS[:, lo + odd, :].rearrange("p (c a i) -> p c a i", c=2, a=2))
                        if e >= NL - 3:
                            last = v.copy_predicated(
                                ATs[:, odd:NH:2], mask[0:NS, 0:NS].unsqueeze(1).to_broadcast([NS, 2, NS]),
                                PS[0:NS, 4 + lo + odd, 0:2 * NS].rearrange("p (a i) -> p a i", a=2))
                    last.then_inc(S["hl_done"], 1)

                boundary(0)
                for e, s in enumerate(LEVELS):
                    if e + 1 < len(LEVELS):
                        boundary(e + 1)
                    v.wait_ge(S["hz"], len(LEVELS) * l + e + 1)
                    lo = 2 * (e % 2)
                    x, q, k, qo, ko = (level_view(z, s) for z in (C2[7 + e % 2], q_, k_, C2[lo], C2[lo + 1]))
                    tt(qo[1], q[1], x[1], M)
                    tt(ko[0], k[0], x[0], M).then_inc(S["hl_ready"], 1)
                    v.wait_ge(S["hl_ready"], (NL - 1) * l + e + 1)
                    if e:
                        merge(e - 1)
                for w, n, s in ((slice(0, SEQ), 2, P), (slice(SEQ, T), NB, DSEQ)):
                    bv = b_[:, :, w].rearrange("p a (n s) -> p a n s", s=s)
                    xv = C2[8][:, :, w].rearrange("p a (n s) -> p a n s", s=s)
                    last = tt(xv, bv[:, :, :, s - 1:s].to_broadcast([P, 2, n, s]), bv, SU)
                last.then_inc(S["hi_ready"], 1)
                merge(NL - 2)
                merge(NL - 1)
                v.wait_ge(S["hi_exp"], done)
                tt(C2[7], C2[7], q_, M)
                tt(C2[8], C2[8], k_, M).then_inc(S["hk_ready"], 1)
                v.wait_ge(S["hk_ps"], done)
                cp(KTK[:, 0, 0:2, :], PS[:, 6, :].rearrange("p (t c) -> p t c", t=2))
                cp(KTK[0:NS, 0, 2, :], PS[0:NS, 7, 0:256]).then_inc(S["hk_done"], 1)
                v.wait_ge(S["hc_ps"], 2 * l + 1)
                sig(cp(SC0[:, :, :], PS[:, 6, 0:P].rearrange("p (a v) -> p a v", a=2)), S["hc_done"], done)
                v.wait_ge(S["hc_ps"], 2 * l + 2)
                for p in range(2):
                    stt(PFIN[:, 2, p], SC0[:, p], GE[:, p, 0:1], PS[:, 7, HD * p:HD * p + HD], M, AD)
                v.wait_ge(S["hy_ps"], done)
                cp(Y[:, Y_HG:Y_HG + 2], PS[:, 4:6, 0:T])
                for p in range(2):
                    last = tt(s0(2)[:, p], s0(2)[:, p], GE[:, p, 1:1 + NB].unsqueeze(2).to_broadcast([P, NB, HD]), M)
                link(last)
                v.wait_ge(S["hst_ps"], done)
                for p in range(2):
                    st = S0[:, 2, 512 * p:512 * p + 512]
                    last = tt(st, st, PS[:, 2 + p, :], AD)
                last.then_inc(S["hst_done"], 1)
                v.wait_ge(S["th_done"], done)
                link(ts(TH, TH, 0.5, 0.5, M, AD))
                tt(TH[:, 2:4], TH[:, 2:4], proj[:, GC:GC + 2], M)
                tt(TH[:, 4:6], TH[:, 4:6], proj[:, GD:GD + 2], M)
                v.wait_ge(S["mean_ps"], done)
                tt(Y[:, 0:2], Y[:, 0:2], PS[:, 0:2, 0:T], SU)
                sig(tt(Y[:, 2:4], Y[:, 2:4], PS[:, 6:8, 0:T], SU), S["centered"], done)
                v.wait_ge(S["sd6_done"], done)
                link(v.reciprocal(SD6, SD6))
                for i, g in enumerate(("ret_norm_g", "mlstm_norm_g", "hgrn_norm_g")):
                    for p in range(2):
                        y = Y[:, 2 * i + p]
                        last = stt(y, y, vec[g][:, 2 * l + p:2 * l + p + 1], SD6[:, 2 * i + p], M, M)
                link(last)
                tt(mixed[:, 2:4], Y[:, Y_ML:Y_ML + 2], TH[:, 0:2], M)
                tt(mixed[:, 4:6], Y[:, Y_RET:Y_RET + 2], TH[:, 2:4], M)
                tt(mixed[:, 6:8], Y[:, Y_HG:Y_HG + 2], TH[:, 4:6], M).then_inc(S["mixed_ready"], 1)

            for l in range(DEPTH):
                with v.Fori(0, 7) as i:
                    for h in range(2):
                        v.wait_ge(S["ps"], i * 2 + (U_IN[l] + h + 1))
                        cp(proj[:, bass.ds(i * 4 + (2 * h + 1), 1), :], PS[:, 2 * h + 1:2 * h + 2, 0:T]
                           ).then_inc(S["ev_d"], 1)
                v.wait_ge(S["ev_d"], D_IN[l] + 14)
                v.wait_ge(S["ev_a"], A_IN[l] + 14)
                mix(l)
                for u in range(4):
                    v.wait_ge(S["ps"], U_OUT[l] + u + 1)
                    x2 = X[:, 2 * u:2 * u + 2]
                    stt(x2, x2, ALPHA, PS[:, 2 * (u % 2):2 * (u % 2) + 2, 0:T], M, AD).then_inc(S["ev_d"], 1)
                v.wait_ge(S["ev_d"], D_OUT[l] + 4)
                layer_norm(2 * l, l, X, "ln_mix_g", "ln_mix_b")
                if l == 0:
                    def up(n, t0, h):
                        v.wait_ge(S["sl"], n + 1)
                        tt(hid[:, t0, :], sil[:, 2 * h:2 * h + 2], PS[:, 4 * h + 2:4 * h + 4, 0:T], M).then_inc(S["ev_d"], 1)
                    with v.Fori(0, 5) as i:
                        for h in range(2):
                            up(i * 2 + h, bass.ds(i * 4 + 2 * h, 2), h)
                    up(10, slice(20, 22), 0)
                    v.wait_ge(S["x_ready_a"], 1)
                    v.wait_ge(S["x_ready_d"], 1)
                    for m in range(4):
                        v.wait_ge(S["ps"], U_DOWN + m + 1)
                        x2 = X[:, 2 * m:2 * m + 2]
                        stt(x2, x2, ALPHA, PS[:, 2 * (m % 2):2 * (m % 2) + 2, 0:T], M, AD).then_inc(S["ev_d"], 1)
                    v.wait_ge(S["ev_d"], D_DOWN + 4)
                    layer_norm(1, 0, X, "ln_ffn_g", "ln_ffn_b")
            v.wait_ge(S["x_ready_a"], 3)
            v.wait_ge(S["x_ready_d"], 3)
            link(v.memset(SM[:, 0:192], 0.0))
            v.wait_ge(S["logits_ps"], 1)
            tt(LG[:, 0:2], PS[:, 0, 0:16].rearrange("p (t e) -> p t e", t=2),
               RB[:, :].unsqueeze(1).to_broadcast([P, 2, NE]), AD)
            link(tt(LG[0:NS, 2], PS[0:NS, 0, 16:24], RB[0:NS, :], AD))

            def bc(x):
                return x.unsqueeze(2).to_broadcast([P, 3, NE])

            def red(o, i, op):
                link(v.tensor_reduce(o, i, AX_X, op))
            iota = tb("iota8").unsqueeze(1).to_broadcast([P, 3, NE])
            red(T3[0], LG, MX)
            sig(tt(LG, LG, bc(T3[0]), SU), S["lg_ready"], 1)
            v.wait_ge(S["pr_exp"], 1)
            red(T3[1], PR, AD)
            link(v.reciprocal(T3[1], T3[1]))
            link(tt(PR, PR, bc(T3[1]), M))
            link(cp(PX, PR))
            for n in range(2):
                red(T3[2], PX, MX)
                link(tt(EQ, PX, bc(T3[2]), ALU.is_equal))
                link(stt(EQ, EQ, -8.0, tb("iota8").unsqueeze(1).to_broadcast([P, 3, NE]), M, AD))
                red(T3[3], EQ, MN)
                link(tt(EQ, EQ, bc(T3[3]), ALU.is_equal))
                link(tt(SEL, SEL, EQ, AD))
                link(stt(PX, EQ, -2.0, PX, M, AD))
            link(tt(PR, PR, SEL, M))
            red(T3[4], PR, AD)
            link(v.reciprocal(T3[4], T3[4]))
            tt(GTOK, PR, bc(T3[4]), M).then_inc(S["gates_done"], 1)
            v.wait_ge(S["gt_ps"], 1)
            cp(GROW, PS[0:NE, 1, 0:T])
            link(cp(SROW, PS[0:NE, 0, 0:T]))
            link(v.tensor_tensor_scan(PROW, SROW, SROW, 0.0, AD, MX))
            link(cp(CNT, PROW[:, T - 1:T]))
            link(tt(PROW, PROW, SROW, M))
            sig(ts(PROW, PROW, 1.0, None, SU), S["slots_done"], 1)
            v.wait_ge(S["pt_ps"], 1)
            cp(PTK[:, 0:2], PS[:, 2, 0:16].rearrange("p (t e) -> p t e", t=2))
            cp(PTK[0:NS, 2], PS[0:NS, 2, 16:24])
            link(v.tensor_reduce(T3[5][0:1, 0:1], PS[0:1, 3, 0:NE], AX_X, MX))
            sig(ts(FLAG[:, :], T3[5][0:1, 0:1], float(CAP), None, ALU.is_gt), S["flag_ready"], 1)
            v.wait_ge(S["gbc_done"], 1)
            dense = v.value_load(FLAG[0:1, 0:1], min_val=0, max_val=1)

            def choose(n, dyn):
                tt(SELT, tb("iotacap").unsqueeze(1).to_broadcast([P, 3, CAP]),
                   PTK[:, :, dyn].to_broadcast([P, 3, CAP]), ALU.is_equal).then_inc(S["sel_ready"], 1)

            def gathered_expert(e, final):
                if not final:
                    v.wait_ge(S["ga_ps"], e + 1)
                    choose(e + 1, bass.ds(e + 1, 1))
                for ft in range(FT_E):
                    v.wait_ge(S["moe_s"], e * FT_E + (ft + 1))
                    tt(hid_g[:, ft], sil_g[:, ft % 2], PS[:, ft % 2, CAP:2 * CAP], M).then_inc(S["moe_h"], 1)
                for k in range(KT):
                    v.wait_ge(S["sc_ps"], e * KT + (k + 1))
                    tt(X[:, k], X[:, k], PS[:, 4 + k % 2, 0:T], AD).then_inc(S["sc_ev"], 1)

            with v.If(dense):
                ts(YE, X, ALPHA, None, M).then_inc(S["ye_ready"], 1)
                v.wait_ge(S["ye_ready"], 1)
                with v.Fori(0, NE) as e:
                    for ft in range(FT_E):
                        h = ft % 2
                        v.wait_ge(S["moe_s"], e * FT_E + (ft + 1))
                        tt(sil_e[:, h], sil_e[:, h], PS[:, 2 * h + 1, 0:T], M).then_inc(S["moe_g"], 1)
                        v.wait_ge(S["moe_g"], e * FT_E + (ft + 1))
                        tt(hid_e[:, ft], sil_e[:, h], GBC[:, bass.ds(e, 1), :].rearrange("p e t -> p (e t)"), M
                           ).then_inc(S["moe_h"], 1)
                    for m in range(KT):
                        v.wait_ge(S["dn_ps"], e * KT + (m + 1))
                        tt(YE[:, m], YE[:, m], PS[:, 4 + m % 2, 0:T], AD).then_inc(S["moe_y"], 1)
                v.wait_ge(S["moe_y"], NE * KT)
                cp(X, YE).then_inc(S["moe_sum"], 1)
            with v.Else():
                ts(X, X, ALPHA, None, M).then_inc(S["ye_ready"], 1)
                choose(0, slice(0, 1))
                for e in range(NE):
                    v.wait_ge(S["pb_ps"], e + 1)
                    last = stt(SG[:, e], PS[0:CAP, e, 0:T], tb("iotarow")[0:CAP], GBC[0:CAP, e], ALU.is_equal, M)
                last.then_inc(S["sg_done"], 1)
                v.wait_ge(S["ye_ready"], 1)
                with v.Fori(0, NE - 1) as e:
                    gathered_expert(e, False)
                gathered_expert(NE - 1, True)
                v.wait_ge(S["sc_ev"], NE * KT)
                v.sem_inc(S["moe_sum"], 1)
            v.wait_ge(S["moe_sum"], 1)
            layer_norm(3, 1, X, "ln_ffn_g", "ln_ffn_b")
            v.wait_ge(S["y_ps"], 1)
            for t in range(3):
                n = P if t < 2 else NS
                last = cp(xtok[0:n, t, 512:1024], PS[0:n, 2 * t + 1, :])
            last.then_inc(S["y_rows_d"], 1)


_INS = ["x_prompt", "x_sample", "state_rglru_h", "state_rglru_conv", "state_mlstm_C", "state_mlstm_n",
        "state_mlstm_m", "state_ret_S", "state_hgrn_S", "w_in", "w_out", "ln_mix_g", "ln_mix_b", "ln_ffn_g",
        "ln_ffn_b", "conv_w", "conv_b", "lru_wr", "lru_br", "lru_wi", "lru_bi", "lru_lambda", "mlstm_bi",
        "mlstm_bf", "mlstm_norm_g", "ret_norm_g", "hgrn_lb", "hgrn_norm_g", "ffn_w1", "ffn_w3", "ffn_w2",
        "moe_router", "moe_router_b", "moe_w1", "moe_w3", "moe_w2"]


def _outs():
    outs = [("y_prompt", (1, SEQ, D)), ("y_sample", (NB, DSEQ, D))]
    for who, b in (("prompt", 1), ("sample", NB)):
        outs += [(f"{who}_rglru_h", (DEPTH, b, GW)), (f"{who}_rglru_conv", (DEPTH, b, 3, GW)),
                 (f"{who}_mlstm_C", (DEPTH, b, NH, HD, HD)), (f"{who}_mlstm_n", (DEPTH, b, NH, HD)),
                 (f"{who}_mlstm_m", (DEPTH, b, NH)), (f"{who}_ret_S", (DEPTH, b, NH, HD, HD)),
                 (f"{who}_hgrn_S", (DEPTH, b, NH, HD, HD))]
    return outs


def kernel(**inputs):
    import concourse.bacc as _bacc
    from concourse.bass_utils import run_bass_kernel_spmd as _run

    nc = _bacc.Bacc("TRN2", target_bir_lowering=False, num_devices=1)
    arrays, args = {}, {}
    for name in _INS:
        a = np.ascontiguousarray(inputs[name])
        arrays[f"in_{name}"] = a
        args[name] = nc.dram_tensor(f"in_{name}", a.shape, mybir.dt.from_np(a.dtype), kind="ExternalInput").ap()
    tables, where = shape_tables()
    arrays["in_shape_tables"] = tables
    tab = nc.dram_tensor("in_shape_tables", tables.shape, F32, kind="ExternalInput").ap()
    out = {n: nc.dram_tensor(f"out_{n}", s, F32, kind="ExternalOutput").ap() for n, s in _outs()}
    decoder_kernel(nc, args, out, tab, where)
    r = _run(nc, [arrays], core_ids=[0])
    return tuple(r.results[0][f"out_{n}"] for n, _ in _outs())
```

```python
from contextlib import ExitStack

import numpy as np

import concourse.bass as bass
from concourse import mybir

F32 = mybir.dt.float32
U32 = mybir.dt.uint32
ALU = mybir.AluOpType
ACT = mybir.ActivationFunctionType
AX_X = mybir.AxisListType.X

P = 128
D, KT = 1024, 8
SEQ, NB, DSEQ = 256, 8, 4
NS = NB * DSEQ
T = SEQ + NS
DEPTH, GW, NH, HD = 2, 256, 4, 64
PAST = 2048
D_FF, NE, D_FE = 2816, 8, 1408
FT_E = D_FE // P
GATE_COL = 2 * GW + 4 * GW
NPT = 28
XA, GA, QB, KB, VB, OB, QC, KC, VC, GC, QD, FD, ID, GD = range(0, NPT, 2)
ALPHA = (2.0 * DEPTH) ** 0.25
LN_EPS, HEAD_EPS = 1e-5, 1e-6
TINY = 2.0 ** -60
WP = 3 + SEQ + NB * (3 + DSEQ)
WC = WP - 3
SC = 3 + SEQ
WS = SEQ + P + NS
LEVELS = (64, 32, 16, 8, 4, 2, 1)
NEG = -1e30

U_IN, U_OUT = (0, 33), (14, 47)
U_UP, U_DOWN, U_MOE = 18, 29, 51
CAP = 96
UP_SLOTS = ((6, 7), (0, 1))
DOWN_SLOTS = ((2, 3, 4), (8, 9, 10))
E_SLOTS = (0, 1, 6, 7, 8, 9, 10, 2, 3, 4, 5)
LOADS_MOE = (19, 19, 4, 4, 4, 2, 6, 6, 2, 2, 2) + (0,) * 6
LOADS_L1 = (12, 12, 3, 3, 3, 1, 6, 6, 2, 2, 2)
A_IN = (2, 16)
D_OUT = (2, 21)
D_UP, D_DOWN = 6, 17
N_INPUTS = 13 + 3 + 3
STORES = 3 * 3 + 2 + 6

VEC = {}
for _name, _rows in (("ln_mix_g", 16), ("ln_mix_b", 16), ("ln_ffn_g", 16), ("ln_ffn_b", 16), ("conv_w", 16),
                     ("conv_b", 4), ("lru_br", 4), ("lru_bi", 4), ("lru_lambda", 4), ("mlstm_norm_g", 4),
                     ("ret_norm_g", 4), ("hgrn_norm_g", 4), ("hgrn_lb", 4)):
    VEC[_name] = (sum(r for _, r in VEC.values()), _rows)
NVEC = sum(r for _, r in VEC.values())


SEMAPHORES = """
tables_in inputs_in g_ps gate_weights_in ps mixed_ready moe_up x_ready w2_used y_rows_a y_rows_d
y_stored small_in lru_zeroed lru_ps lru_in states_stored s0_in v_tok a_done rot_done rst_ps mst_ps
vm_ready rst_done mst_done hst_done orow_done cols_ps x_ps ln_mean_ps ln_sq ln_var_ps ev_a me_done
v_ps rs_ps rk_ps rw_done ry_ps rk_done ry_done ms_ps mk_ps mw_done mq_done mk_done hl_ready hl_done
hl_ps my_ps my_done hk_ready hk_ps hk_done hc_ps hc_done hy_ps hst_ps mean_ps outc_done centered
orow_ps sq6_done var_ps rrow_done rb_ps ev_d g_sb gif_ps xc_ready li_done mrow_done lru_read mcol_ps
mb_ps mb_done mcol_done swap_ps ma_ps mixed_part logits_ps xtk_ps gates_done gt_ps slots_done
xtk_done pt_ps flag_ready gbc_ps sel_ready ga_ps xe_done moe_h dn_ps yt_done sc_ev sc_ps gbc_done
moe_y pb_ps sg_done moe_sum y_ps prep_e prep_exp prep_s ln_xc ln_sd ln_xn gl_sq mz act_chain m_ln
gl_in gl_tanh m_rows la_ready a_exp om_ready a_sqrt hf_ready hf_exp hg_ready hq_tanh hg_ln hx hz
th_done hi_ready hi_exp sd6_done sl lg_ready pr_exp moe_s dve_chain ye_ready moe_g
""".split()


def shape_tables():
    parts, where, at = [], {}, 0

    def put(name, a):
        nonlocal at
        a = np.asarray(a, np.float32)
        full = np.zeros((P,) + a.shape[1:], np.float32)
        full[:a.shape[0]] = a
        flat = full.reshape(P, -1)
        where[name] = (at, a.shape[0], a.shape[1:])
        parts.append(flat)
        at += flat.shape[1]

    r = np.arange(P)
    put("ident", np.eye(P))
    put("iota8", np.ones((P, 1)) * np.arange(NE)[None])
    put("iotacap", np.ones((P, 1)) * np.arange(CAP)[None])
    put("iotarow", r[:, None])
    put("ones", np.ones((P, P)))
    put("lnmean", np.full((P, P), 1.0 / D))
    put("headmean", (r[:, None] // HD == r[None] // HD) / HD)
    hs = np.zeros((P, 6, 12))
    for i in range(6):
        hs[r, i, 2 * i + r // HD] = 1.0 / HD
    put("headrows", hs)
    half = HD // 2
    put("swap", r[:, None] == (r[None] // HD) * HD + (r[None] % HD + half) % HD)
    pos = np.concatenate([np.arange(SEQ), PAST + np.tile(np.arange(DSEQ), NB)]).astype(np.float32)
    inv = (np.float32(10000.0) ** (-np.arange(half, dtype=np.float32) / np.float32(half))).astype(np.float32)
    ang = (pos[None, :] * inv[:, None]).astype(np.float32)
    rows = r % HD % half
    put("cos", np.cos(ang.astype(np.float64))[rows])
    put("sin", np.sin(ang.astype(np.float64))[rows] * np.where(r % HD < half, -1.0, 1.0)[:, None])
    j = r[:, None]
    i_seq = np.arange(SEQ)[None]
    s_i = np.arange(NS)[None]
    sample_ok = (j < NS) & (j // DSEQ == s_i // DSEQ) & (j <= s_i)
    dist = np.concatenate([i_seq - j, np.arange(P)[None] - j, np.where(sample_ok, s_i - j, -1)], 1)
    put("causal", np.where(dist >= 0, 0.0, NEG))
    lg = np.log1p(-(2.0 ** (-5.0 - np.arange(NH))))
    decay = np.exp(lg[None, :, None] * np.maximum(dist, 0)[:, None, :]) * (dist >= 0)[:, None, :]
    put("retdecay", decay * HD ** -0.5)
    w = np.zeros((P, 3, NH))
    w[:, 0] = np.exp(lg[None] * (SEQ - 1 - j))
    w[:, 1] = np.exp(lg[None] * (P - 1 - j))
    w[:, 2] = np.exp(lg[None] * (DSEQ - 1 - j % DSEQ))
    put("retkeyw", w * HD ** -0.5)
    head_of = np.stack([r // HD, 2 + r // HD], 1)
    put("retinter", np.exp(lg[head_of][:, :, None] * (1 + np.arange(NS) % DSEQ)))
    put("retstate", np.exp(lg[head_of] * DSEQ))
    put("selpair", np.arange(NH)[:, None, None] == head_of.T[None])
    put("batchmask", (np.arange(NS)[:, None] // DSEQ == np.arange(NB)[None]))
    lv = []
    for s in LEVELS:
        same = j // (2 * s) == r[None] // (2 * s)
        lv.append(same & (j % (2 * s) < s) & (r[None] % (2 * s) >= s))
    lv.append(j == r[None])
    put("levels", np.stack(lv, 1))
    t = np.arange(T)
    start4 = (t >= SEQ) & ((t - SEQ) % DSEQ == 0)
    put("keep128", np.ones((P, 1)) * (1.0 - (start4 | (t == 0) | (t == P)))[None])
    put("keep256", np.ones((NH, 1)) * (1.0 - (start4 | (t == 0)))[None])
    put("negstart", np.ones((NH, 1)) * np.where(start4, NEG, 0.0)[None])

    return np.ascontiguousarray(np.concatenate(parts, 1)), where



def decoder_kernel(nc, A, out, tab, where):
    with ExitStack() as ctx:
        def sb(name, shape):
            return ctx.enter_context(nc.sbuf_tensor(name, shape, F32))

        S = {n: ctx.enter_context(nc.semaphore(n)) for n in SEMAPHORES}
        full = [ctx.enter_context(nc.semaphore(f"slot_full_{i}")) for i in range(17)]

        UP = sb("up_slots", [P, 11, 2048])
        OV = sb("overlay", [P, 11264])
        TB = sb("tables", [P, tab.shape[1]])
        X = sb("x", [P, KT, T])[:, :, :]
        VE = sb("vectors", [P, NVEC])
        STC = sb("state_cols", [P, 160])
        OUTC = sb("out_cols", [P, 96])
        MB = sb("mix_or_moe", [P, 8576])
        WG = sb("gate_weights", [P, KT, 8])
        LW = sb("lru_weights", [P, 2, 2, P])
        GB = sb("mlstm_gate_bias", [NH, 2, DEPTH])
        M0 = sb("mlstm_m", [NH, DEPTH, NB])
        M1 = sb("mlstm_m_new", [NH, 1 + NB])
        SM = sb("small", [P, 600])
        LC = sb("layer_consts", [P, 16])
        RW = sb("router", [P, KT, NE])
        RB = sb("router_bias", [P, NE])
        PS = ctx.enter_context(nc.psum_tensor("ps", [P, 8, 512], F32))

        def tb(name):
            at, rows, shape = where[name]
            n = int(np.prod(shape))
            a = TB[0:rows, at:at + n]
            if len(shape) == 2:
                a = a.rearrange("p (a b) -> p a b", a=shape[0])
            return a

        def cut(buf, at, *shape):
            a = buf[:, at:at + int(np.prod(shape))]
            if len(shape) == 2:
                a = a.rearrange("p (a b) -> p a b", a=shape[0])
            if len(shape) == 3:
                a = a.rearrange("p (a b c) -> p a b c", a=shape[0], b=shape[1])
            if len(shape) == 4:
                a = a.rearrange("p (a b c d) -> p a b c d", a=shape[0], b=shape[1], c=shape[2])
            return a

        ident = tb("ident")
        onesc = tb("ones")
        proj = cut(OV, 0, NPT, T)
        mixed = cut(OV, NPT * T, KT, T)
        ROWS = OV[0:NH, (NPT + KT) * T:11264]
        hid = cut(OV, 0, 22, T)
        sil = cut(OV, 22 * T, 4, T)
        SQ = cut(OV, 0, KT, T)
        RSTD = cut(OV, KT * T, 1, T)[:, 0]
        SDEV = cut(OV, KT * T + T, 1, T)[:, 0]
        W2 = cut(OV, 0, 11, 1024)
        xtok = cut(OV, 0, 3, D)
        vrows = OV[:, 3 * D:3 * D + P]
        srows = OV[:, 3 * D + P:3 * D + 2 * P]
        nrows = OV[:, 3 * D + 2 * P:3 * D + 3 * P]
        scr = UP[:, 8:11, :].rearrange("p a b -> p (a b)")
        R = [scr[:, 640 * i:640 * i + 640] for i in range(9)]
        VT = cut(MB, 0, 3, 6 * P)
        KTK = cut(MB, 2304, 2, 3, 2 * P)
        S0 = cut(MB, 3840, 3, 2 * NB * HD)
        WT = cut(MB, 6912, NH, WS)
        hid_e = cut(MB, 0, FT_E, T)
        sil_e = cut(MB, 3168, 2, T)
        YE = cut(MB, 3744, KT, T)
        GBC = cut(MB, 6048, NE, T)
        XTK = cut(MB, 0, 3, D)
        XE = cut(MB, 3072, KT, CAP)
        SELT = cut(MB, 3840, 3, CAP)
        sil_g = cut(MB, 4128, 2, CAP)
        free_tb = where["headmean"][0]
        SG = cut(TB, free_tb, NE, T)[0:CAP]
        hid_g = cut(TB, free_tb + NE * T, FT_E, CAP)
        YTK = TB[0:CAP, free_tb + NE * T + FT_E * CAP:free_tb + NE * T + FT_E * CAP + D]
        vec = {name: VE[:, at:at + n] for name, (at, n) in VEC.items()}

        def slot(s):
            return UP[:, s, :].rearrange("p (k n) -> p k n", k=8)

        w_in = A["w_in"].rearrange("l (k p) c -> l p k c", p=P)
        w_out = A["w_out"].rearrange("l (k p) c -> l p k c", p=P)
        f_w1 = A["ffn_w1"].rearrange("l (k p) c -> l p k c", p=P)
        f_w3 = A["ffn_w3"].rearrange("l (k p) c -> l p k c", p=P)
        f_w2 = A["ffn_w2"].rearrange("l (k p) c -> l p k c", p=P)
        m_w1 = A["moe_w1"].rearrange("l e (k p) c -> (l e) p k c", p=P)
        m_w3 = A["moe_w3"].rearrange("l e (k p) c -> (l e) p k c", p=P)
        m_w2 = A["moe_w2"].rearrange("l e (k p) c -> (l e) p k c", p=P)

        PFIN = sb("prompt_states", [P, 3, 2, HD])
        OROW = sb("out_rows", [96, P])
        QH = sb("sample_queries", [P, 2, 2, NS])
        GE = sb("end_decay", [P, 2, 1 + NB])
        SC0 = sb("chunk_state", [P, 2, HD])
        N0S = sb("tmp_small", [P, 64])
        rli, rlf, rtmp = ROWS[:, 0:T], ROWS[:, T:2 * T], ROWS[:, 2 * T:3 * T]
        risc = ROWS[:, 3 * T:3 * T + NS]
        rb, rm = SM[0:NH, 0:T], SM[0:NH, T:2 * T]
        gsb = SM[0:8, 0:T]
        mcol = SM[:, 2 * T:2 * T + 24].rearrange("p (t k h) -> p t k h", t=3, k=2)
        A2 = {n: R[i][:, 0:2 * WP].rearrange("p (a w) -> p a w", a=2)
              for n, i in (("xc", 1), ("r", 2), ("ig", 3), ("a", 4), ("h", 5), ("om", 6))}
        xpad = R[0][:, 0:2 * WP].rearrange("p (a w) -> p a w", a=2)
        C2 = [R[i][:, 0:2 * T].rearrange("p (a t) -> p a t", a=2) for i in range(9)]
        rotmp = MB[:, 6912:6912 + 4 * T].rearrange("p (a t) -> p a t", a=4)
        Vm = scr[0:NS, 0:4 * NB * HD].rearrange("p (h b v) -> p h b v", h=NH, b=NB)
        E = scr[:, 3840:3840 + NH * WS].rearrange("p (h w) -> p h w", h=NH)
        embc = R[4][:, 0:640].rearrange("p (a w) -> p a w", a=2)
        k_hg, q_hg, lg_hg, b_hg = proj[:, FD:FD + 2], mixed[:, 6:8], proj[:, GA:GA + 2], proj[:, XA:XA + 2]
        TH = scr[:, 2560:2560 + 6 * T].rearrange("p (a t) -> p a t", a=6)
        ATALL = mixed[:, 2:6].rearrange("p k t -> p (k t)")
        AT = ATALL[:, 0:2 * NH * P].rearrange("p (c h i) -> p c h i", c=2, h=NH)
        ATs = ATALL[0:NS, 2 * NH * P:2 * NH * P + NH * NS].rearrange("p (h i) -> p h i", h=NH)
        LVL = [proj[:, tile:tile + 2] for tile in (VB, ID, GA, QD)]
        VROW, RROW = SM[0:12, 0:T], SM[0:12, T:2 * T]
        Y = proj[:, QC:QC + 6]
        Y_RET, Y_ML, Y_HG = 0, 2, 4
        SQ6 = proj[:, QB:QB + 6]
        SD6 = proj[:, QD:QD + 6]
        NL = len(LEVELS) + 1
        LG, PR, EQ, TM, SEL, PX = (SM[:, 24 * i:24 * i + 24].rearrange("p (t e) -> p t e", t=3) for i in range(6))
        T3 = [SM[:, 144 + 3 * i:147 + 3 * i] for i in range(6)]
        GTOK = SM[:, 168:192].rearrange("p (t e) -> p t e", t=3)
        CNT = SM[0:NE, 162:163]
        FLAG = ctx.enter_context(nc.sbuf_tensor("dense_flag", [1, 1], mybir.dt.int32))
        GROW = SM[0:NE, 200:200 + T]
        free_tb += NE * T + FT_E * CAP + D
        SROW = TB[0:NE, free_tb:free_tb + T]
        PROW = TB[0:NE, free_tb + T:free_tb + 2 * T]
        PTK = SM[:, 500:524].rearrange("p (t e) -> p t e", t=3)
        block = ctx.enter_context(nc.Block())

        def level_view(x, s):
            w = SEQ if s >= DSEQ else T
            b = x[:, :, 0:w].rearrange("p a (n h s) -> p a n h s", h=2, s=s)
            return b[:, :, :, 0], b[:, :, :, 1]

        def right(x, e):
            return x.rearrange("p (n h s) -> p n h s", h=2, s=LEVELS[e])[:, :, 1]

        def right_only(x, e):
            return x.rearrange("p (n s) -> p n s", s=LEVELS[e])

        def state_view(ap, l, b0, nb):
            return ap[l, b0:b0 + nb].rearrange("b (p h) d v -> (h d) p b v", h=2)

        def s0(kind):
            return S0[:, kind].rearrange("p (a b v) -> p a b v", a=2, b=NB)

        @block.sync
        def _(sp):
            sp.dma_start(TB[:, 0:P], tab[:, 0:P]).then_inc(S["tables_in"], 16)
            for name, (at, n) in VEC.items():
                src = A[name]
                src = src.rearrange("l c (w p) -> (l c w) p", p=P) if len(src.shape) == 3 else \
                    src.rearrange("l (w p) -> (l w) p", p=P)
                sp.dma_start(vrows[at:at + n, :], src).then_inc(S["inputs_in"], 16)
            sp.dma_start(srows[0:96, :], A["state_rglru_conv"].rearrange("l b c (w p) -> (l b c w) p", p=P)
                         ).then_inc(S["inputs_in"], 16)
            sp.dma_start(srows[96:128, :], A["state_rglru_h"].rearrange("l b (w p) -> (l b w) p", p=P)
                         ).then_inc(S["inputs_in"], 16)
            sp.dma_start(nrows[0:32, :], A["state_mlstm_n"].rearrange("l b (w h) d -> (l b w) (h d)", h=2)
                         ).then_inc(S["inputs_in"], 16)
            xp = A["x_prompt"].rearrange("a (t p) d -> (a t) p d", p=P)
            for t in range(2):
                sp.dma_start(xtok[:, t], xp[t]).then_inc(S["inputs_in"], 16)
            sp.dma_start(xtok[0:NS, 2], A["x_sample"].rearrange("b t d -> (b t) d")).then_inc(S["inputs_in"], 16)

            def refill(s, dst, src):
                sp.dma_start(dst, src).then_inc(full[s], 16)

            def in_panel(l, u, h):
                skip = 8 if isinstance(u, int) and u >= 6 else 0
                refill(h, slot(h), w_in[l][:, :, u * 256 + skip:u * 256 + skip + 256])

            for l in range(DEPTH):
                if l:
                    sp.wait_ge(S["g_ps"], l)
                sp.dma_start(WG[:, :, :], w_in[l][:, :, GATE_COL:GATE_COL + 8]).then_inc(S["gate_weights_in"], 16)
                if l:
                    sp.wait_ge(S["ps"], U_UP + 10)
                for h in range(2):
                    in_panel(l, h, h)
                if l == 0:
                    sp.dma_start(TB[:, P:], tab[:, P:]).then_inc(S["tables_in"], 16)
                for first, end, skip in ((1, 3, 0), (3, 7, 8)):
                    with sp.Fori(first, end) as i:
                        for h in range(2):
                            sp.wait_ge(S["ps"], i * 2 + (U_IN[l] + h - 1))
                            refill(h, slot(h), w_in[l][:, :, bass.ds(i * 512 + (h * 256 + skip), 256)])
                if l:
                    sp.wait_ge(S["ps"], U_DOWN + 4)
                for u in range(4):
                    refill(2 + u, slot(2 + u), w_out[l][:, :, u * 256:u * 256 + 256])
                if l == 0:
                    def up_panel(h, c):
                        for s, w in zip(UP_SLOTS[h], (f_w1, f_w3)):
                            refill(s, slot(s), w[0][:, :, c])
                    up_panel(0, slice(0, 256))
                    sp.wait_ge(S["ps"], U_IN[0] + 14)
                    up_panel(1, slice(256, 512))
                    with sp.Fori(1, 5) as i:
                        for h in range(2):
                            sp.wait_ge(S["ps"], i * 2 + (U_UP + h - 1))
                            up_panel(h, bass.ds(i * 512 + h * 256, 256))
                    sp.wait_ge(S["ps"], U_UP + 9)
                    up_panel(0, slice(2560, 2816))
                    sp.wait_ge(S["ps"], U_OUT[0] + 4)
                    for m in range(4):
                        if m == 1:
                            sp.wait_ge(S["mixed_ready"], 1)
                        elif m > 1:
                            sp.wait_ge(S["ps"], U_DOWN + m - 1)
                        for j, s in enumerate(DOWN_SLOTS[m % 2]):
                            nk = min(8, 22 - 8 * j)
                            refill(s, slot(s)[:, 0:nk], f_w2[0][:, 8 * j:8 * j + nk, m * 256:m * 256 + 256])

            def expert(e, first):
                for ft in range(FT_E):
                    s = E_SLOTS[ft]
                    if first:
                        if ft == 0:
                            sp.wait_ge(S["ps"], U_IN[1] + 14)
                        if s == 8:
                            sp.wait_ge(S["mixed_ready"], 2)
                        if s == 2:
                            sp.wait_ge(S["ps"], U_OUT[1] + 4)
                    else:
                        sp.wait_ge(S["moe_up"], e * FT_E + (ft + 1 - FT_E))
                    for i, w in enumerate((m_w1, m_w3)):
                        src = w[bass.ds(e, 1), :, :, ft * P:ft * P + P].rearrange("e p k c -> p (e k) c")
                        sp.dma_start(slot(s)[:, :, i * P:i * P + P], src).then_inc(full[s], 16)
                if first:
                    sp.wait_ge(S["x_ready"], 3 * KT)
                else:
                    sp.wait_ge(S["w2_used"], e)
                for j in range(6):
                    nk = min(2, FT_E - 2 * j)
                    src = m_w2[bass.ds(e, 1), :, 2 * j:2 * j + nk, :].rearrange("e p k c -> p (e k) c")
                    refill(11 + j, W2[:, 2 * j:2 * j + nk, :], src)
            expert(0, True)
            with sp.Fori(1, NE) as e:
                expert(e, False)
            sp.wait_ge(S["y_rows_a"], 1)
            sp.wait_ge(S["y_rows_d"], 1)
            yp = out["y_prompt"].rearrange("a (t p) d -> (a t) p d", p=P)
            for t in range(2):
                sp.dma_start(yp[t], xtok[:, t]).then_inc(S["y_stored"], 16)
            sp.dma_start(out["y_sample"].rearrange("b t d -> (b t) d"), xtok[0:NS, 2]).then_inc(S["y_stored"], 16)
            sp.wait_ge(S["y_stored"], 48)

        @block.gpsimd
        def _(pool):
            pool.dma_start(GB[:, 0, :], A["mlstm_bi"].rearrange("l h -> h l"), allow_slow_non_contiguous=True).then_inc(S["small_in"], 16)
            pool.dma_start(GB[:, 1, :], A["mlstm_bf"].rearrange("l h -> h l"), allow_slow_non_contiguous=True).then_inc(S["small_in"], 16)
            pool.dma_start(M0[:, :, :], A["state_mlstm_m"].rearrange("l b h -> h l b"), allow_slow_non_contiguous=True).then_inc(S["small_in"], 16)
            pool.dma_start(RW[:, :, :], A["moe_router"][0].rearrange("(k p) e -> p k e", p=P)).then_inc(S["small_in"], 16)
            pool.dma_start(RB[:, :], A["moe_router_b"][0:1, :].to_broadcast([P, NE])).then_inc(S["small_in"], 16)
            pool.memset(LW[:, :, :, :], 0.0).then_inc(S["lru_zeroed"], 1)
            pool.wait_ge(S["lru_zeroed"], 1)
            for l in range(DEPTH):
                if l:
                    pool.wait_ge(S["lru_ps"], l)
                for ri, name in enumerate(("lru_wr", "lru_wi")):
                    src = A[name][l].rearrange("(p h) i j -> h i p j", h=2)
                    for h in range(2):
                        pool.dma_start(LW[HD * h:HD * h + HD, ri, :, HD * h:HD * h + HD], src[h]
                                       ).then_inc(S["lru_in"], 16)
                if l:
                    pool.wait_ge(S["states_stored"], 16 * STORES * l)
                for kind, name in enumerate(("state_mlstm_C", "state_ret_S", "state_hgrn_S")):
                    for p in range(2):
                        pool.dma_start(s0(kind)[:, p], state_view(A[name], l, 0, NB)[:, p]).then_inc(S["s0_in"], 16)
                for kind in (1, 0, 2):
                    pool.wait_ge(S["v_tok"], l + 1)
                    if kind == 1:
                        pool.wait_ge(S["a_done"], l + 1)
                        pool.wait_ge(S["rot_done"], l + 1)
                    elif kind == 0:
                        pool.wait_ge(S["rst_ps"], l + 1)
                    else:
                        pool.wait_ge(S["mst_ps"], l + 1)
                    pool.tensor_tensor(
                        Vm, VT[0:NS, 2, kind * 256:kind * 256 + 256].rearrange("p (h v) -> p h v", h=NH)
                        .unsqueeze(2).to_broadcast([NS, NH, NB, HD]),
                        tb("batchmask").unsqueeze(1).unsqueeze(3).to_broadcast([NS, NH, NB, HD]),
                        ALU.mult).then_inc(S["vm_ready"], 1)
                def store(dst, src, **kw):
                    pool.dma_start(dst, src, **kw).then_inc(S["states_stored"], 16)
                for kind, done, tail in ((1, S["rst_done"], "ret_S"), (0, S["mst_done"], "mlstm_C"),
                                         (2, S["hst_done"], "hgrn_S")):
                    pool.wait_ge(done, l + 1)
                    store(state_view(out["prompt_" + tail], l, 0, 1)[:, :, 0], PFIN[:, kind])
                    for p in range(2):
                        store(state_view(out["sample_" + tail], l, 0, NB)[:, p], s0(kind)[:, p])
                    if kind == 0:
                        store(out["prompt_mlstm_m"][l].rearrange("b h -> h b"), M1[:, 0:1], allow_slow_non_contiguous=True)
                        store(out["sample_mlstm_m"][l].rearrange("b h -> h b"), M1[:, 1:1 + NB],
                              allow_slow_non_contiguous=True)
                pool.wait_ge(S["orow_done"], l + 1)
                store(out["prompt_rglru_conv"][l].rearrange("b c (w p) -> (b c w) p", p=P), OROW[0:6, :])
                store(out["sample_rglru_conv"][l].rearrange("b c (w p) -> (b c w) p", p=P), OROW[6:54, :])
                store(out["prompt_rglru_h"][l].rearrange("b (w p) -> (b w) p", p=P), OROW[54:56, :])
                store(out["sample_rglru_h"][l].rearrange("b (w p) -> (b w) p", p=P), OROW[56:72, :])
                store(out["prompt_mlstm_n"][l].rearrange("b (w h) d -> (b w) (h d)", h=2), OROW[72:74, :])
                store(out["sample_mlstm_n"][l].rearrange("b (w h) d -> (b w) (h d)", h=2), OROW[74:90, :])
            pool.wait_ge(S["states_stored"], 16 * DEPTH * STORES)

        @block.tensor
        def _(pe):
            def mm(o, lhsT, rhs, start=True, stop=True):
                return pe.matmul(o, lhsT, rhs, start=start, stop=stop)

            def tr(o, src, k):
                return pe.transpose(o, src, ident[0:k, 0:k])

            pe.wait_ge(S["tables_in"], 16)
            pe.wait_ge(S["inputs_in"], 16 * N_INPUTS)
            tr(PS[:, 0, 0:NVEC], vrows[0:NVEC, :], NVEC)
            tr(PS[:, 1, 0:P], srows, P)
            tr(PS[:, 1, P:P + 32], nrows[0:32, :], 32).then_inc(S["cols_ps"], 1)
            for t in range(3):
                n = P if t < 2 else NS
                for k in range(KT):
                    last = tr(PS[:, 2 + 2 * t + k // 4, (k % 4) * P:(k % 4) * P + n],
                              xtok[0:n, t, k * P:k * P + P], n)
            last.then_inc(S["x_ps"], 1)

            def mean(summed, count, tiles):
                pe.wait_ge(summed, count)
                for k in tiles:
                    last = mm(PS[:, 6, 0:T], tb("lnmean"), X[:, k], k == 0, k == KT - 1)
                if k == KT - 1:
                    last.then_inc(S["ln_mean_ps"], 1)

            def variance(q):
                for k in range(KT):
                    if k % 4 == 0:
                        pe.wait_ge(S["ln_sq"], 2 * q + k // 4 + 1)
                    last = mm(PS[:, 7, 0:T], tb("lnmean"), SQ[:, k], k == 0, k == KT - 1)
                last.then_inc(S["ln_var_ps"], 1)

            def tile_out(bank, w, nk, rhs, k0=0, kend=None):
                kend = nk if kend is None else kend
                for k in range(nk):
                    last = mm(PS[:, bank, 0:T], w(k), rhs[:, k0 + k], k0 + k == 0, k0 + k == kend - 1)
                return last

            def mix(l):
                done = l + 1
                pe.wait_ge(S["ev_a"], A_IN[l] + 14)
                pe.wait_ge(S["me_done"], done)
                for t in range(3):
                    n = P if t < 2 else NS
                    for i, tile in enumerate((VB, VB + 1, VC, VC + 1, ID, ID + 1)):
                        last = tr(PS[0:n, 2 * t + i // 3, (i % 3) * P:(i % 3) * P + P],
                                  proj[:, tile, t * P:t * P + n], P)
                last.then_inc(S["v_ps"], 1)

                def rows_of(h):
                    return HD * (h % 2), h // 2

                def scores(q, k, ready):
                    for h in range(NH):
                        r, p = rows_of(h)
                        kk, qq = proj[r:r + HD, k + p], proj[r:r + HD, q + p]
                        mm(PS[:, h, 0:SEQ], kk[:, 0:P], qq[:, 0:SEQ])
                        mm(PS[:, h, SEQ:SEQ + P], kk[:, P:SEQ], qq[:, P:SEQ])
                        last = mm(PS[0:NS, h, SEQ + P:WS], kk[:, SEQ:T], qq[:, SEQ:T])
                    last.then_inc(ready, 1)

                def keys(src, ready):
                    for t in range(3):
                        n = P if t < 2 else NS
                        for p in range(2):
                            at = (t % 2) * 256 + p * P
                            last = tr(PS[0:n, 6 + t // 2, at:at + P], src(p)[:, t * P:t * P + n], P)
                    last.then_inc(ready, 1)

                def outputs(bank, kind, v, carry, heads=range(NH)):
                    for h in heads:
                        r, p = rows_of(h)
                        o = PS[r:r + HD, bank + p]
                        mm(o[:, 0:SEQ], v(0, h), WT[:, h, 0:SEQ], True, False)
                        mm(o[:, P:SEQ], v(1, h), WT[:, h, SEQ:SEQ + P], False, True)
                        mm(o[:, SEQ:T], v(2, h), WT[0:NS, h, SEQ + P:WS], True, False)
                        for b in range(NB):
                            c = slice(DSEQ * b, DSEQ * b + DSEQ)
                            last = mm(o[:, SEQ + DSEQ * b:SEQ + DSEQ * b + DSEQ], carry(r, p, b),
                                      QH[r:r + HD, kind, p, c], False, b == NB - 1)
                    return last

                def value(kind):
                    return lambda t, h: VT[0:(P if t < 2 else NS), t, kind * 256 + h * HD:kind * 256 + h * HD + HD]

                def key(buf, t, h):
                    return KTK[0:(P if t < 2 else NS), buf, t, h * HD:h * HD + HD]

                def sample_states(buf, bank):
                    for h in range(NH):
                        r, p = rows_of(h)
                        last = mm(PS[r:r + HD, bank + p, :], key(buf, 2, h), Vm[:, h].rearrange("p b v -> p (b v)"))
                    return last

                pe.wait_ge(S["v_tok"], done)
                scores(QC, KC, S["rs_ps"])
                keys(lambda p: proj[:, KC + p], S["rk_ps"])
                pe.wait_ge(S["rw_done"], done)
                pe.wait_ge(S["s0_in"], 96 * done)
                outputs(4, 1, value(1), lambda r, p, b: s0(1)[r:r + HD, p, b, :]).then_inc(S["ry_ps"], 1)
                pe.wait_ge(S["rk_done"], done)
                for h in range(NH):
                    r, p = rows_of(h)
                    o = PS[r:r + HD, 6, p * HD:p * HD + HD]
                    mm(o, key(1, 0, h), value(1)(0, h), True, False)
                    mm(o, key(1, 1, h), value(1)(1, h), False, True)
                pe.wait_ge(S["vm_ready"], 3 * l + 1)
                sample_states(1, 0).then_inc(S["rst_ps"], 1)
                pe.wait_ge(S["ry_done"], done)
                pe.wait_ge(S["rst_done"], done)
                scores(QB, KB, S["ms_ps"])
                pe.wait_ge(S["rk_done"], done)
                keys(lambda p: proj[:, KB + p], S["mk_ps"])
                pe.wait_ge(S["mw_done"], done)
                pe.wait_ge(S["mq_done"], done)
                pe.wait_ge(S["mk_done"], done)

                def level(e):
                    lo = 2 * (e % 2)
                    pe.wait_ge(S["hl_ready"], (NL - 1) * l + min(e + 1, NL - 1))
                    if e >= 2:
                        pe.wait_ge(S["hl_done"], NL * l + e - 1)
                    qq, kk = (LVL[lo], LVL[lo + 1]) if e < NL - 1 else (q_hg, k_hg)
                    for h in range(NH):
                        r, p = rows_of(h)
                        for c in range(2):
                            at = 2 * c + p
                            k, q = kk[r:r + HD, p, c * P:c * P + P], qq[r:r + HD, p, c * P:c * P + P]
                            if e == NL - 1:
                                last = mm(PS[:, lo + h % 2, at * P:at * P + P], k, q)
                            else:
                                last = mm(right_only(PS[:, lo + h % 2, at * HD:at * HD + HD], e), k, right(q, e))
                        if e >= NL - 3:
                            k, q = kk[r:r + HD, p, SEQ:T], qq[r:r + HD, p, SEQ:T]
                            if e == NL - 1:
                                last = mm(PS[0:NS, 4 + lo + h % 2, p * NS:p * NS + NS], k, q)
                            else:
                                at = 4 * HD + p * NS // 2
                                last = mm(right_only(PS[0:NS, lo + h % 2, at:at + NS // 2], e), k, right(q, e))
                    last.then_inc(S["hl_ps"], 1)

                for h in range(NH):
                    outputs(4, 0, value(0), lambda r, p, b: s0(0)[r:r + HD, p, b, :], [h])
                    last = outputs(6, 0, lambda t, h: onesc[0:(P if t < 2 else NS), 0:HD],
                                   lambda r, p, b: STC[r:r + HD, 128 + 16 * l + 2 * b + p:129 + 16 * l + 2 * b + p]
                                   .to_broadcast([HD, HD]), [h])
                    if h == NH - 1:
                        last.then_inc(S["my_ps"], 1)
                    level(h)
                level(NH)
                pe.wait_ge(S["my_done"], done)
                for h in range(NH):
                    r, p = rows_of(h)
                    for c, n, rhs in ((p * HD, HD, lambda t: value(0)(t, h)), (P + p, 1, lambda t: onesc[:, 0:1])):
                        o = PS[r:r + HD, 6, c:c + n]
                        mm(o, key(0, 0, h), rhs(0), True, False)
                        mm(o, key(0, 1, h), rhs(1), False, True)
                    mm(PS[r:r + HD, 6, P + 8 + 8 * p:P + 16 + 8 * p], key(0, 2, h), tb("batchmask"))
                pe.wait_ge(S["vm_ready"], 3 * l + 2)
                sample_states(0, 4).then_inc(S["mst_ps"], 1)
                for e in range(NH + 1, NL):
                    if e == NL - 1:
                        pe.wait_ge(S["mst_done"], done)
                    level(e)
                pe.wait_ge(S["hk_ready"], done)
                keys(lambda p: C2[8][:, p], S["hk_ps"])
                pe.wait_ge(S["hk_done"], done)
                for c in range(2):
                    for h in range(NH):
                        r, p = rows_of(h)
                        last = mm(PS[r:r + HD, 6 + c, p * HD:p * HD + HD], key(0, c, h), value(2)(c, h))
                    last.then_inc(S["hc_ps"], 1)
                pe.wait_ge(S["hl_done"], NL * done)
                pe.wait_ge(S["hc_done"], done)
                for h in range(NH):
                    r, p = rows_of(h)
                    o = PS[r:r + HD, 4 + p]
                    mm(o[:, 0:P], value(2)(0, h), AT[:, 0, h])
                    mm(o[:, P:SEQ], value(2)(1, h), AT[:, 1, h], True, False)
                    mm(o[:, P:SEQ], SC0[r:r + HD, p], C2[7][r:r + HD, p, P:SEQ], False, True)
                    mm(o[:, SEQ:T], value(2)(2, h), ATs[:, h], True, False)
                    for b in range(NB):
                        c = slice(SEQ + DSEQ * b, SEQ + DSEQ * b + DSEQ)
                        last = mm(o[:, c], s0(2)[r:r + HD, p, b, :], C2[7][r:r + HD, p, c], False, b == NB - 1)
                last.then_inc(S["hy_ps"], 1)
                pe.wait_ge(S["vm_ready"], 3 * l + 3)
                sample_states(0, 2).then_inc(S["hst_ps"], 1)
                for i in range(4):
                    if i == 2:
                        pe.wait_ge(S["hst_done"], done)
                    last = mm(PS[:, (0, 1, 6, 7)[i], 0:T], tb("headmean"), Y[:, i])
                last.then_inc(S["mean_ps"], 1)
                pe.wait_ge(S["outc_done"], done)
                pe.wait_ge(S["centered"], done)
                tr(PS[0:90, 7, 0:P], OUTC[:, 0:90], P).then_inc(S["orow_ps"], 1)
                pe.wait_ge(S["sq6_done"], done)
                for i in range(6):
                    last = mm(PS[0:12, 6, 0:T], tb("headrows")[:, i], SQ6[:, i], i == 0, i == 5)
                last.then_inc(S["var_ps"], 1)
                pe.wait_ge(S["rrow_done"], done)
                pe.wait_ge(S["orow_done"], done)
                for i in (2, 3, 0, 1, 4, 5):
                    for h in range(2):
                        c = 2 * i + h
                        last = mm(PS[HD * h:HD * h + HD, 2 + i, 0:T], ident[0:12, c:c + 1].to_broadcast([12, HD]), RROW)
                    if i % 2:
                        last.then_inc(S["rb_ps"], 1)

            for l in range(DEPTH):
                done = l + 1
                pe.wait_ge(S["ev_a"], A_IN[l])
                pe.wait_ge(S["ev_d"], D_OUT[l])

                def panel(i, h):
                    pe.wait_ge(full[h], i * 16 + 16 * ((LOADS_L1[h] if l else 0) + 1))
                    pe.wait_ge(S["ev_a"], i * 2 + (A_IN[l] + h - 1))
                    for b in range(2):
                        last = tile_out(2 * h + b, lambda k: slot(h)[:, k, b * P:b * P + P], KT, X)
                    last.then_inc(S["ps"], 1)

                pe.wait_ge(S["gate_weights_in"], 16 * done)
                for k in range(KT):
                    if l:
                        pe.wait_ge(S["x_ready"], (2 * l - 1) * KT + k + 1)
                    last = mm(PS[0:8, 6, 0:T], WG[:, k, :], X[:, k], k == 0, k == KT - 1)
                last.then_inc(S["g_ps"], 1)
                panel(0, 0)
                panel(0, 1)
                pe.wait_ge(S["g_sb"], done)
                pe.wait_ge(S["tables_in"], 32)
                mm(PS[0:NH, 7, 0:T], ident[0:8, 0:NH], gsb)
                mm(PS[0:NH, 6, 0:T], ident[0:8, NH:8], gsb).then_inc(S["gif_ps"], 1)
                panel(1, 0)
                panel(1, 1)
                pe.wait_ge(S["xc_ready"], done)
                pe.wait_ge(S["lru_in"], 64 * done)
                pe.wait_ge(S["li_done"], done)
                for ri in range(2):
                    for p in range(2):
                        last = mm(PS[:, 4 + 2 * ri + p, 0:WC], LW[:, ri, p, :], A2["xc"][:, p, 0:WC])
                last.then_inc(S["lru_ps"], 1)
                with pe.Fori(2, 4) as i:
                    for h in range(2):
                        panel(i, h)
                pe.wait_ge(S["mrow_done"], done)
                pe.wait_ge(S["lru_read"], done)
                for t in range(3):
                    n = P if t < 2 else NS
                    for k, row in enumerate((rli, rtmp)):
                        last = tr(PS[0:n, 7, t * 8 + k * 4:t * 8 + k * 4 + 4], row[:, t * P:t * P + n], NH)
                last.then_inc(S["mcol_ps"], 1)
                for p in range(2):
                    mm(PS[:, 4 + p, 0:T], tb("selpair")[:, p], rlf)
                    last = mm(PS[:, 4 + p, T:T + NS], tb("selpair")[:, p], risc)
                last.then_inc(S["mb_ps"], 1)
                panel(4, 0)
                panel(4, 1)
                pe.wait_ge(S["mb_done"], done)
                pe.wait_ge(S["mcol_done"], done)
                for i in range(4):
                    last = mm(PS[:, 4 + i, 0:T], tb("swap"), proj[:, QC + i])
                last.then_inc(S["swap_ps"], 1)
                panel(5, 0)
                panel(5, 1)
                pe.wait_ge(S["rot_done"], done)
                for h in range(NH):
                    sel = ident[0:NH, h:h + 1].to_broadcast([NH, P])
                    mm(PS[:, 4 + h, 0:WS], ident, tb("causal"), True, False)
                    mm(PS[:, 4 + h, 0:SEQ], sel, rb[:, 0:SEQ], False, False)
                    mm(PS[:, 4 + h, SEQ:SEQ + P], sel, rb[:, P:SEQ], False, False)
                    last = mm(PS[:, 4 + h, SEQ + P:WS], sel, rb[:, SEQ:T], False, True)
                last.then_inc(S["ma_ps"], 1)
                panel(6, 0)
                panel(6, 1)
                mix(l)
                for u in range(4):
                    s = 2 + u
                    pe.wait_ge(full[s], 16 * ((LOADS_L1[s] if l else 0) + 1))
                    if u >= 2:
                        pe.wait_ge(S["ev_d"], D_OUT[l] + u - 1)
                    for b in range(2):
                        def weights(k):
                            if u == 0 and b == 0 and k in (2, 4, 6):
                                pe.wait_ge(*((S["mixed_part"], 2 * l + k // 2) if k < 6 else (S["mixed_ready"], l + 1)))
                            return slot(s)[:, k, b * P:b * P + P]
                        last = tile_out(2 * (u % 2) + b, weights, KT, mixed)
                    last.then_inc(S["ps"], 1)
                    if u:
                        mean(S["ev_d"], D_OUT[l] + u, (2 * u - 2, 2 * u - 1))
                mean(S["ev_d"], D_OUT[l] + 4, (6, 7))
                variance(2 * l)
                if l == 0:
                    def up(n, h):
                        for j, s in enumerate(UP_SLOTS[h]):
                            pe.wait_ge(full[s], n * 8 + (16 * ((0, 7)[h] + 1) - 8 * h))
                            for b in range(2):
                                def weights(k):
                                    if h == 0 and j == 0 and b == 0:
                                        pe.wait_ge(S["x_ready"], k + 1)
                                    return slot(s)[:, k, b * P:b * P + P]
                                last = tile_out(4 * h + 2 * j + b, weights, KT, X)
                        last.then_inc(S["ps"], 1)
                    pe.wait_ge(S["ev_d"], D_UP)
                    with pe.Fori(0, 5) as i:
                        for h in range(2):
                            pe.wait_ge(S["ev_d"], i * 2 + (D_UP + h - 1))
                            up(i * 2 + h, h)
                    pe.wait_ge(S["ev_d"], D_UP + 9)
                    up(10, 0)
                    pe.wait_ge(S["ev_d"], D_UP + 11)
                    for m in range(4):
                        if m >= 2:
                            pe.wait_ge(S["ev_d"], D_DOWN + m - 1)
                        for j, s in enumerate(DOWN_SLOTS[m % 2]):
                            before = (1, 0)[m % 2] + m // 2
                            pe.wait_ge(full[s], 16 * (before + 1))
                        for b in range(2):
                            for j, s in enumerate(DOWN_SLOTS[m % 2]):
                                last = tile_out(2 * (m % 2) + b, lambda k: slot(s)[:, k, b * P:b * P + P],
                                                min(8, 22 - 8 * j), hid, 8 * j, 22)
                        last.then_inc(S["ps"], 1)
                        if m:
                            mean(S["ev_d"], D_DOWN + m, (2 * m - 2, 2 * m - 1))
                    mean(S["ev_d"], D_DOWN + 4, (6, 7))
                    variance(1)
            pe.wait_ge(S["small_in"], 16 * 5)
            pe.wait_ge(S["x_ready"], 3 * KT)
            for t in range(3):
                n = P if t < 2 else NS
                for k in range(KT):
                    last = mm(PS[0:n, 0, t * NE:t * NE + NE], X[:, k, t * P:t * P + n], RW[:, k], k == 0, k == KT - 1)
            last.then_inc(S["logits_ps"], 1)
            for t in range(3):
                n = P if t < 2 else NS
                for k in range(KT):
                    last = tr(PS[0:n, 2 + 2 * t + k // 4, (k % 4) * P:(k % 4) * P + P], X[:, k, t * P:t * P + n], P)
            last.then_inc(S["xtk_ps"], 1)
            pe.wait_ge(S["gates_done"], 1)
            for bank, src in ((1, GTOK), (0, SEL)):
                for t in range(3):
                    n = P if t < 2 else NS
                    last = tr(PS[0:NE, bank, t * P:t * P + n], src[0:n, t], n)
            last.then_inc(S["gt_ps"], 1)
            pe.wait_ge(S["slots_done"], 1)
            pe.wait_ge(S["xtk_done"], 1)
            for t in range(3):
                n = P if t < 2 else NS
                tr(PS[0:n, 2, t * NE:t * NE + NE], PROW[:, t * P:t * P + n], NE)
            tr(PS[0:1, 3, 0:NE], CNT, NE).then_inc(S["pt_ps"], 1)
            pe.wait_ge(S["flag_ready"], 1)
            for e in range(NE):
                last = mm(PS[:, e, 0:T], ident[0:NE, e:e + 1].to_broadcast([NE, P]), GROW)
            last.then_inc(S["gbc_ps"], 1)
            dense = pe.value_load(FLAG[0:1, 0:1], min_val=0, max_val=1)

            def gather(n):
                pe.wait_ge(S["sel_ready"], n + 1)
                for k in range(KT):
                    for t in range(3):
                        r = P if t < 2 else NS
                        last = mm(PS[:, 6 + k // 4, (k % 4) * CAP:(k % 4) * CAP + CAP],
                                  XTK[0:r, t, k * P:k * P + P], SELT[0:r, t], t == 0, t == 2)
                last.then_inc(S["ga_ps"], 1)

            def gathered_expert(e, final):
                pe.wait_ge(S["xe_done"], e + 1)
                for ft in range(FT_E):
                    s = E_SLOTS[ft]
                    pe.wait_ge(full[s], e * 32 + (16 * LOADS_MOE[s] + 32))
                    if ft >= 2:
                        pe.wait_ge(S["moe_h"], e * FT_E + (ft - 1))
                    for b in range(2):
                        for k in range(KT):
                            last = mm(PS[:, ft % 2, b * CAP:b * CAP + CAP], slot(s)[:, k, b * P:b * P + P],
                                      XE[:, k], k == 0, k == KT - 1)
                    last.then_inc(S["moe_up"], 1)
                if not final:
                    gather(e + 1)
                pe.wait_ge(S["moe_h"], e * FT_E + FT_E)
                for j in range(6):
                    pe.wait_ge(full[11 + j], e * 16 + 16)
                for h in range(2):
                    for ft in range(FT_E):
                        last = mm(PS[0:CAP, 2 + h, :], hid_g[:, ft], W2[:, ft, 512 * h:512 * h + 512],
                                  ft == 0, ft == FT_E - 1)
                    last.then_inc(S["dn_ps"], 1)
                for k in range(KT):
                    if k % 4 == 0:
                        pe.wait_ge(S["yt_done"], e * 2 + (k // 4 + 1))
                    if k >= 2:
                        pe.wait_ge(S["sc_ev"], e * KT + (k - 1))
                    mm(PS[:, 4 + k % 2, 0:T], YTK[:, k * P:k * P + P],
                       SG[:, bass.ds(e, 1), :].rearrange("p e t -> p (e t)")).then_inc(S["sc_ps"], 1)
                    if k == 0:
                        pe.wait_ge(S["dn_ps"], e * 2 + 2)
                        pe.sem_inc(S["w2_used"], 1)

            with pe.If(dense):
                pe.wait_ge(S["gbc_done"], 1)
                with pe.Fori(0, NE) as e:
                    for ft in range(FT_E):
                        s = E_SLOTS[ft]
                        pe.wait_ge(full[s], e * 32 + (16 * LOADS_MOE[s] + 32))
                        if ft >= 2:
                            pe.wait_ge(S["moe_h"], e * FT_E + (ft - 1))
                        for b in range(2):
                            last = tile_out(2 * (ft % 2) + b, lambda k: slot(s)[:, k, b * P:b * P + P], KT, X)
                        last.then_inc(S["moe_up"], 1)
                    pe.wait_ge(S["moe_h"], e * FT_E + FT_E)
                    for j in range(6):
                        pe.wait_ge(full[11 + j], e * 16 + 16)
                    for m in range(KT):
                        if m >= 2:
                            pe.wait_ge(S["moe_y"], e * KT + (m - 1))
                        tile_out(4 + m % 2, lambda k: W2[:, k, m * P:m * P + P], FT_E, hid_e).then_inc(S["dn_ps"], 1)
                    pe.wait_ge(S["dn_ps"], e * KT + KT)
                    pe.sem_inc(S["w2_used"], 1)
            with pe.Else():
                pe.wait_ge(S["gbc_done"], 1)
                for e in range(NE):
                    mm(PS[:, e, 0:T], ident[0:NE, e:e + 1].to_broadcast([NE, P]), PROW).then_inc(S["pb_ps"], 1)
                pe.wait_ge(S["sg_done"], 1)
                gather(0)
                with pe.Fori(0, NE - 1) as e:
                    gathered_expert(e, False)
                gathered_expert(NE - 1, True)
            mean(S["moe_sum"], 1, range(KT))
            variance(3)
            for t in range(3):
                n = P if t < 2 else NS
                for k in range(KT):
                    pe.wait_ge(S["x_ready"], 3 * KT + k + 1)
                    last = tr(PS[0:n, 2 * t + k // 4, (k % 4) * P:(k % 4) * P + P], X[:, k, t * P:t * P + n], P)
            last.then_inc(S["y_ps"], 1)

        @block.scalar
        def _(act):
            def f(o, i, fn, **kw):
                return act.activation(o, i, fn, **kw)

            act.wait_ge(S["x_ps"], 1)
            f(X[:, 4:8, 0:P], PS[:, 3, :].rearrange("p (k t) -> p k t", k=4), ACT.Copy)
            f(X[:, 4:8, P:SEQ], PS[:, 5, :].rearrange("p (k t) -> p k t", k=4), ACT.Copy)
            f(X[:, 4:8, SEQ:T], PS[:, 7, :].rearrange("p (k t) -> p k t", k=4)[:, :, 0:NS], ACT.Copy
              ).then_inc(S["ev_a"], 2)
            act.wait_ge(S["prep_e"], 1)
            f(N0S[:, 0:4], N0S[:, 0:4], ACT.Exp).then_inc(S["prep_exp"], 1)
            act.wait_ge(S["prep_s"], 1)
            f(N0S[:, 40:44], N0S[:, 40:44], ACT.Exp).then_inc(S["prep_exp"], 1)

            def layer_norm(q, l, g, b):
                for h in range(2):
                    act.wait_ge(S["ln_xc"], 2 * q + h + 1)
                    f(SQ[:, 4 * h:4 * h + 4], X[:, 4 * h:4 * h + 4], ACT.Square).then_inc(S["ln_sq"], 1)
                act.wait_ge(S["ln_var_ps"], q + 1)
                f(SDEV, PS[:, 7, 0:T], ACT.Sqrt, bias=LN_EPS).then_inc(S["ln_sd"], 1)
                for k in range(KT):
                    act.wait_ge(S["ln_xn"], q * KT + k + 1)
                    f(X[:, k], X[:, k], ACT.Identity, bias=vec[b][:, KT * l + k:KT * l + k + 1]
                      ).then_inc(S["x_ready"], 1)

            def mix(l):
                done = l + 1

                def panel(i, h):
                    act.wait_ge(S["ps"], i * 2 + (U_IN[l] + h + 1))
                    f(proj[:, bass.ds(i * 4 + 2 * h, 2), :], PS[:, 2 * h:2 * h + 2, 0:T], ACT.Copy
                      ).then_inc(S["ev_a"], 1)
                panel(0, 0)
                panel(0, 1)
                act.wait_ge(S["ev_a"], A_IN[l] + 2)
                f(C2[7], proj[:, GA:GA + 2], ACT.Square).then_inc(S["gl_sq"], 1)
                panel(1, 0)
                act.wait_ge(S["mz"], done)
                f(rtmp, rtmp, ACT.Exp, scale=-1.0).then_inc(S["act_chain"], 1)
                act.wait_ge(S["act_chain"], done)
                f(rtmp, rtmp, ACT.Ln, bias=1.0).then_inc(S["m_ln"], 1)
                panel(1, 1)
                act.wait_ge(S["lru_ps"], done)
                for ri, name in enumerate(("r", "ig")):
                    for p in range(2):
                        c = 2 * l + p
                        last = f(A2[name][:, p, 0:WC], PS[:, 4 + 2 * ri + p, 0:WC], ACT.Tanh, scale=0.5,
                                 bias=vec[("lru_br", "lru_bi")[ri]][:, c:c + 1])
                last.then_inc(S["lru_read"], 1)
                act.wait_ge(S["gl_in"], done)
                f(C2[7], C2[7], ACT.Tanh).then_inc(S["gl_tanh"], 1)
                panel(2, 0)
                act.wait_ge(S["m_rows"], done)
                f(rlf, rm, ACT.Exp, scale=-1.0)
                f(risc, risc, ACT.Exp)
                f(rtmp, rtmp, ACT.Exp).then_inc(S["mrow_done"], 1)
                act.wait_ge(S["la_ready"], done)
                f(A2["a"][:, :, 0:WC], A2["r"][:, :, 0:WC], ACT.Exp)
                f(A2["h"][:, :, 0:WC], A2["r"][:, :, 0:WC], ACT.Tanh).then_inc(S["a_exp"], 1)
                panel(2, 1)
                act.wait_ge(S["om_ready"], done)
                f(A2["om"][:, :, 0:WC], A2["om"][:, :, 0:WC], ACT.Sqrt, scale=-1.0).then_inc(S["a_sqrt"], 1)
                panel(3, 0)
                panel(3, 1)
                act.wait_ge(S["mb_ps"], done)
                act.wait_ge(S["a_done"], done)
                f(embc, PS[:, 4:6, 0:T + NS], ACT.Copy).then_inc(S["mb_done"], 1)
                panel(4, 0)
                panel(4, 1)
                panel(5, 0)
                panel(5, 1)
                act.wait_ge(S["hf_ready"], done)
                f(k_hg, k_hg, ACT.Exp).then_inc(S["hf_exp"], 1)
                act.wait_ge(S["ma_ps"], done)
                act.wait_ge(S["mcol_done"], done)
                for h in range(NH):
                    f(E[:, h, 0:SEQ], PS[:, 4 + h, 0:SEQ], ACT.Exp, bias=mcol[:, 0, 0, h:h + 1])
                    f(E[:, h, SEQ:SEQ + P], PS[:, 4 + h, SEQ:SEQ + P], ACT.Exp, bias=mcol[:, 1, 0, h:h + 1])
                    last = f(E[0:NS, h, SEQ + P:WS], PS[0:NS, 4 + h, SEQ + P:WS], ACT.Exp,
                             bias=mcol[0:NS, 2, 0, h:h + 1])
                last.then_inc(S["me_done"], 1)
                panel(6, 0)
                act.wait_ge(S["hg_ready"], done)
                f(q_hg, proj[:, QD:QD + 2], ACT.Tanh, scale=0.5).then_inc(S["hq_tanh"], 1)
                f(lg_hg, lg_hg, ACT.Ln)
                f(b_hg, b_hg, ACT.Ln).then_inc(S["hg_ln"], 1)
                panel(6, 1)
                act.wait_ge(S["v_ps"], done)
                for t in range(3):
                    n = P if t < 2 else NS
                    for i in range(2):
                        last = f(VT[0:n, t, 384 * i:384 * i + 384], PS[0:n, 2 * t + i, 0:384], ACT.Copy)
                last.then_inc(S["v_tok"], 1)
                for e, s in enumerate(LEVELS):
                    act.wait_ge(S["hx"], len(LEVELS) * l + e + 1)
                    left, right = level_view(C2[7 + e % 2], s)
                    f(right, right, ACT.Exp)
                    f(left, left, ACT.Exp, scale=-1.0).then_inc(S["hz"], 1)
                act.wait_ge(S["mst_done"], done)
                for i, tile in enumerate((OB, GC, GD)):
                    last = f(TH[:, 2 * i:2 * i + 2], proj[:, tile:tile + 2], ACT.Tanh, scale=0.5)
                last.then_inc(S["th_done"], 1)
                act.wait_ge(S["hi_ready"], done)
                f(C2[7], b_hg, ACT.Exp)
                f(C2[8], C2[8], ACT.Exp)
                f(GE[:, :, 0:1], b_hg[:, :, SEQ - 1:SEQ], ACT.Exp)
                f(GE[:, :, 1:1 + NB], b_hg[:, :, SEQ + DSEQ - 1:T:DSEQ], ACT.Exp).then_inc(S["hi_exp"], 1)
                act.wait_ge(S["centered"], done)
                f(SQ6, Y, ACT.Square).then_inc(S["sq6_done"], 1)
                act.wait_ge(S["orow_ps"], done)
                f(OROW[0:90, :], PS[0:90, 7, 0:P], ACT.Copy).then_inc(S["orow_done"], 1)
                act.wait_ge(S["var_ps"], done)
                f(VROW, PS[0:12, 6, 0:T], ACT.Sqrt, bias=HEAD_EPS).then_inc(S["sd6_done"], 1)

            for l in range(DEPTH):
                mix(l)
                layer_norm(2 * l, l, "ln_mix_g", "ln_mix_b")
                if l == 0:
                    def up(n, h):
                        act.wait_ge(S["ps"], n + (U_UP + 1))
                        act.wait_ge(S["ev_d"], n + (D_UP - 1))
                        f(sil[:, 2 * h:2 * h + 2], PS[:, 4 * h:4 * h + 2, 0:T], ACT.Silu).then_inc(S["sl"], 1)
                    with act.Fori(0, 5) as i:
                        for h in range(2):
                            up(i * 2 + h, h)
                    up(10, 0)
                    layer_norm(1, 0, "ln_ffn_g", "ln_ffn_b")
            act.wait_ge(S["xtk_ps"], 1)
            act.wait_ge(S["states_stored"], 16 * STORES * DEPTH)
            for t in range(3):
                n = P if t < 2 else NS
                for i in range(2):
                    last = f(XTK[0:n, t, 512 * i:512 * i + 512], PS[0:n, 2 + 2 * t + i, :], ACT.Copy)
            last.then_inc(S["xtk_done"], 1)
            act.wait_ge(S["lg_ready"], 1)
            f(PR, LG, ACT.Exp).then_inc(S["pr_exp"], 1)
            act.wait_ge(S["gbc_ps"], 1)
            for e in range(NE):
                last = f(GBC[:, e], PS[:, e, 0:T], ACT.Copy)
            last.then_inc(S["gbc_done"], 1)
            dense = act.value_load(FLAG[0:1, 0:1], min_val=0, max_val=1)

            def tokens(n):
                act.wait_ge(S["ga_ps"], n + 1)
                for i in range(2):
                    last = f(XE[:, 4 * i:4 * i + 4], PS[:, 6 + i, 0:4 * CAP].rearrange("p (k c) -> p k c", k=4), ACT.Copy)
                last.then_inc(S["xe_done"], 1)

            def gathered_expert(e, final):
                for ft in range(FT_E):
                    act.wait_ge(S["moe_up"], e * FT_E + (ft + 1))
                    if ft >= 2:
                        act.wait_ge(S["moe_h"], e * FT_E + (ft - 1))
                    f(sil_g[:, ft % 2], PS[:, ft % 2, 0:CAP], ACT.Silu).then_inc(S["moe_s"], 1)
                if not final:
                    tokens(e + 1)
                for h in range(2):
                    act.wait_ge(S["dn_ps"], e * 2 + (h + 1))
                    f(YTK[:, 512 * h:512 * h + 512], PS[0:CAP, 2 + h, :], ACT.Copy).then_inc(S["yt_done"], 1)

            with act.If(dense):
                with act.Fori(0, NE) as e:
                    for ft in range(FT_E):
                        act.wait_ge(S["moe_up"], e * FT_E + (ft + 1))
                        if ft >= 2:
                            act.wait_ge(S["moe_h"], e * FT_E + (ft - 1))
                        f(sil_e[:, ft % 2], PS[:, 2 * (ft % 2), 0:T], ACT.Silu).then_inc(S["moe_s"], 1)
            with act.Else():
                tokens(0)
                with act.Fori(0, NE - 1) as e:
                    gathered_expert(e, False)
                gathered_expert(NE - 1, True)
            layer_norm(3, 1, "ln_ffn_g", "ln_ffn_b")
            act.wait_ge(S["y_ps"], 1)
            for t in range(3):
                n = P if t < 2 else NS
                last = f(xtok[0:n, t, 0:512], PS[0:n, 2 * t, :], ACT.Copy)
            last.then_inc(S["y_rows_a"], 1)

        @block.vector
        def _(v):
            chain = [0]

            def link(ins):
                chain[0] += 1
                ins.then_inc(S["dve_chain"], 1)
                v.wait_ge(S["dve_chain"], chain[0])

            def sig(ins, s, n):
                ins.then_inc(s, 1)
                v.wait_ge(s, n)

            tt, ts, stt, cp = v.tensor_tensor, v.tensor_scalar, v.scalar_tensor_tensor, v.tensor_copy
            M, AD, SU, MX, MN = ALU.mult, ALU.add, ALU.subtract, ALU.max, ALU.min

            v.wait_ge(S["cols_ps"], 1)
            cp(VE[:, :], PS[:, 0, 0:NVEC])
            link(cp(STC[:, :], PS[:, 1, 0:160]))
            v.wait_ge(S["x_ps"], 1)
            cp(X[:, 0:4, 0:P], PS[:, 2, :].rearrange("p (k t) -> p k t", k=4))
            cp(X[:, 0:4, P:SEQ], PS[:, 4, :].rearrange("p (k t) -> p k t", k=4))
            cp(X[:, 0:4, SEQ:T], PS[:, 6, :].rearrange("p (k t) -> p k t", k=4)[:, :, 0:NS]).then_inc(S["ev_d"], 2)
            lam = vec["lru_lambda"]
            e_, z, y2, pl, t0 = (N0S[:, 4 * i:4 * i + 4] for i in range(5))
            hlb = vec["hgrn_lb"]
            mx2, d2 = N0S[:, 24:26], N0S[:, 40:44]
            link(stt(t0, lam, -1.0, lam, M, MX))
            sig(ts(e_, t0, -1.0, None, M), S["prep_e"], 1)
            link(tt(mx2, hlb[:, 0:2], hlb[:, 2:4], MX))
            tt(d2[:, 0:2], hlb[:, 0:2], mx2, SU)
            sig(tt(d2[:, 2:4], hlb[:, 2:4], mx2, SU), S["prep_s"], 1)
            v.wait_ge(S["prep_exp"], 2)
            link(ts(t0, e_, 2.0, None, AD))
            link(v.reciprocal(t0, t0))
            link(tt(z, e_, t0, M))
            link(tt(y2, z, z, M))
            link(ts(pl, y2, 1.0 / 19, 1.0 / 17, M, AD))
            for n in (15, 13, 11, 9, 7, 5, 3, 1):
                link(tt(pl, pl, y2, M))
                link(ts(pl, pl, 1.0 / n, None, AD))
            link(tt(pl, pl, z, M))
            link(ts(t0, lam, -1.0, 0.0, M, MX))
            link(stt(t0, pl, 2.0, t0, M, AD))
            link(ts(LC[:, 0:4], t0, -4.0, None, M))
            for name in ("lru_br", "lru_bi"):
                link(ts(vec[name], vec[name], 0.5, None, M))
            s2 = N0S[:, 26:28]
            link(tt(s2, d2[:, 0:2], d2[:, 2:4], AD))
            link(v.reciprocal(s2, s2))
            tt(d2[:, 0:2], d2[:, 0:2], s2, M)
            link(tt(d2[:, 2:4], d2[:, 2:4], s2, M))
            link(tt(d2[:, 2:4], d2[:, 0:2], d2[:, 2:4], AD))
            link(tt(d2[:, 2:4], d2[:, 2:4], d2[:, 0:2], SU))
            link(tt(d2[:, 0:2], d2[:, 0:2], d2[:, 0:2], SU))
            ts(LC[:, 4:8], d2, 1e-30, None, MX)
            link(ts(LC[:, 8:12], d2, -1.0, 1.0, M, AD))
            link(v.memset(SM[:, :], 0.0))

            def layer_norm(q, l, src, g, b):
                v.wait_ge(S["ln_mean_ps"], q + 1)
                for h in range(2):
                    k = slice(4 * h, 4 * h + 4)
                    sig(tt(X[:, k], src[:, k], PS[:, 6, 0:T].unsqueeze(1).to_broadcast([P, 4, T]), SU),
                        S["ln_xc"], 2 * q + h + 1)
                v.wait_ge(S["ln_sd"], q + 1)
                link(v.reciprocal(RSTD, SDEV))
                for k in range(KT):
                    stt(X[:, k], X[:, k], vec[g][:, KT * l + k:KT * l + k + 1], RSTD, M, M).then_inc(S["ln_xn"], 1)

            def mix(l):
                done = l + 1
                if l:
                    v.wait_ge(S["orow_ps"], l)
                    v.wait_ge(S["states_stored"], 16 * STORES * l)
                v.wait_ge(S["g_ps"], done)
                cp(gsb, PS[0:8, 6, 0:T]).then_inc(S["g_sb"], 1)
                v.wait_ge(S["ev_a"], A_IN[l] + 1)
                xs = xpad[:, :, SC:WP].rearrange("p a (b s) -> p a b s", b=NB)
                v.memset(xpad[:, :, 0:3], 0.0)
                cp(xpad[:, :, 3:SC], proj[:, XA:XA + 2, 0:SEQ])
                cp(xs[:, :, :, 3:7], proj[:, XA:XA + 2, SEQ:T].rearrange("p a (b t) -> p a b t", b=NB))
                link(cp(xs[:, :, :, 0:3], STC[:, 48 * l:48 * l + 48].rearrange("p (b c w) -> p w b c", b=NB, c=3)))
                cw, cb, xc = vec["conv_w"], vec["conv_b"], A2["xc"]
                for j in range(4):
                    for p in range(2):
                        c = 8 * l + 2 * j + p
                        src = xpad[:, p, j:j + WC]
                        if j == 0:
                            last = ts(xc[:, p, 0:WC], src, cw[:, c:c + 1], cb[:, 2 * l + p:2 * l + p + 1], M, AD)
                        else:
                            last = stt(xc[:, p, 0:WC], src, cw[:, c:c + 1], xc[:, p, 0:WC], M, AD)
                    if j < 3:
                        link(last)
                last.then_inc(S["xc_ready"], 1)
                cp(OUTC[:, 0:6].rearrange("p (c w) -> p w c", c=3), xpad[:, :, SEQ:SEQ + 3])
                cp(OUTC[:, 6:54].rearrange("p (b c w) -> p w b c", b=NB, c=3), xs[:, :, :, 4:7])
                v.wait_ge(S["gif_ps"], done)
                v.wait_ge(S["small_in"], 80)
                ts(rli, PS[0:NH, 7, 0:T], GB[:, 0, l:l + 1], None, AD)
                sig(ts(rlf, PS[0:NH, 6, 0:T], GB[:, 1, l:l + 1], None, AD), S["li_done"], done)
                stt(rtmp, rlf, -1.0, rlf, M, MX).then_inc(S["mz"], 1)
                ga = proj[:, GA:GA + 2]
                v.wait_ge(S["gl_sq"], done)
                c0 = 0.7978845608028654
                link(ts(C2[7], C2[7], 0.044715 * c0, c0, M, AD))
                tt(C2[7], C2[7], ga, M).then_inc(S["gl_in"], 1)
                v.wait_ge(S["m_ln"], done)
                link(stt(rlf, rlf, 0.0, rtmp, MN, SU))
                v.tensor_tensor_scan(rb, tb("keep256"), rlf, 0.0, M, AD)
                tt(rtmp, rlf, tb("negstart"), AD)
                link(tt(N0S[0:NH, 48:56], rlf[:, SEQ:T:DSEQ], M0[:, l, :], AD))
                link(cp(rlf, rli))
                link(tt(rlf[:, SEQ:T:DSEQ], rli[:, SEQ:T:DSEQ], N0S[0:NH, 48:56], MX))
                link(v.tensor_tensor_scan(rm, rtmp, rlf, 0.0, AD, MX))
                cp(M1[:, 0:1], rm[:, SEQ - 1:SEQ])
                cp(M1[:, 1:1 + NB], rm[:, SEQ + DSEQ - 1:T:DSEQ])
                tt(rli, rli, rb, SU)
                link(tt(rb, rb, rm, SU))
                m0b = M0[:, l, :].unsqueeze(2).to_broadcast([NH, NB, DSEQ])
                four = "p (b t) -> p b t"
                tt(risc.rearrange(four, b=NB), rb[:, SEQ:T].rearrange(four, b=NB), m0b, AD)
                ts(rtmp[:, 0:SEQ], rli[:, 0:SEQ], rb[:, SEQ - 1:SEQ], None, AD)
                aend = rb[:, SEQ + DSEQ - 1:T:DSEQ].unsqueeze(2).to_broadcast([NH, NB, DSEQ])
                tt(rtmp[:, SEQ:T].rearrange(four, b=NB), rli[:, SEQ:T].rearrange(four, b=NB), aend, AD
                   ).then_inc(S["m_rows"], 1)
                r, ig, a, hh, om = (A2[n][:, :, 0:WC] for n in ("r", "ig", "a", "h", "om"))
                v.wait_ge(S["lru_read"], done)
                for p in range(2):
                    c = LC[:, 2 * l + p:2 * l + p + 1]
                    last = ts(r[:, p], r[:, p], c, c, M, AD)
                last.then_inc(S["la_ready"], 1)
                link(ts(ig, ig, 0.5, 0.5, M, AD))
                link(tt(ig, ig, xc[:, :, 0:WC], M))
                v.wait_ge(S["a_exp"], done)
                link(tt(om, a, a, M))
                stt(om, om, 1.0, hh, AD, M).then_inc(S["om_ready"], 1)
                v.wait_ge(S["a_sqrt"], done)
                link(tt(ig, ig, om, M))
                starts = slice(SC, WC, 3 + DSEQ)
                h0 = STC[:, 96 + 16 * l:112 + 16 * l].rearrange("p (b w) -> p w b", b=NB)
                tmp = N0S[:, 0:16].rearrange("p (w b) -> p w b", w=2)
                link(tt(tmp, a[:, :, starts], h0, M))
                link(tt(ig[:, :, starts], ig[:, :, starts], tmp, AD))
                link(v.memset(a[:, :, starts], 0.0))
                for p in range(2):
                    last = v.tensor_tensor_scan(hh[:, p], a[:, p], ig[:, p], 0.0, M, AD)
                link(last)
                cp(OUTC[:, 54:56], hh[:, :, SEQ - 1])
                cp(OUTC[:, 56:72].rearrange("p (b w) -> p w b", b=NB), hh[:, :, SC + DSEQ - 1:WC:3 + DSEQ])
                v.wait_ge(S["gl_tanh"], done)
                link(ts(C2[7], C2[7], 0.5, 0.5, M, AD))
                link(tt(C2[7], C2[7], ga, M))
                tt(mixed[:, 0:2, 0:SEQ], hh[:, :, 0:SEQ], C2[7][:, :, 0:SEQ], M)
                tt(mixed[:, 0:2, SEQ:T].rearrange("p a (b t) -> p a b t", b=NB),
                   A2["h"][:, :, SC:WP].rearrange("p a (b s) -> p a b s", b=NB)[:, :, :, 0:DSEQ],
                   C2[7][:, :, SEQ:T].rearrange("p a (b t) -> p a b t", b=NB), M).then_inc(S["a_done"], 1)
                v.wait_ge(S["mcol_ps"], done)
                cp(mcol[:, 0:2], PS[:, 7, 0:16].rearrange("p (t k h) -> p t k h", t=2, k=2))
                sig(cp(mcol[0:NS, 2], PS[0:NS, 7, 16:24].rearrange("p (k h) -> p k h", k=2)), S["mcol_done"], done)
                v.wait_ge(S["mb_done"], done)
                tt(QH[:, 0], proj[:, QB:QB + 2, SEQ:T], embc[:, :, T:T + NS], M).then_inc(S["mq_done"], 1)
                v.wait_ge(S["swap_ps"], done)
                qk = proj[:, QC:QC + 4]
                tt(rotmp, PS[:, 4:8, 0:T], tb("sin").unsqueeze(1).to_broadcast([P, 4, T]), M)
                link(tt(qk, qk, tb("cos").unsqueeze(1).to_broadcast([P, 4, T]), M))
                sig(tt(qk, qk, rotmp, AD), S["rot_done"], done)
                link(tt(QH[:, 1], qk[:, 0:2, SEQ:T], tb("retinter"), M))
                k_, q_, b_, lg = k_hg, q_hg, b_hg, lg_hg
                v.wait_ge(S["ev_a"], A_IN[l] + 12)
                ts(k_, k_, -1.0, 80.0, M, MN).then_inc(S["hf_ready"], 1)
                v.wait_ge(S["hf_exp"], done)
                link(ts(b_, k_, 1.0, None, AD))
                link(v.reciprocal(b_, b_))
                for p in range(2):
                    c = 2 * l + p
                    link(stt(k_[:, p], k_[:, p], LC[:, 8 + c:9 + c], b_[:, p], M, M))
                    last = ts(b_[:, p], b_[:, p], LC[:, 8 + c:9 + c], LC[:, 4 + c:5 + c], M, AD)
                link(last)
                ts(lg, b_, TINY, None, MX)
                ts(b_, b_, TINY, 1.0 / TINY, MN, M).then_inc(S["hg_ready"], 1)
                v.wait_ge(S["hq_tanh"], done)
                link(ts(q_, q_, 0.5, 0.5, M, AD))
                link(tt(q_, q_, proj[:, QD:QD + 2], M))
                v.wait_ge(S["hg_ln"], done)
                link(tt(lg, lg, b_, AD))
                for p in range(2):
                    last = v.tensor_tensor_scan(b_[:, p], tb("keep128"), lg[:, p], 0.0, M, AD)
                link(last)
                link(v.memset(ATALL, 0.0))
                v.wait_ge(S["v_tok"], done)
                v.wait_ge(S["rs_ps"], done)
                rd = tb("retdecay")
                tt(WT[:, :, 0:SEQ + P], PS[:, 0:4, 0:SEQ + P], rd[:, :, 0:SEQ + P], M)
                tt(WT[0:NS, :, SEQ + P:WS], PS[0:NS, 0:4, SEQ + P:WS], rd[0:NS, :, SEQ + P:WS], M
                   ).then_inc(S["rw_done"], 1)
                v.wait_ge(S["rk_ps"], done)
                kw = tb("retkeyw")
                for t in range(3):
                    n = P if t < 2 else NS
                    last = tt(KTK[0:n, 1, t, :].rearrange("p (h d) -> p h d", h=NH),
                              PS[0:n, 6 + t // 2, (t % 2) * 256:(t % 2) * 256 + 256].rearrange("p (h d) -> p h d", h=NH),
                              kw[0:n, t].unsqueeze(2).to_broadcast([n, NH, HD]), M)
                last.then_inc(S["rk_done"], 1)
                v.wait_ge(S["ry_ps"], done)
                cp(Y[:, Y_RET:Y_RET + 2], PS[:, 4:6, 0:T]).then_inc(S["ry_done"], 1)
                v.wait_ge(S["rst_ps"], done)
                cp(PFIN[:, 1], PS[:, 6, 0:P].rearrange("p (a v) -> p a v", a=2))
                for p in range(2):
                    st = S0[:, 1, 512 * p:512 * p + 512]
                    last = stt(st, st, tb("retstate")[:, p:p + 1], PS[:, p, :], M, AD)
                last.then_inc(S["rst_done"], 1)
                v.wait_ge(S["ms_ps"], done)
                stt(WT[:, :, 0:SEQ + P], PS[:, 0:4, 0:SEQ + P], HD ** -0.5, E[:, :, 0:SEQ + P], M, M)
                stt(WT[0:NS, :, SEQ + P:WS], PS[0:NS, 0:4, SEQ + P:WS], HD ** -0.5, E[0:NS, :, SEQ + P:WS], M, M
                    ).then_inc(S["mw_done"], 1)
                v.wait_ge(S["mk_ps"], done)
                for t in range(3):
                    n = P if t < 2 else NS
                    last = stt(KTK[0:n, 0, t, :].rearrange("p (h d) -> p h d", h=NH),
                               PS[0:n, 6 + t // 2, (t % 2) * 256:(t % 2) * 256 + 256].rearrange("p (h d) -> p h d", h=NH),
                               HD ** -0.5, mcol[0:n, t, 1].unsqueeze(2).to_broadcast([n, NH, HD]), M, M)
                last.then_inc(S["mk_done"], 1)
                v.wait_ge(S["mk_done"], done)
                def boundary(e):
                    s = LEVELS[e]
                    w = SEQ if s >= DSEQ else T
                    bv = b_[:, :, 0:w].rearrange("p a (n s) -> p a n s", s=2 * s)
                    xv = C2[7 + e % 2][:, :, 0:w].rearrange("p a (n s) -> p a n s", s=2 * s)
                    ref = bv[:, :, :, s - 1:s].to_broadcast([P, 2, w // (2 * s), 2 * s])
                    tt(xv, bv, ref, SU).then_inc(S["hx"], 1)

                def merge(e):
                    lo = 2 * (e % 2)
                    v.wait_ge(S["hl_ps"], NL * l + e + 1)
                    if l or e:
                        v.wait_ge(S["hl_done"], NL * l + e)
                    mask = tb("levels")[:, e].bitcast(U32)
                    for odd in range(2):
                        at = ATALL[:, 0:2 * NH * P].rearrange("p (c o i) -> p c o i", o=2, i=P)[:, :, odd]
                        ats = ATs[:, odd:NH:2]
                        if e == NL - 1:
                            last = v.copy_predicated(at, mask.unsqueeze(1).to_broadcast([P, 4, P]),
                                                     PS[:, lo + odd, :].rearrange("p (c i) -> p c i", c=4))
                            last = v.copy_predicated(
                                ats, mask[0:NS, 0:NS].unsqueeze(1).to_broadcast([NS, 2, NS]),
                                PS[0:NS, 4 + lo + odd, 0:2 * NS].rearrange("p (a i) -> p a i", a=2))
                            continue
                        s = LEVELS[e]
                        halves, both = "p c (n h s) -> p c n h s", "p (c n s) -> p c n s"
                        last = v.copy_predicated(
                            at.rearrange(halves, h=2, s=s)[:, :, :, 1],
                            right(mask, e).unsqueeze(1).to_broadcast([P, 4, HD // s, s]),
                            PS[:, lo + odd, 0:4 * HD].rearrange(both, c=4, s=s))
                        if e >= NL - 3:
                            n = NS // 2
                            last = v.copy_predicated(
                                ats.rearrange(halves, h=2, s=s)[:, :, :, 1],
                                right(mask[0:NS, 0:NS], e).unsqueeze(1).to_broadcast([NS, 2, n // s, s]),
                                PS[0:NS, lo + odd, 4 * HD:4 * HD + 2 * n].rearrange(both, c=2, s=s))
                    last.then_inc(S["hl_done"], 1)

                def mlstm_outputs():
                    v.wait_ge(S["my_ps"], done)
                    ym = Y[:, Y_ML:Y_ML + 2]
                    link(tt(ym, PS[:, 6:8, 0:T], embc[:, :, 0:T], MX))
                    link(stt(ym, PS[:, 6:8, 0:T], -1.0, ym, M, MX))
                    link(v.reciprocal(ym, ym))
                    sig(tt(ym, ym, PS[:, 4:6, 0:T], M), S["my_done"], done)

                def mlstm_states():
                    v.wait_ge(S["mst_ps"], done)
                    cp(PFIN[:, 0], PS[:, 6, 0:P].rearrange("p (a v) -> p a v", a=2))
                    cp(OUTC[:, 72:74], PS[:, 6, P:P + 2])
                    cs = embc[:, :, T + DSEQ - 1:T + NS:DSEQ]
                    n0 = STC[:, 128 + 16 * l:144 + 16 * l].rearrange("p (b w) -> p w b", b=NB)
                    tt(tmp, n0, cs, M)
                    for p in range(2):
                        last = tt(s0(0)[:, p], s0(0)[:, p], cs[:, p].unsqueeze(2).to_broadcast([P, NB, HD]), M)
                    link(last)
                    tt(OUTC[:, 74:90].rearrange("p (b w) -> p w b", b=NB), tmp,
                       PS[:, 6, P + 8:P + 24].rearrange("p (w b) -> p w b", w=2), AD).then_inc(S["outc_done"], 1)
                    for p in range(2):
                        st = S0[:, 0, 512 * p:512 * p + 512]
                        last = tt(st, st, PS[:, 4 + p, :], AD)
                    last.then_inc(S["mst_done"], 1)

                boundary(0)
                for e, s in enumerate(LEVELS):
                    if e + 1 < len(LEVELS):
                        boundary(e + 1)
                    v.wait_ge(S["hz"], len(LEVELS) * l + e + 1)
                    lo = 2 * (e % 2)
                    x, q, k, qo, ko = (level_view(z, s) for z in (C2[7 + e % 2], q_, k_, LVL[lo], LVL[lo + 1]))
                    tt(qo[1], q[1], x[1], M)
                    tt(ko[0], k[0], x[0], M).then_inc(S["hl_ready"], 1)
                    v.wait_ge(S["hl_ready"], (NL - 1) * l + e + 1)
                    if e == NH:
                        mlstm_outputs()
                    elif e == NH + 2:
                        mlstm_states()
                    if e:
                        merge(e - 1)
                for w, n, s in ((slice(0, SEQ), 2, P), (slice(SEQ, T), NB, DSEQ)):
                    bv = b_[:, :, w].rearrange("p a (n s) -> p a n s", s=s)
                    xv = C2[8][:, :, w].rearrange("p a (n s) -> p a n s", s=s)
                    last = tt(xv, bv[:, :, :, s - 1:s].to_broadcast([P, 2, n, s]), bv, SU)
                last.then_inc(S["hi_ready"], 1)
                merge(NL - 2)
                merge(NL - 1)
                v.wait_ge(S["hi_exp"], done)
                tt(C2[7], C2[7], q_, M)
                tt(C2[8], C2[8], k_, M).then_inc(S["hk_ready"], 1)
                v.wait_ge(S["hk_ps"], done)
                cp(KTK[:, 0, 0:2, :], PS[:, 6, :].rearrange("p (t c) -> p t c", t=2))
                cp(KTK[0:NS, 0, 2, :], PS[0:NS, 7, 0:256]).then_inc(S["hk_done"], 1)
                v.wait_ge(S["hc_ps"], 2 * l + 1)
                sig(cp(SC0[:, :, :], PS[:, 6, 0:P].rearrange("p (a v) -> p a v", a=2)), S["hc_done"], done)
                v.wait_ge(S["hc_ps"], 2 * l + 2)
                for p in range(2):
                    stt(PFIN[:, 2, p], SC0[:, p], GE[:, p, 0:1], PS[:, 7, HD * p:HD * p + HD], M, AD)
                v.wait_ge(S["hy_ps"], done)
                cp(Y[:, Y_HG:Y_HG + 2], PS[:, 4:6, 0:T])
                for p in range(2):
                    last = tt(s0(2)[:, p], s0(2)[:, p], GE[:, p, 1:1 + NB].unsqueeze(2).to_broadcast([P, NB, HD]), M)
                link(last)
                v.wait_ge(S["hst_ps"], done)
                for p in range(2):
                    st = S0[:, 2, 512 * p:512 * p + 512]
                    last = tt(st, st, PS[:, 2 + p, :], AD)
                last.then_inc(S["hst_done"], 1)
                v.wait_ge(S["th_done"], done)
                link(ts(TH, TH, 0.5, 0.5, M, AD))
                tt(TH[:, 2:4], TH[:, 2:4], proj[:, GC:GC + 2], M)
                link(tt(TH[:, 4:6], TH[:, 4:6], proj[:, GD:GD + 2], M))
                v.wait_ge(S["mean_ps"], done)
                tt(Y[:, 0:2], Y[:, 0:2], PS[:, 0:2, 0:T], SU)
                sig(tt(Y[:, 2:4], Y[:, 2:4], PS[:, 6:8, 0:T], SU), S["centered"], done)
                v.wait_ge(S["sd6_done"], done)
                v.reciprocal(RROW, VROW).then_inc(S["rrow_done"], 1)
                groups = ((Y_ML, "mlstm_norm_g", "mixed_part"), (Y_RET, "ret_norm_g", "mixed_part"),
                          (Y_HG, "hgrn_norm_g", "mixed_ready"))
                for n, (at, g, ready) in enumerate(groups):
                    v.wait_ge(S["rb_ps"], 3 * l + n + 1)
                    for p in range(2):
                        y = Y[:, at + p]
                        last = stt(y, y, vec[g][:, 2 * l + p:2 * l + p + 1], PS[:, 2 + at + p, 0:T], M, M)
                    link(last)
                    tt(mixed[:, 2 + 2 * n:4 + 2 * n], Y[:, at:at + 2], TH[:, 2 * n:2 * n + 2], M).then_inc(S[ready], 1)

            for l in range(DEPTH):
                mix(l)
                for u in range(4):
                    v.wait_ge(S["ps"], U_OUT[l] + u + 1)
                    x2 = X[:, 2 * u:2 * u + 2]
                    stt(x2, x2, ALPHA, PS[:, 2 * (u % 2):2 * (u % 2) + 2, 0:T], M, AD).then_inc(S["ev_d"], 1)
                v.wait_ge(S["ev_d"], D_OUT[l] + 4)
                layer_norm(2 * l, l, X, "ln_mix_g", "ln_mix_b")
                if l == 0:
                    def up(n, t0, h):
                        v.wait_ge(S["sl"], n + 1)
                        tt(hid[:, t0, :], sil[:, 2 * h:2 * h + 2], PS[:, 4 * h + 2:4 * h + 4, 0:T], M).then_inc(S["ev_d"], 1)
                    with v.Fori(0, 5) as i:
                        for h in range(2):
                            up(i * 2 + h, bass.ds(i * 4 + 2 * h, 2), h)
                    up(10, slice(20, 22), 0)
                    v.wait_ge(S["x_ready"], KT)
                    for m in range(4):
                        v.wait_ge(S["ps"], U_DOWN + m + 1)
                        x2 = X[:, 2 * m:2 * m + 2]
                        stt(x2, x2, ALPHA, PS[:, 2 * (m % 2):2 * (m % 2) + 2, 0:T], M, AD).then_inc(S["ev_d"], 1)
                    v.wait_ge(S["ev_d"], D_DOWN + 4)
                    layer_norm(1, 0, X, "ln_ffn_g", "ln_ffn_b")
            v.wait_ge(S["x_ready"], 3 * KT)
            link(v.memset(SM[:, 0:192], 0.0))
            v.wait_ge(S["logits_ps"], 1)
            tt(LG[:, 0:2], PS[:, 0, 0:16].rearrange("p (t e) -> p t e", t=2),
               RB[:, :].unsqueeze(1).to_broadcast([P, 2, NE]), AD)
            link(tt(LG[0:NS, 2], PS[0:NS, 0, 16:24], RB[0:NS, :], AD))

            def bc(x):
                return x.unsqueeze(2).to_broadcast([P, 3, NE])

            def red(o, i, op):
                link(v.tensor_reduce(o, i, AX_X, op))
            iota = tb("iota8").unsqueeze(1).to_broadcast([P, 3, NE])
            red(T3[0], LG, MX)
            sig(tt(LG, LG, bc(T3[0]), SU), S["lg_ready"], 1)
            v.wait_ge(S["pr_exp"], 1)
            red(T3[1], PR, AD)
            link(v.reciprocal(T3[1], T3[1]))
            link(tt(PR, PR, bc(T3[1]), M))
            link(cp(PX, PR))
            for n in range(2):
                red(T3[2], PX, MX)
                link(tt(EQ, PX, bc(T3[2]), ALU.is_equal))
                link(stt(EQ, EQ, -8.0, tb("iota8").unsqueeze(1).to_broadcast([P, 3, NE]), M, AD))
                red(T3[3], EQ, MN)
                link(tt(EQ, EQ, bc(T3[3]), ALU.is_equal))
                link(tt(SEL, SEL, EQ, AD))
                link(stt(PX, EQ, -2.0, PX, M, AD))
            link(tt(PR, PR, SEL, M))
            red(T3[4], PR, AD)
            link(v.reciprocal(T3[4], T3[4]))
            tt(GTOK, PR, bc(T3[4]), M).then_inc(S["gates_done"], 1)
            v.wait_ge(S["gt_ps"], 1)
            cp(GROW, PS[0:NE, 1, 0:T])
            link(cp(SROW, PS[0:NE, 0, 0:T]))
            link(v.tensor_tensor_scan(PROW, SROW, SROW, 0.0, AD, MX))
            link(cp(CNT, PROW[:, T - 1:T]))
            link(tt(PROW, PROW, SROW, M))
            sig(ts(PROW, PROW, 1.0, None, SU), S["slots_done"], 1)
            v.wait_ge(S["pt_ps"], 1)
            cp(PTK[:, 0:2], PS[:, 2, 0:16].rearrange("p (t e) -> p t e", t=2))
            cp(PTK[0:NS, 2], PS[0:NS, 2, 16:24])
            link(v.tensor_reduce(T3[5][0:1, 0:1], PS[0:1, 3, 0:NE], AX_X, MX))
            sig(ts(FLAG[:, :], T3[5][0:1, 0:1], float(CAP), None, ALU.is_gt), S["flag_ready"], 1)
            v.wait_ge(S["gbc_done"], 1)
            dense = v.value_load(FLAG[0:1, 0:1], min_val=0, max_val=1)

            def choose(n, dyn):
                tt(SELT, tb("iotacap").unsqueeze(1).to_broadcast([P, 3, CAP]),
                   PTK[:, :, dyn].to_broadcast([P, 3, CAP]), ALU.is_equal).then_inc(S["sel_ready"], 1)

            def gathered_expert(e, final):
                if not final:
                    v.wait_ge(S["ga_ps"], e + 1)
                    choose(e + 1, bass.ds(e + 1, 1))
                for ft in range(FT_E):
                    v.wait_ge(S["moe_s"], e * FT_E + (ft + 1))
                    tt(hid_g[:, ft], sil_g[:, ft % 2], PS[:, ft % 2, CAP:2 * CAP], M).then_inc(S["moe_h"], 1)
                for k in range(KT):
                    v.wait_ge(S["sc_ps"], e * KT + (k + 1))
                    tt(X[:, k], X[:, k], PS[:, 4 + k % 2, 0:T], AD).then_inc(S["sc_ev"], 1)

            with v.If(dense):
                ts(YE, X, ALPHA, None, M).then_inc(S["ye_ready"], 1)
                v.wait_ge(S["ye_ready"], 1)
                with v.Fori(0, NE) as e:
                    for ft in range(FT_E):
                        h = ft % 2
                        v.wait_ge(S["moe_s"], e * FT_E + (ft + 1))
                        tt(sil_e[:, h], sil_e[:, h], PS[:, 2 * h + 1, 0:T], M).then_inc(S["moe_g"], 1)
                        v.wait_ge(S["moe_g"], e * FT_E + (ft + 1))
                        tt(hid_e[:, ft], sil_e[:, h], GBC[:, bass.ds(e, 1), :].rearrange("p e t -> p (e t)"), M
                           ).then_inc(S["moe_h"], 1)
                    for m in range(KT):
                        v.wait_ge(S["dn_ps"], e * KT + (m + 1))
                        tt(YE[:, m], YE[:, m], PS[:, 4 + m % 2, 0:T], AD).then_inc(S["moe_y"], 1)
                v.wait_ge(S["moe_y"], NE * KT)
                cp(X, YE).then_inc(S["moe_sum"], 1)
            with v.Else():
                ts(X, X, ALPHA, None, M).then_inc(S["ye_ready"], 1)
                choose(0, slice(0, 1))
                for e in range(NE):
                    v.wait_ge(S["pb_ps"], e + 1)
                    last = stt(SG[:, e], PS[0:CAP, e, 0:T], tb("iotarow")[0:CAP], GBC[0:CAP, e], ALU.is_equal, M)
                last.then_inc(S["sg_done"], 1)
                v.wait_ge(S["ye_ready"], 1)
                with v.Fori(0, NE - 1) as e:
                    gathered_expert(e, False)
                gathered_expert(NE - 1, True)
                v.wait_ge(S["sc_ev"], NE * KT)
                v.sem_inc(S["moe_sum"], 1)
            v.wait_ge(S["moe_sum"], 1)
            layer_norm(3, 1, X, "ln_ffn_g", "ln_ffn_b")
            v.wait_ge(S["y_ps"], 1)
            for t in range(3):
                n = P if t < 2 else NS
                last = cp(xtok[0:n, t, 512:1024], PS[0:n, 2 * t + 1, :])
            last.then_inc(S["y_rows_d"], 1)


_INS = ["x_prompt", "x_sample", "state_rglru_h", "state_rglru_conv", "state_mlstm_C", "state_mlstm_n",
        "state_mlstm_m", "state_ret_S", "state_hgrn_S", "w_in", "w_out", "ln_mix_g", "ln_mix_b", "ln_ffn_g",
        "ln_ffn_b", "conv_w", "conv_b", "lru_wr", "lru_br", "lru_wi", "lru_bi", "lru_lambda", "mlstm_bi",
        "mlstm_bf", "mlstm_norm_g", "ret_norm_g", "hgrn_lb", "hgrn_norm_g", "ffn_w1", "ffn_w3", "ffn_w2",
        "moe_router", "moe_router_b", "moe_w1", "moe_w3", "moe_w2"]


def _outs():
    outs = [("y_prompt", (1, SEQ, D)), ("y_sample", (NB, DSEQ, D))]
    for who, b in (("prompt", 1), ("sample", NB)):
        outs += [(f"{who}_rglru_h", (DEPTH, b, GW)), (f"{who}_rglru_conv", (DEPTH, b, 3, GW)),
                 (f"{who}_mlstm_C", (DEPTH, b, NH, HD, HD)), (f"{who}_mlstm_n", (DEPTH, b, NH, HD)),
                 (f"{who}_mlstm_m", (DEPTH, b, NH)), (f"{who}_ret_S", (DEPTH, b, NH, HD, HD)),
                 (f"{who}_hgrn_S", (DEPTH, b, NH, HD, HD))]
    return outs


def kernel(**inputs):
    import concourse.bacc as _bacc
    from concourse.bass_utils import run_bass_kernel_spmd as _run

    nc = _bacc.Bacc("TRN2", target_bir_lowering=False, num_devices=1)
    arrays, args = {}, {}
    for name in _INS:
        a = np.ascontiguousarray(inputs[name])
        arrays[f"in_{name}"] = a
        args[name] = nc.dram_tensor(f"in_{name}", a.shape, mybir.dt.from_np(a.dtype), kind="ExternalInput").ap()
    tables, where = shape_tables()
    arrays["in_shape_tables"] = tables
    tab = nc.dram_tensor("in_shape_tables", tables.shape, F32, kind="ExternalInput").ap()
    out = {n: nc.dram_tensor(f"out_{n}", s, F32, kind="ExternalOutput").ap() for n, s in _outs()}
    decoder_kernel(nc, args, out, tab, where)
    r = _run(nc, [arrays], core_ids=[0])
    return tuple(r.results[0][f"out_{n}"] for n, _ in _outs())
```
